# Optimizing a Trainium2 kernel written in Bass

```python
import jax, jax.numpy as jnp
from jax import lax
import numpy as np

D_MODEL = 1024
BATCH = 1
SEQ = 512
DEPTH = 2

GRID_W = 64
ROPE_THETA = 10000.0

ATTN_HEADS = 8
ATTN_KV_HEADS = 2
ATTN_HEAD_DIM = 64
ATTN_WIDTH = ATTN_HEADS * ATTN_HEAD_DIM
KV_WIDTH = ATTN_KV_HEADS * ATTN_HEAD_DIM
Q_BLOCK = 128

CONV_CH = D_MODEL - ATTN_WIDTH
CONV_WIDTH = 31
CONV_PAD = CONV_WIDTH // 2
L0_IN = ATTN_WIDTH + 2 * KV_WIDTH + 2 * CONV_CH

RET_HEADS = 4
RET_KEY_DIM = D_MODEL // RET_HEADS
RET_VAL_DIM = 2 * RET_KEY_DIM
RET_QK_WIDTH = RET_HEADS * RET_KEY_DIM
RET_V_WIDTH = RET_HEADS * RET_VAL_DIM
L1_IN = 2 * RET_QK_WIDTH + 2 * RET_V_WIDTH
RET_CHUNK = 128

FFN_HIDDEN = -(-8 * D_MODEL // (3 * 256)) * 256

DEEPNORM_ALPHA = (2 * DEPTH) ** 0.25
DEEPNORM_BETA = (8 * DEPTH) ** -0.25
LN_EPS = 1e-5
RMS_EPS = 1e-6

kernel_name = 'hybrid_attn_conv_retention_encoder'

def layer_norm(x, g, b, eps=LN_EPS):
    xf = x.astype(jnp.float32)
    mu = jnp.mean(xf, axis=-1, keepdims=True)
    var = jnp.mean(jnp.square(xf - mu), axis=-1, keepdims=True)
    y = (xf - mu) * lax.rsqrt(var + eps)
    return (y * g.astype(jnp.float32) + b.astype(jnp.float32)).astype(x.dtype)

def rms_norm(x, g, eps=RMS_EPS):
    xf = x.astype(jnp.float32)
    y = xf * lax.rsqrt(jnp.mean(jnp.square(xf), axis=-1, keepdims=True) + eps)
    return (y * g.astype(jnp.float32)).astype(x.dtype)

def axial_rope(seq_len, head_dim):
    rows = seq_len // GRID_W
    row = jnp.broadcast_to(jnp.arange(rows, dtype=jnp.float32)[:, None], (rows, GRID_W)).reshape(seq_len)
    col = jnp.broadcast_to(jnp.arange(GRID_W, dtype=jnp.float32)[None, :], (rows, GRID_W)).reshape(seq_len)
    axis_dim = head_dim // 2
    inv_freq = ROPE_THETA ** (-jnp.arange(0, axis_dim, 2, dtype=jnp.float32) / axis_dim)
    ang = jnp.concatenate([row[:, None] * inv_freq, col[:, None] * inv_freq], axis=-1)
    return jnp.cos(ang), jnp.sin(ang)

def apply_rope(x, cos, sin):
    half = x.shape[-1] // 2
    xf = x.astype(jnp.float32)
    x1, x2 = xf[..., :half], xf[..., half:]
    c = cos[None, :, None, :]
    s = sin[None, :, None, :]
    return jnp.concatenate([x1 * c - x2 * s, x1 * s + x2 * c], axis=-1).astype(x.dtype)

def block_attention(q, k, v):
    B, S = q.shape[0], q.shape[1]
    G = ATTN_HEADS // ATTN_KV_HEADS
    nblk = S // Q_BLOCK
    qb = q.reshape(B, nblk, Q_BLOCK, ATTN_KV_HEADS, G, ATTN_HEAD_DIM).transpose(1, 0, 2, 3, 4, 5)
    scale = ATTN_HEAD_DIM ** -0.5

    def one_block(q_blk):
        s = jnp.einsum('bqkgd,bskd->bkgqs', q_blk, k).astype(jnp.float32) * scale
        p = jax.nn.softmax(s, axis=-1).astype(v.dtype)
        return jnp.einsum('bkgqs,bskd->bqkgd', p, v)

    o = lax.map(one_block, qb)
    return o.transpose(1, 0, 2, 3, 4, 5).reshape(B, S, ATTN_WIDTH)

def conformer_conv(u, dw_w, dw_b, norm_g, norm_b):
    a, gate = jnp.split(u, 2, axis=-1)
    z = a * jax.nn.sigmoid(gate)
    z = lax.conv_general_dilated(
        z, dw_w[:, None, :].astype(z.dtype), window_strides=(1,),
        padding=[(CONV_PAD, CONV_PAD)], dimension_numbers=('NWC', 'WIO', 'NWC'),
        feature_group_count=CONV_CH) + dw_b
    z = layer_norm(z, norm_g, norm_b)
    return jax.nn.silu(z)

def attn_conv_mixer(x, w_in, q_norm_g, k_norm_g, dw_w, dw_b, conv_norm_g, conv_norm_b, w_out, cos, sin):
    B, S, _ = x.shape
    proj = x @ w_in
    q, k, v, u = jnp.split(proj, [ATTN_WIDTH, ATTN_WIDTH + KV_WIDTH, ATTN_WIDTH + 2 * KV_WIDTH], axis=-1)
    q = q.reshape(B, S, ATTN_HEADS, ATTN_HEAD_DIM)
    k = k.reshape(B, S, ATTN_KV_HEADS, ATTN_HEAD_DIM)
    v = v.reshape(B, S, ATTN_KV_HEADS, ATTN_HEAD_DIM)
    q = apply_rope(rms_norm(q, q_norm_g), cos, sin)
    k = apply_rope(rms_norm(k, k_norm_g), cos, sin)
    attn = block_attention(q, k, v)
    conv = conformer_conv(u, dw_w, dw_b, conv_norm_g, conv_norm_b)
    return jnp.concatenate([attn, conv], axis=-1) @ w_out

def retention_scan(q, k, v, log_gamma, strict):
    B, H, S, dk = q.shape
    dv = v.shape[-1]
    C = RET_CHUNK
    nC = S // C
    lg = log_gamma.astype(jnp.float32)
    pos = jnp.arange(C, dtype=jnp.float32)
    diff = pos[:, None] - pos[None, :]
    mask = (diff > 0) if strict else (diff >= 0)
    intra = jnp.where(mask[None], jnp.exp(lg[:, None, None] * jnp.where(mask, diff, 0.0)[None]), 0.0)
    q_decay = jnp.exp(lg[:, None] * (pos + 1.0)[None])
    k_decay = jnp.exp(lg[:, None] * (C - 1.0 - pos)[None])
    chunk_decay = jnp.exp(lg * C)

    def to_chunks(t):
        return t.reshape(B, H, nC, C, t.shape[-1]).transpose(2, 0, 1, 3, 4)

    def step(state, inp):
        qi, ki, vi = inp
        scores = jnp.einsum('bhqd,bhkd->bhqk', qi, ki) * intra[None]
        o = jnp.einsum('bhqk,bhkv->bhqv', scores, vi) + jnp.einsum(
            'bhqd,bhdv->bhqv', qi * q_decay[None, :, :, None], state)
        state = state * chunk_decay[None, :, None, None] + jnp.einsum(
            'bhkd,bhkv->bhdv', ki * k_decay[None, :, :, None], vi)
        return state, o

    state0 = jnp.zeros((B, H, dk, dv), jnp.float32)
    _, o = lax.scan(step, state0, (to_chunks(q), to_chunks(k), to_chunks(v)))
    return o.transpose(1, 2, 0, 3, 4).reshape(B, H, S, dv)

def retention_mixer(x, w_in, log_decay_fwd, log_decay_bwd, ret_norm_g, w_out, cos, sin):
    B, S, _ = x.shape
    proj = x @ w_in
    q, k, v, g = jnp.split(proj, [RET_QK_WIDTH, 2 * RET_QK_WIDTH, 2 * RET_QK_WIDTH + RET_V_WIDTH], axis=-1)
    q = apply_rope(q.reshape(B, S, RET_HEADS, RET_KEY_DIM), cos, sin)
    k = apply_rope(k.reshape(B, S, RET_HEADS, RET_KEY_DIM), cos, sin)
    v = v.reshape(B, S, RET_HEADS, RET_VAL_DIM)
    qh = q.transpose(0, 2, 1, 3).astype(jnp.float32)
    kh = k.transpose(0, 2, 1, 3).astype(jnp.float32) * (RET_KEY_DIM ** -0.5)
    vh = v.transpose(0, 2, 1, 3).astype(jnp.float32)
    o_fwd = retention_scan(qh, kh, vh, log_decay_fwd, strict=False)
    o_bwd = jnp.flip(retention_scan(jnp.flip(qh, 2), jnp.flip(kh, 2), jnp.flip(vh, 2),
                                    log_decay_bwd, strict=True), 2)
    y = (o_fwd + o_bwd).transpose(0, 2, 1, 3)
    mu = jnp.mean(y, axis=-1, keepdims=True)
    var = jnp.mean(jnp.square(y - mu), axis=-1, keepdims=True)
    y = ((y - mu) * lax.rsqrt(var + LN_EPS)).reshape(B, S, RET_V_WIDTH)
    y = (y * ret_norm_g.astype(jnp.float32)).astype(x.dtype)
    return (jax.nn.silu(g) * y) @ w_out

def swiglu(x, w_gate, w_up, w_down):
    return (jax.nn.silu(x @ w_gate) * (x @ w_up)) @ w_down

def setup_inputs(seed: int = 0) -> dict:
    key = jax.random.key(seed)
    ks = iter(jax.random.split(key, 40))

    def normal(shape, scale):
        return jax.random.normal(next(ks), shape, jnp.float32) * scale

    def gain(n):
        return 1.0 + normal((n,), 0.02)

    base_decay = jnp.asarray(np.log(1.0 - 2.0 ** (-5.0 - np.arange(RET_HEADS))), jnp.float32)
    d = D_MODEL
    inp = {}
    inp['x'] = normal((BATCH, SEQ, d), 1.0)
    inp['l0_w_in'] = normal((d, L0_IN), d ** -0.5)
    inp['l0_q_norm_g'] = gain(ATTN_HEAD_DIM)
    inp['l0_k_norm_g'] = gain(ATTN_HEAD_DIM)
    inp['l0_dw_w'] = normal((CONV_WIDTH, CONV_CH), CONV_WIDTH ** -0.5)
    inp['l0_dw_b'] = normal((CONV_CH,), 0.02)
    inp['l0_conv_norm_g'] = gain(CONV_CH)
    inp['l0_conv_norm_b'] = normal((CONV_CH,), 0.02)
    inp['l0_w_out'] = normal((ATTN_WIDTH + CONV_CH, d), (ATTN_WIDTH + CONV_CH) ** -0.5 * DEEPNORM_BETA)
    inp['l0_ln_mix_g'] = gain(d)
    inp['l0_ln_mix_b'] = normal((d,), 0.02)
    inp['l0_ffn_w_gate'] = normal((d, FFN_HIDDEN), d ** -0.5)
    inp['l0_ffn_w_up'] = normal((d, FFN_HIDDEN), d ** -0.5)
    inp['l0_ffn_w_down'] = normal((FFN_HIDDEN, d), FFN_HIDDEN ** -0.5 * DEEPNORM_BETA)
    inp['l0_ln_ffn_g'] = gain(d)
    inp['l0_ln_ffn_b'] = normal((d,), 0.02)
    inp['l1_w_in'] = normal((d, L1_IN), d ** -0.5)
    inp['l1_log_decay_fwd'] = base_decay * (1.0 + normal((RET_HEADS,), 0.05))
    inp['l1_log_decay_bwd'] = base_decay * (1.0 + normal((RET_HEADS,), 0.05))
    inp['l1_ret_norm_g'] = gain(RET_V_WIDTH)
    inp['l1_w_out'] = normal((RET_V_WIDTH, d), RET_V_WIDTH ** -0.5 * DEEPNORM_BETA)
    inp['l1_ln_mix_g'] = gain(d)
    inp['l1_ln_mix_b'] = normal((d,), 0.02)
    inp['l1_ffn_w_gate'] = normal((d, FFN_HIDDEN), d ** -0.5)
    inp['l1_ffn_w_up'] = normal((d, FFN_HIDDEN), d ** -0.5)
    inp['l1_ffn_w_down'] = normal((FFN_HIDDEN, d), FFN_HIDDEN ** -0.5 * DEEPNORM_BETA)
    inp['l1_ln_ffn_g'] = gain(d)
    inp['l1_ln_ffn_b'] = normal((d,), 0.02)
    return inp

def reference(x, l0_w_in, l0_q_norm_g, l0_k_norm_g, l0_dw_w, l0_dw_b, l0_conv_norm_g, l0_conv_norm_b,
              l0_w_out, l0_ln_mix_g, l0_ln_mix_b, l0_ffn_w_gate, l0_ffn_w_up, l0_ffn_w_down,
              l0_ln_ffn_g, l0_ln_ffn_b, l1_w_in, l1_log_decay_fwd, l1_log_decay_bwd, l1_ret_norm_g,
              l1_w_out, l1_ln_mix_g, l1_ln_mix_b, l1_ffn_w_gate, l1_ffn_w_up, l1_ffn_w_down,
              l1_ln_ffn_g, l1_ln_ffn_b):
    S = x.shape[1]
    cos_a, sin_a = axial_rope(S, ATTN_HEAD_DIM)
    cos_r, sin_r = axial_rope(S, RET_KEY_DIM)

    mixer_params = (
        (l0_w_in, l0_q_norm_g, l0_k_norm_g, l0_dw_w, l0_dw_b, l0_conv_norm_g, l0_conv_norm_b, l0_w_out),
        (l1_w_in, l1_log_decay_fwd, l1_log_decay_bwd, l1_ret_norm_g, l1_w_out),
    )
    mix_norms = ((l0_ln_mix_g, l0_ln_mix_b), (l1_ln_mix_g, l1_ln_mix_b))
    ffn_params = ((l0_ffn_w_gate, l0_ffn_w_up, l0_ffn_w_down), (l1_ffn_w_gate, l1_ffn_w_up, l1_ffn_w_down))
    ffn_norms = ((l0_ln_ffn_g, l0_ln_ffn_b), (l1_ln_ffn_g, l1_ln_ffn_b))

    for layer in range(DEPTH):
        if layer % 2 == 0:
            m = attn_conv_mixer(x, *mixer_params[layer], cos_a, sin_a)
        else:
            m = retention_mixer(x, *mixer_params[layer], cos_r, sin_r)
        x = layer_norm(DEEPNORM_ALPHA * x + m, *mix_norms[layer])
        x = layer_norm(DEEPNORM_ALPHA * x + swiglu(x, *ffn_params[layer]), *ffn_norms[layer])
    return x


_drawn_inputs = setup_inputs


def setup_inputs(seed=0):
    import zlib

    import numpy as np

    out = dict(_drawn_inputs(seed))
    spreads = {}
    factors = {'l0_q_norm_g': 8.0,
     'l0_k_norm_g': 8.0,
     'l0_dw_b': 8.0,
     'l0_conv_norm_g': 8.0,
     'l0_conv_norm_b': 8.0,
     'l1_ret_norm_g': 23.91,
     'l1_ln_mix_g': 2.69,
     'l1_ln_mix_b': 2.761,
     'l1_ln_ffn_g': 7.813,
     'l1_ln_ffn_b': 8.713}
    for name, (base, spread) in spreads.items():
        noise = np.random.default_rng([zlib.crc32(name.encode()), seed]).standard_normal(out[name].shape)
        drawn = base * np.exp(spread * noise) if base else spread * noise
        out[name] = __import__('jax').numpy.asarray(drawn.astype(out[name].dtype))
    for name, factor in factors.items():
        out[name] = (out[name] * factor).astype(out[name].dtype)
    return out
```

```python
from contextlib import ExitStack

import numpy as np

import concourse.bass as bass
from concourse import mybir

ALU = mybir.AluOpType
ACT = mybir.ActivationFunctionType
AX = mybir.AxisListType
F32 = mybir.dt.float32
F32R = mybir.dt.float32r

P = 128
SEQ = 512
D = 1024
TT = SEQ // P
KD = D // P
N = 512
HIDDEN = 2816
NH = HIDDEN // P
CHUNK = 2048
ALPHA = 4.0 ** 0.25
LN_EPS, RMS_EPS = 1e-5, 1e-6
GRID_W, THETA = 64, 10000.0

HEADS, KV, HD = 8, 2, 64
QK = (HEADS + KV) * HD
CT = 4
TAPS = 31
PAD = TAPS // 2
RH, RK, RV = 4, 256, 512
SPAN = 2 * SEQ - P

C_GLU = 0
C_Q = 4
C_KV = 6
C_OUT0 = 7
C_FFN0 = 11
C_DOWN0 = C_FFN0 + NH
C_RET = C_DOWN0 + NH // 2
C_OUT1 = C_RET + 6 * RH
C_FFN1 = C_OUT1 + 8
C_DOWN1 = C_FFN1 + NH
N_CHUNKS = C_DOWN1 + NH // 2

SEAMS = (C_FFN0, C_RET, C_FFN1)

FREE = 4


def build_encoder(nc, ins, out):
    ctx = ExitStack()
    with ctx:
        top = [-(-nc.sbuf_base // 32) * 32]

        def place(name, shape, dt, at=None):
            size = 4 * int(np.prod(shape[1:]))
            offset = top[0] if at is None else at
            if at is None:
                top[0] += -(-size // 32) * 32
            return nc.alloc_sbuf_tensor_at(name, shape, dt, offset=offset)

        x_tok = place("x_tok", [P, TT, D], F32)
        xt_at = top[0]
        xT_hi = place("xT_hi", [P, KD, SEQ], F32R)
        xT_lo = place("xT_lo", [P, KD, SEQ], F32R)
        raw = [place(f"raw{s}", [P, CHUNK], F32) for s in range(2)]
        w_hi = [place(f"w_hi{s}", [P, CHUNK], F32R) for s in range(2)]
        w_lo = [place(f"w_lo{s}", [P, CHUNK], F32R) for s in range(2)]
        gb_at = top[0]
        ln_gb = place("ln_gb", [P, 2, D], F32)
        tmp = [place(f"tmp{i}", [P, N], F32) for i in range(4)]
        ident = place("ident", [P, P], F32)
        conv_par = place("conv_par", [P, CT, TAPS + 3], F32)
        qk_gain = place("qk_gain", [P, HEADS + KV, HD], F32)
        rope0 = place("rope0", [P, TT, 2, HD // 2], F32)
        decay = place("decay", [P, 2, RH], F32)
        ret_gain = place("ret_gain", [P, RH * RV // P], F32)
        minus_half = place("minus_half", [P, 16], F32)
        stats = place("stats", [P, TT, 2, 6], F32)
        moments = place("moments", [P, TT, 2], F32)
        var_eps = place("var_eps", [P, TT], F32)
        rstd = place("rstd", [P, TT], F32)
        qk_ms = place("qk_ms", [P, TT, HEADS + KV], F32)
        qk_rstd = place("qk_rstd", [P, TT, HEADS + KV], F32)
        row_max = place("row_max", [P, HEADS * TT], F32)
        neg_max = place("neg_max", [P, HEADS * TT], F32)
        row_sum = place("row_sum", [P, HEADS * TT], F32)
        row_inv = place("row_inv", [P, HEADS * TT], F32)
        work = top[0]
        hT_hi = place("hT_hi", [P, NH, SEQ], F32R, work)
        hT_lo = place("hT_lo", [P, NH, SEQ], F32R, work + NH * SEQ * 4)
        KB = 1024
        catT_hi = place("catT_hi", [P, KD, SEQ], F32R, work)
        catT_lo = place("catT_lo", [P, KD, SEQ], F32R, work + 16 * KB)
        qk_tok = place("qk_tok", [P, TT, QK], F32, work)
        roped = place("roped", [P, TT, (HEADS + 2 * KV) * HD], F32, work + 12 * KB)
        qT_hi = place("qT_hi", [P, 4, SEQ], F32R, work + 32 * KB)
        qT_lo = place("qT_lo", [P, 4, SEQ], F32R, work + 40 * KB)
        kT_hi = place("kT_hi", [P, KV, 2, SEQ], F32R, work + 48 * KB)
        kT_lo = place("kT_lo", [P, KV, 2, SEQ], F32R, work + 56 * KB)
        v_hi = place("v_hi", [P, TT, KV, 2, P], F32R, work + 64 * KB)
        v_lo = place("v_lo", [P, TT, KV, 2, P], F32R, work + 72 * KB)
        zpad = place("zpad", [P, CT, SEQ + 2 * PAD], F32, work + 80 * KB)
        conv_norm = place("conv_norm", [P, TT, CT * P], F32, work + 80 * KB)
        acc = place("acc", [P, CT, SEQ], F32, gb_at)
        probT_hi = place("probT_hi", [P, 2, TT, SEQ], F32R, xt_at)
        probT_lo = place("probT_lo", [P, 2, TT, SEQ], F32R, xt_at + 16 * KB)
        y_tok = place("y_tok", [P, TT, RH * RV], F32, work)
        rq_hi = place("rq_hi", [P, 2, SEQ], F32R, work + 32 * KB)
        rq_lo = place("rq_lo", [P, 2, SEQ], F32R, work + 36 * KB)
        rk_hi = place("rk_hi", [P, 2, SEQ], F32R, work + 40 * KB)
        rk_lo = place("rk_lo", [P, 2, SEQ], F32R, work + 44 * KB)
        rv_hi = place("rv_hi", [P, TT, RV], F32R, work + 48 * KB)
        rv_lo = place("rv_lo", [P, TT, RV], F32R, work + 56 * KB)
        sT_hi = place("sT_hi", [P, 2, SEQ], F32R, work + 64 * KB)
        sT_lo = place("sT_lo", [P, 2, SEQ], F32R, work + 68 * KB)
        ahead = place("ahead", [P, SPAN], F32, work + 72 * KB)
        behind = place("behind", [P, SPAN], F32, work + 72 * KB + 4 * SPAN)
        mask = place("mask", [P, SPAN], F32, work + 72 * KB + 8 * SPAN)
        mask_b = place("mask_b", [P, SPAN], F32, work + 72 * KB + 12 * SPAN)
        yT_hi = place("yT_hi", [P, 8, SEQ], F32R, work + 32 * KB)
        yT_lo = place("yT_lo", [P, 8, SEQ], F32R, work + 48 * KB)
        rope1 = place("rope1", [P, 2, SEQ], F32, gb_at)

        ps = ctx.enter_context(nc.psum_tensor("ps", [P, 8, N], F32))

        def f32(ap):
            return ap.bitcast(F32)

        def sem(name):
            return ctx.enter_context(nc.semaphore(name))

        raw_landed = [sem(f"raw_landed{s}") for s in range(2)]
        x_landed = [sem(f"x_landed{t}") for t in range(TT)]
        par_landed = sem("par_landed")
        gb_landed = sem("gb_landed")
        rope1_landed = sem("rope1_landed")
        out_landed = sem("out_landed")
        hi_made = sem("hi_made")
        lo_made = sem("lo_made")
        seam_lo_made = sem("seam_lo_made")
        chunk_used = sem("chunk_used")
        part_made = sem("part_made")
        consts_made = sem("consts_made")
        dve_own = sem("dve_own")
        stats_seen = sem("stats_seen")
        turned = sem("turned")
        xT_hi_made = sem("xT_hi_made")
        xT_lo_made = sem("xT_lo_made")
        var_made = sem("var_made")
        rstd_made = sem("rstd_made")
        x_normed = sem("x_normed")
        resid_read = sem("resid_read")
        gate_read = sem("gate_read")
        up_read = sem("up_read")
        h_hi_made = sem("h_hi_made")
        h_lo_made = sem("h_lo_made")
        sig_made = sem("sig_made")
        z_made = sem("z_made")
        tap_done = sem("tap_done")
        q_copied = sem("q_copied")
        k_copied = sem("k_copied")
        vh_made = sem("vh_made")
        v_split = sem("v_split")
        sq_made = sem("sq_made")
        ms_made = sem("ms_made")
        qk_scaled = sem("qk_scaled")
        pool_own = sem("pool_own")
        rope_made = sem("rope_made")
        qk_turned = sem("qk_turned")
        qkT_hi_made = sem("qkT_hi_made")
        qkT_lo_made = sem("qkT_lo_made")
        scores_made = sem("scores_made")
        max_made = sem("max_made")
        exp_made = sem("exp_made")
        inv_made = sem("inv_made")
        prob_made = sem("prob_made")
        prob_turned = sem("prob_turned")
        probT_hi_made = sem("probT_hi_made")
        probT_lo_made = sem("probT_lo_made")
        head_done = sem("head_done")
        cat_hi_made = sem("cat_hi_made")
        cat_lo_made = sem("cat_lo_made")
        conv_turned = sem("conv_turned")
        conv_var = sem("conv_var")
        conv_rstd = sem("conv_rstd")
        conv_normed = sem("conv_normed")
        conv_back = sem("conv_back")
        silu_made = sem("silu_made")
        rot_made = sem("rot_made")
        rot_hi = sem("rot_hi")
        rot_lo = sem("rot_lo")
        rv_hi_made = sem("rv_hi_made")
        rv_lo_made = sem("rv_lo_made")
        exponent_made = sem("exponent_made")
        mask_made = sem("mask_made")
        ret_scored = sem("ret_scored")
        ret_masked = sem("ret_masked")
        sT_hi_made = sem("sT_hi_made")
        sT_lo_made = sem("sT_lo_made")
        sT_used = sem("sT_used")
        o_made = sem("o_made")
        o_var = sem("o_var")
        o_rstd = sem("o_rstd")
        o_normed = sem("o_normed")
        g_read = sem("g_read")
        y_made = sem("y_made")
        y_turned = sem("y_turned")
        yT_hi_made = sem("yT_hi_made")
        yT_lo_made = sem("yT_lo_made")
        yT_used = sem("yT_used")

        PM_GLU, PM_Q, PM_KV, PM_OUT0, PM_FFN0 = 0, 4, 7, 10, 13
        PM_DOWN0 = PM_FFN0 + NH
        PM_RET = PM_DOWN0 + 3
        PM_OUT1A = PM_RET + RH * (2 + 3 + 3)
        PM_OUT1B = PM_OUT1A + 3
        PM_FFN1 = PM_OUT1B + 3
        PM_DOWN1 = PM_FFN1 + NH

        def by_row_tile(w):
            return w.rearrange("(k p) n -> p k n", p=P)

        W0, WO0 = by_row_tile(ins["l0_w_in"]), by_row_tile(ins["l0_w_out"])
        W1, WO1 = by_row_tile(ins["l1_w_in"]), by_row_tile(ins["l1_w_out"])
        gate_w = [by_row_tile(ins[f"l{i}_ffn_w_gate"]) for i in range(2)]
        up_w = [by_row_tile(ins[f"l{i}_ffn_w_up"]) for i in range(2)]
        down_w = [by_row_tile(ins[f"l{i}_ffn_w_down"]) for i in range(2)]
        A0 = HEADS * HD + 2 * KV * HD

        class Chunk:

            def __init__(self, first, turn=0, stride=2):
                self.s = first % 2
                self.first = first
                self.c = first + stride * turn
                self.nth = first // 2 + stride // 2 * turn
                self.lo = self.c + 1 - 2 * sum(first >= seam for seam in SEAMS)

        def wait_split(eng, c):
            for n, seam in enumerate(SEAMS):
                if seam <= c < seam + 2:
                    eng.wait_ge(seam_lo_made, 2 * n + c - seam + 1)
                    return
            eng.wait_ge(lo_made, Chunk(c).lo)

        def load(eng, ch, src, looped=False):
            if looped:
                eng.wait_ge(lo_made, ch.lo - 2)
            elif ch.first >= 2:
                wait_split(eng, ch.first - 2)
            k, n = src.shape[1], src.shape[2]
            eng.dma_start(raw[ch.s][:].rearrange("p (k n) -> p k n", k=k), src)\
               .then_inc(raw_landed[ch.s], 16)

        def make_hi(act, ch):
            act.wait_ge(raw_landed[ch.s], 16 * ch.nth + 16)
            if ch.first >= 2:
                act.wait_ge(chunk_used, ch.c - 1)
            act.activation(w_hi[ch.s][:], raw[ch.s][:], ACT.Copy).then_inc(hi_made, 1)

        def make_lo(eng, ch, made=lo_made):
            eng.wait_ge(hi_made, ch.c + 1)
            eng.tensor_tensor(w_lo[ch.s][:], raw[ch.s][:], f32(w_hi[ch.s][:]), ALU.subtract)\
               .then_inc(made, 1)

        block = ctx.enter_context(nc.Block())

        @block.sync
        def _(sp):
            for t in range(TT):
                sp.dma_start(x_tok[:, t, :], ins["x"][0, t * P:(t + 1) * P, :]).then_inc(x_landed[t], 16)
            for p in range(2):
                load(sp, Chunk(C_GLU + 2 * p), W0[:, :, A0 + 256 * p:A0 + 256 * p + 256])
                load(sp, Chunk(C_GLU + 2 * p + 1), W0[:, :, A0 + 512 + 256 * p:A0 + 768 + 256 * p])
            for j in range(2):
                load(sp, Chunk(C_Q + j), W0[:, 4 * j:4 * j + 4, 0:512])
            load(sp, Chunk(C_KV), W0[:, :, 512:768])
            for j in range(4):
                load(sp, Chunk(C_OUT0 + j), WO0[:, 2 * j:2 * j + 2, :])

            def norm_params(d, name):
                sp.dma_start(ln_gb[:, 0, :], ins[f"{name}_g"].partition_broadcast(P)).then_inc(gb_landed, 16)
                sp.dma_start(ln_gb[:, 1, :], ins[f"{name}_b"].partition_broadcast(P)).then_inc(gb_landed, 16)

            def ffn_loads(layer, c_ffn, c_down):
                for i in range(2):
                    for k, w in enumerate((gate_w[layer], up_w[layer])):
                        load(sp, Chunk(c_ffn + 2 * i + k), w[:, :, i * 256:i * 256 + 256])
                with sp.Fori(2, NH // 2) as i:
                    load(sp, Chunk(c_ffn, i), gate_w[layer][:, :, bass.ds(i * 256, 256)], looped=True)
                    load(sp, Chunk(c_ffn + 1, i), up_w[layer][:, :, bass.ds(i * 256, 256)], looped=True)
                for j in range(NH // 2):
                    if j == 2:
                        sp.wait_ge(x_normed, 4 * (2 * layer + 1))
                        norm_params(2 * layer + 1, f"l{layer}_ln_ffn")
                    load(sp, Chunk(c_down + j), down_w[layer][:, 2 * j:2 * j + 2, :])

            sp.wait_ge(conv_turned, TT)
            norm_params(0, "l0_ln_mix")
            ffn_loads(0, C_FFN0, C_DOWN0)
            for c in range(2):
                load(sp, Chunk(C_RET + c), W1[:, :, D * c:D * c + 256])
            sp.wait_ge(x_normed, 4 * 2)
            sp.dma_start(rope1[:], ins["rope1"]).then_inc(rope1_landed, 16)
            for h in range(RH):
                if h:
                    for c in range(2):
                        load(sp, Chunk(C_RET + c + 6 * h), W1[:, :, D * c + RK * h:D * c + RK * h + 256])
                for c in range(4):
                    col = 2 * D + RH * RV * (c // 2) + RV * h
                    load(sp, Chunk(C_RET + 2 + c + 6 * h), W1[:, 4 * (c % 2):4 * (c % 2) + 4, col:col + RV])
            for j in range(8):
                if j == 2:
                    sp.wait_ge(rot_made, 4 * RH)
                    norm_params(2, "l1_ln_mix")
                kt, col = 4 * (j % 4), N * (j // 4)
                load(sp, Chunk(C_OUT1 + j), WO1[:, kt:kt + 4, col:col + N])
            ffn_loads(1, C_FFN1, C_DOWN1)
            for t in range(TT):
                sp.wait_ge(x_normed, 4 * 3 + t + 1)
                sp.dma_start(out[0, t * P:(t + 1) * P, :], x_tok[:, t, :]).then_inc(out_landed, 16)
            sp.wait_ge(out_landed, 16 * TT)

        @block.gpsimd
        def _(pool):
            own = [0]

            def mine(instruction):
                own[0] += 1
                instruction.then_inc(pool_own, 1)
                pool.wait_ge(pool_own, own[0])

            mine(nc.gpsimd.memset(ident[:], 0.0))
            mine(nc.gpsimd.affine_select(out=ident[:], in_=ident[:], compare_op=ALU.not_equal, fill=1.0,
                                         base=0, pattern=[[-1, P]], channel_multiplier=1))
            nc.gpsimd.memset(minus_half[:], -0.5).then_inc(consts_made, 1)
            nc.gpsimd.memset(zpad[:], 0.0).then_inc(consts_made, 1)
            for z in (kT_hi, kT_lo, v_hi, v_lo):
                nc.gpsimd.memset(f32(z[:]), 0.0).then_inc(consts_made, 1)

            def lo_at_seam(c):
                for k in range(2):
                    make_lo(pool, Chunk(c + k), seam_lo_made)

            pool.wait_ge(par_landed, 16 * 6)
            for t in range(TT):
                pool.wait_ge(ms_made, t + 1)
                mine(nc.gpsimd.tensor_tensor(qk_rstd[:, t, :], qk_ms[:, t, :], minus_half[:, 0:HEADS + KV], ALU.pow))
                view = qk_tok[:, t, :].rearrange("p (h d) -> p h d", d=HD)
                mine(nc.gpsimd.tensor_tensor(view, view, qk_rstd[:, t, :].unsqueeze(2).broadcast_to([P, HEADS + KV, HD]),
                                             ALU.mult))
                nc.gpsimd.tensor_tensor(view, view, qk_gain[:], ALU.mult).then_inc(qk_scaled, 1)
            for s in range(HEADS * TT):
                pool.wait_ge(inv_made, s + 1)
                prob = tmp[s % 3]
                nc.gpsimd.tensor_tensor(prob[:], prob[:], row_inv[:, s:s + 1].broadcast_to([P, SEQ]), ALU.mult)\
                    .then_inc(prob_made, 1)
            for t in range(TT):
                pool.wait_ge(conv_var, t + 1)
                nc.gpsimd.tensor_tensor(rstd[:, t:t + 1], var_eps[:, t:t + 1], minus_half[:, 0:1], ALU.pow)\
                    .then_inc(conv_rstd, 1)

            def norm_rstd(d):
                for t in range(TT):
                    pool.wait_ge(var_made, 4 * d + t + 1)
                    nc.gpsimd.tensor_tensor(rstd[:, t:t + 1], var_eps[:, t:t + 1], minus_half[:, 0:1], ALU.pow)\
                        .then_inc(rstd_made, 1)

            norm_rstd(0)
            lo_at_seam(C_FFN0)
            norm_rstd(1)
            lo_at_seam(C_RET)
            pool.wait_ge(x_normed, 4 * 2)
            mine(nc.gpsimd.iota(mask[:], pattern=[[1, SPAN]], base=-(SEQ - P), channel_multiplier=-1,
                                allow_small_or_imprecise_dtypes=True))
            mine(nc.gpsimd.tensor_scalar(ahead[:], mask[:], 0.0, None, ALU.max))
            mine(nc.gpsimd.tensor_tensor(behind[:], ahead[:], mask[:], ALU.subtract))
            base = own[0]
            with pool.Fori(0, RH) as h:
                pool.wait_ge(ret_masked, 4 * h + FREE)
                nc.gpsimd.tensor_tensor(mask[:], ahead[:], decay[:, 0, bass.ds(h, 1)].broadcast_to([P, SPAN]), ALU.mult)\
                    .then_inc(pool_own, 1)
                nc.gpsimd.tensor_tensor(mask_b[:], behind[:], decay[:, 1, bass.ds(h, 1)].broadcast_to([P, SPAN]), ALU.mult)\
                    .then_inc(pool_own, 1)
                pool.wait_ge(pool_own, base + 2 * h + 2)
                nc.gpsimd.tensor_tensor(mask[:], mask[:], mask_b[:], ALU.add).then_inc(exponent_made, 1)
                for t in range(TT):
                    pool.wait_ge(o_var, 4 * h + t + 1)
                    nc.gpsimd.tensor_tensor(rstd[:, t:t + 1], var_eps[:, t:t + 1], minus_half[:, 0:1], ALU.pow)\
                        .then_inc(o_rstd, 1)
            norm_rstd(2)
            lo_at_seam(C_FFN1)
            norm_rstd(3)

        @block.scalar
        def _(act):
            for dst, src in ((conv_par[:], ins["conv_par"]),
                             (qk_gain[:, 0:HEADS, :], ins["l0_q_norm_g"].partition_broadcast(P).unsqueeze(1)
                              .broadcast_to([P, HEADS, HD])),
                             (qk_gain[:, HEADS:HEADS + KV, :], ins["l0_k_norm_g"].partition_broadcast(P).unsqueeze(1)
                              .broadcast_to([P, KV, HD])),
                             (rope0[:], ins["rope0"]),
                             (decay[:], ins["decay"].partition_broadcast(P)),
                             (ret_gain[:], ins["ret_gain"])):
                act.dma_start(dst, src).then_inc(par_landed, 16)

            def xT_tile_hi(stage, t):
                for half in range(2):
                    n = 8 * stage + 2 * t + half
                    act.wait_ge(turned, n + 1)
                    nc.scalar.activation(xT_hi[:, 4 * half:4 * half + 4, t * P:(t + 1) * P],
                                         ps[:, t + 4 * half, :].rearrange("p (k c) -> p k c", c=P), ACT.Copy)\
                        .then_inc(xT_hi_made, 1)

            act.preload_act_table(ACT.Sigmoid)
            make_hi(act, Chunk(0))
            for t in range(TT):
                xT_tile_hi(0, t)
                if t == 0:
                    make_hi(act, Chunk(1))
            for p in range(2):
                make_hi(act, Chunk(2 * p + 2))
                for m in range(2):
                    ct = 2 * p + m
                    if m == 0:
                        act.wait_ge(part_made, PM_GLU + 2 * p + 2)
                    else:
                        act.wait_ge(chunk_used, C_GLU + 2 * p + 2)
                        make_hi(act, Chunk(2 * p + 3))
                    if ct:
                        act.wait_ge(z_made, ct)
                    nc.scalar.activation(tmp[3][:], ps[:, 2 + m, :], ACT.Sigmoid).then_inc(sig_made, 1)
            act.preload_act_table(ACT.Exp)
            make_hi(act, Chunk(C_KV))
            for t in range(TT):
                act.wait_ge(part_made, PM_Q + t + 1) if t < TT - 1 else act.wait_ge(chunk_used, C_KV)
                nc.scalar.activation(qk_tok[:, t, 0:HEADS * HD], ps[:, 4 + t, :], ACT.Copy).then_inc(q_copied, 1)
            make_hi(act, Chunk(C_OUT0))
            for t in range(TT):
                act.wait_ge(part_made, PM_KV + t + 1) if t < TT - 1 else act.wait_ge(chunk_used, C_KV + 1)
                nc.scalar.activation(qk_tok[:, t, HEADS * HD:QK], ps[:, t, 0:KV * HD], ACT.Copy).then_inc(k_copied, 1)
                act.wait_ge(q_copied, t + 1)
                act.wait_ge(k_copied, t + 1)
                nc.scalar.activation(roped[:, t, 0:QK], qk_tok[:, t, :], ACT.Square).then_inc(sq_made, 1)
                act.wait_ge(consts_made, 6)
                for side in range(2):
                    nc.scalar.activation(v_hi[:, t, :, side, HD * side:HD * side + HD],
                                         ps[:, t, KV * HD:2 * KV * HD].rearrange("p (g d) -> p g d", d=HD), ACT.Copy)\
                        .then_inc(vh_made, 1)
            make_hi(act, Chunk(C_OUT0 + 1))
            for j in range(4):
                act.wait_ge(qk_turned, j + 1)
                nc.scalar.activation(qT_hi[:, j, :], ps[:, 4 + j, :], ACT.Copy).then_inc(qkT_hi_made, 1)
            for g in range(KV):
                act.wait_ge(qk_turned, 4 + g + 1)
                for side in range(2):
                    rows = slice(HD * side, HD * side + HD)
                    nc.scalar.activation(kT_hi[rows, g, side, :], ps[rows, g, :], ACT.Copy).then_inc(qkT_hi_made, 1)

            def attention_step(s):
                if s < HEADS * TT:
                    act.wait_ge(max_made, s + 1)
                    if s >= 3:
                        act.wait_ge(prob_turned, s - 2)
                    nc.scalar.activation(tmp[s % 3][:], ps[:, s % 3, :], ACT.Exp, bias=neg_max[:, s:s + 1],
                                         scale=HD ** -0.5, accum_out=row_sum[:, s:s + 1]).then_inc(exp_made, 1)
                u = s - 2
                if 0 <= u < HEADS * TT:
                    h, t = u // TT, u % TT
                    act.wait_ge(prob_turned, u + 1)
                    if h >= 2 and t == 0:
                        act.wait_ge(head_done, h - 1)
                    nc.scalar.activation(probT_hi[:, h % 2, :, t * P:(t + 1) * P],
                                         ps[:, 3 + u % 3, :].rearrange("p (k c) -> p k c", c=P), ACT.Copy)\
                        .then_inc(probT_hi_made, 1)
                if s % 8 == 5 and s >= 13:
                    j = (s - 13) // 8
                    act.wait_ge(head_done, 2 * j + 2)
                    nc.scalar.activation(catT_hi[:, j, :], ps[:, 6 + j % 2, :], ACT.Copy).then_inc(cat_hi_made, 1)

            for s in range(HEADS * TT + 6):
                attention_step(s)
            act.preload_act_table(ACT.Silu)
            for ct in range(CT):
                act.wait_ge(conv_back, ct + 1)
                nc.scalar.activation(tmp[ct][:], ps[:, 4 + ct, :], ACT.Silu, bias=conv_par[:, ct, TAPS + 2:TAPS + 3],
                                     scale=conv_par[:, ct, TAPS + 1:TAPS + 2]).then_inc(silu_made, 1)
                act.wait_ge(silu_made, ct + 1)
                nc.scalar.activation(catT_hi[:, 4 + ct, :], tmp[ct][:], ACT.Copy).then_inc(cat_hi_made, 1)

            def seam(stage, c):
                for t in range(TT):
                    xT_tile_hi(stage, t)
                    if t == 1:
                        make_hi(act, Chunk(c))
                    if t == 2:
                        make_hi(act, Chunk(c + 1))

            def swiglu(layer, c_ffn, c_down, pm):
                g0, f0 = NH * layer, (NH + 2) * layer
                act.sem_inc(gate_read, 2)
                with act.Fori(0, NH // 2) as i:
                    for m in range(2):
                        if m == 0:
                            act.wait_ge(part_made, pm + 2 * i + 1)
                        else:
                            act.wait_ge(chunk_used, c_ffn + 2 * i + 1)
                            make_hi(act, Chunk(c_ffn + 2, i))
                        act.wait_ge(up_read, f0 + 2 * i + m + 1)
                        nc.scalar.activation(tmp[m][:], ps[:, m, :], ACT.Silu).then_inc(gate_read, 1)
                    for m in range(2):
                        act.wait_ge(up_read, f0 + 2 * i + m + 3)
                        nc.scalar.activation(hT_hi[:, bass.ds(2 * i + m, 1), :], tmp[2 + m][:].unsqueeze(1), ACT.Copy)\
                            .then_inc(h_hi_made, 1)
                        if m == 0:
                            make_hi(act, Chunk(c_ffn + 3, i))
                for j in range(NH // 2 - 2):
                    make_hi(act, Chunk(c_down + j + 2))

            for j in range(2):
                make_hi(act, Chunk(C_OUT0 + 2 + j))
            seam(1, C_FFN0)
            swiglu(0, C_FFN0, C_DOWN0, PM_FFN0)
            seam(2, C_RET)
            act.sem_inc(g_read, FREE)
            with act.Fori(0, RH) as h:
                make_hi(act, Chunk(C_RET + 2, h, 6))
                for x, dst in ((0, rq_hi), (1, rk_hi)):
                    for half in range(2):
                        act.wait_ge(rot_made, 4 * h + 2 * x + half + 1)
                        nc.scalar.activation(dst[:, half, :], tmp[2 + half][:], ACT.Copy).then_inc(rot_hi, 1)
                    if x == 0:
                        make_hi(act, Chunk(C_RET + 3, h, 6))
                act.wait_ge(exponent_made, h + 1)
                nc.scalar.activation(mask[:], mask[:], ACT.Exp).then_inc(mask_made, 1)
                make_hi(act, Chunk(C_RET + 4, h, 6))
                for t in range(TT):
                    if t < TT - 1:
                        act.wait_ge(part_made, PM_RET + 8 * h + 2 + t + 1)
                    else:
                        act.wait_ge(chunk_used, C_RET + 6 * h + 4)
                    nc.scalar.activation(rv_hi[:, t, :], ps[:, 4 + t, :], ACT.Copy).then_inc(rv_hi_made, 1)
                make_hi(act, Chunk(C_RET + 5, h, 6))
                for kt in range(TT):
                    act.wait_ge(ret_masked, 4 * h + kt + 1 + FREE)
                    if kt >= 2:
                        act.wait_ge(sT_used, 3 * h + kt - 1)
                    nc.scalar.activation(sT_hi[:, kt % 2, :], tmp[kt % 2][:], ACT.Copy).then_inc(sT_hi_made, 1)
                make_hi(act, Chunk(C_RET + 6, h, 6))
                for t in range(TT):
                    if t < TT - 1:
                        act.wait_ge(part_made, PM_RET + 8 * h + 5 + t + 1)
                    else:
                        act.wait_ge(chunk_used, C_RET + 6 * h + 6)
                    if t >= 2:
                        act.wait_ge(y_made, 4 * h + t - 1)
                    else:
                        act.wait_ge(rot_lo, 4 * h + 4)
                    nc.scalar.activation(tmp[2 + t % 2][:], ps[:, t, :], ACT.Silu).then_inc(g_read, 1)
                make_hi(act, Chunk(C_RET + 7, h, 6))

            for q in range(32):
                kt = q % 16
                act.wait_ge(y_turned, q + 1)
                if q >= 8:
                    if q % 4 == 3:
                        act.wait_ge(chunk_used, C_OUT1 + (q - 8) // 4 + 1)
                    else:
                        act.wait_ge(yT_used, q - 7 - (q - 8) // 4)
                nc.scalar.activation(yT_hi[:, q % 8, :], ps[:, 4 + q % 4 if q < 20 else q % 4, :], ACT.Copy,
                                     scale=ret_gain[:, kt:kt + 1]).then_inc(yT_hi_made, 1)
                if q % 4 == 3 and 7 <= q < 28:
                    make_hi(act, Chunk(C_OUT1 + (q - 7) // 4 + 2))
            seam(3, C_FFN1)
            swiglu(1, C_FFN1, C_DOWN1, PM_FFN1)

        @block.vector
        def _(dve):
            class Own:
                n, per_turn, turn = 0, 0, 0

                def value(self):
                    return self.n + self.per_turn * self.turn if self.per_turn else self.n

            own = Own()

            def mine(instruction, wait=True):
                instruction.then_inc(dve_own, 1)
                own.n += 1
                if wait:
                    dve.wait_ge(dve_own, own.value())

            def xT_tile_lo(stage, t):
                for half in range(2):
                    n = 8 * stage + 2 * t + half
                    dve.wait_ge(xT_hi_made, n + 1)
                    spot = (slice(None), slice(4 * half, 4 * half + 4), slice(t * P, (t + 1) * P))
                    nc.vector.tensor_tensor(xT_lo[spot], ps[:, t + 4 * half, :].rearrange("p (k c) -> p k c", c=P),
                                            f32(xT_hi[spot]), ALU.subtract).then_inc(xT_lo_made, 1)

            taps = [(2 * pair + c, k) for pair in range(2) for k in range(TAPS) for c in range(2)]
            tapped = [0]

            def conv(count):
                for ct, k in taps[tapped[0]:tapped[0] + count]:
                    o = tapped[0]
                    if k == 0:
                        dve.wait_ge(par_landed, 16 * 6)
                        dve.wait_ge(z_made, ct + 1)
                        nc.vector.tensor_scalar(acc[:, ct, :], zpad[:, ct, k:k + SEQ], conv_par[:, ct, k:k + 1],
                                                conv_par[:, ct, TAPS:TAPS + 1], ALU.mult, ALU.add).then_inc(tap_done, 1)
                    else:
                        dve.wait_ge(tap_done, o - 1)
                        nc.vector.scalar_tensor_tensor(acc[:, ct, :], zpad[:, ct, k:k + SEQ], conv_par[:, ct, k:k + 1],
                                                       acc[:, ct, :], ALU.mult, ALU.add).then_inc(tap_done, 1)
                    tapped[0] += 1

            make_lo(dve, Chunk(0))
            for t in range(TT):
                xT_tile_lo(0, t)
                if t == 0:
                    make_lo(dve, Chunk(1))
            dve.wait_ge(consts_made, 2)
            for p in range(2):
                make_lo(dve, Chunk(2 * p + 2))
                for m in range(2):
                    ct = 2 * p + m
                    if m:
                        make_lo(dve, Chunk(2 * p + 3))
                    dve.wait_ge(sig_made, ct + 1)
                    nc.vector.tensor_tensor(zpad[:, ct, PAD:PAD + SEQ], tmp[3][:], ps[:, m, :], ALU.mult)\
                        .then_inc(z_made, 1)
                    if ct:
                        conv(8)
            make_lo(dve, Chunk(C_KV))
            conv(8)
            make_lo(dve, Chunk(C_OUT0))
            def qk_mean_square(t):
                dve.wait_ge(sq_made, t + 1)
                mine(nc.vector.tensor_reduce(qk_ms[:, t, :], roped[:, t, 0:QK].rearrange("p (h d) -> p h d", d=HD),
                                             AX.X, ALU.add))
                nc.vector.tensor_scalar(qk_ms[:, t, :], qk_ms[:, t, :], 1.0 / HD, RMS_EPS, ALU.mult, ALU.add)\
                    .then_inc(ms_made, 1)

            def v_tile_lo(t):
                dve.wait_ge(vh_made, 2 * t + 2)
                for side in range(2):
                    cols = slice(HD * side, HD * side + HD)
                    nc.vector.tensor_tensor(v_lo[:, t, :, side, cols],
                                            ps[:, t, KV * HD:2 * KV * HD].rearrange("p (g d) -> p g d", d=HD),
                                            f32(v_hi[:, t, :, side, cols]), ALU.subtract).then_inc(v_split, 1)

            def rope_tile(t):
                dve.wait_ge(qk_scaled, t + 1)
                x = qk_tok[:, t, :].rearrange("p (h s d) -> p h s d", s=2, d=HD // 2)
                cos, sin = (rope0[:, t, i, :].unsqueeze(1).broadcast_to([P, HEADS + KV, HD // 2]) for i in range(2))
                a = tmp[0][:, 0:QK // 2].rearrange("p (h d) -> p h d", d=HD // 2)
                b = tmp[1][:, 0:QK // 2].rearrange("p (h d) -> p h d", d=HD // 2)
                q_out = roped[:, t, 0:HEADS * HD].rearrange("p (h s d) -> p h s d", s=2, d=HD // 2)
                k_out = roped[:, t, HEADS * HD:].rearrange("p (h r s d) -> p h r s d", r=2, s=2, d=HD // 2)
                for s, op in ((0, ALU.subtract), (1, ALU.add)):
                    mine(nc.vector.tensor_tensor(a, x[:, :, 0, :], (cos, sin)[s], ALU.mult), wait=False)
                    mine(nc.vector.tensor_tensor(b, x[:, :, 1, :], (sin, cos)[s], ALU.mult))
                    mine(nc.vector.tensor_tensor(q_out[:, :, s, :], a[:, 0:HEADS], b[:, 0:HEADS], op), wait=False)
                    for r in range(2):
                        last = nc.vector.tensor_tensor(k_out[:, :, r, s, :], a[:, HEADS:], b[:, HEADS:], op)
                        if (s, r) == (1, 1):
                            last.then_inc(rope_made, 1)
                        else:
                            mine(last, wait=False)
                    dve.wait_ge(dve_own, own.value())
                dve.wait_ge(rope_made, t + 1)

            for t in range(TT):
                qk_mean_square(t)
                v_tile_lo(t)
            make_lo(dve, Chunk(C_OUT0 + 1))
            for t in range(TT):
                conv(2)
                rope_tile(t)
            for j in range(4):
                dve.wait_ge(qkT_hi_made, j + 1)
                nc.vector.tensor_tensor(qT_lo[:, j, :], ps[:, 4 + j, :], f32(qT_hi[:, j, :]), ALU.subtract)\
                    .then_inc(qkT_lo_made, 1)
            for g in range(KV):
                for side in range(2):
                    rows = slice(HD * side, HD * side + HD)
                    dve.wait_ge(qkT_hi_made, 4 + 2 * g + side + 1)
                    nc.vector.tensor_tensor(kT_lo[rows, g, side, :], ps[rows, g, :], f32(kT_hi[rows, g, side, :]),
                                            ALU.subtract).then_inc(qkT_lo_made, 1)

            def attention_step(s):
                if s < HEADS * TT:
                    dve.wait_ge(scores_made, s + 1)
                    mine(nc.vector.tensor_reduce(row_max[:, s:s + 1], ps[:, s % 3, :], AX.X, ALU.max))
                    nc.vector.tensor_scalar(neg_max[:, s:s + 1], row_max[:, s:s + 1], -HD ** -0.5, None, ALU.mult)\
                        .then_inc(max_made, 1)
                conv(2)
                u = s - 1
                if 0 <= u < HEADS * TT:
                    dve.wait_ge(exp_made, u + 1)
                    nc.vector.reciprocal(row_inv[:, u:u + 1], row_sum[:, u:u + 1]).then_inc(inv_made, 1)
                u = s - 3
                if 0 <= u < HEADS * TT:
                    h, t = u // TT, u % TT
                    dve.wait_ge(probT_hi_made, u + 1)
                    spot = (slice(None), h % 2, slice(None), slice(t * P, (t + 1) * P))
                    nc.vector.tensor_tensor(probT_lo[spot], ps[:, 3 + u % 3, :].rearrange("p (k c) -> p k c", c=P),
                                            f32(probT_hi[spot]), ALU.subtract).then_inc(probT_lo_made, 1)
                conv(1)
                if s % 8 == 5 and s >= 13:
                    j = (s - 13) // 8
                    dve.wait_ge(cat_hi_made, j + 1)
                    nc.vector.tensor_tensor(catT_lo[:, j, :], ps[:, 6 + j % 2, :], f32(catT_hi[:, j, :]), ALU.subtract)\
                        .then_inc(cat_lo_made, 1)

            for s in range(HEADS * TT + 6):
                attention_step(s)
            conv(len(taps))

            def variance(t, halves, made, eps):
                for i, x in enumerate(halves):
                    mine(nc.vector.bn_stats(stats[:, t, i, :], x), wait=(i == len(halves) - 1))
                if own.per_turn:
                    dve.sem_inc(stats_seen, 1)
                mine(nc.vector.bn_aggr(moments[:, t, :], stats[:, t, 0:len(halves), :]))
                nc.vector.tensor_scalar(var_eps[:, t:t + 1], moments[:, t, 1:2], eps, None, ALU.add).then_inc(made, 1)

            for t in range(TT):
                dve.wait_ge(conv_turned, t + 1)
                variance(t, [ps[:, t, :]], conv_var, LN_EPS)
            for t in range(TT):
                dve.wait_ge(conv_rstd, t + 1)
                nc.vector.tensor_scalar(conv_norm[:, t, :], ps[:, t, :], moments[:, t, 0:1], rstd[:, t:t + 1],
                                        ALU.subtract, ALU.mult).then_inc(conv_normed, 1)
            for ct in range(CT):
                dve.wait_ge(cat_hi_made, 4 + ct + 1)
                nc.vector.tensor_tensor(catT_lo[:, 4 + ct, :], tmp[ct][:], f32(catT_hi[:, 4 + ct, :]), ALU.subtract)\
                    .then_inc(cat_lo_made, 1)
            for j in range(2):
                make_lo(dve, Chunk(C_OUT0 + 2 + j))

            def layer_norm(d, tile_sums, halves=(0, 1), turn=True):
                def first(t):
                    tile_sums(t)
                    for half in halves:
                        cols = slice(N * half, N * half + N)
                        mine(nc.vector.scalar_tensor_tensor(x_tok[:, t, cols], x_tok[:, t, cols], ALPHA,
                                                            ps[:, t + 4 * half, :], ALU.mult, ALU.add), wait=(half == 1))
                    variance(t, [x_tok[:, t, 0:N], x_tok[:, t, N:D]], var_made, LN_EPS)

                def second(t):
                    if t == 0:
                        dve.wait_ge(gb_landed, 32 * (d + 1))
                    dve.wait_ge(rstd_made, 4 * d + t + 1)
                    mine(nc.vector.scalar_tensor_tensor(x_tok[:, t, :], x_tok[:, t, :], moments[:, t, 0:1], ln_gb[:, 0, :],
                                                        ALU.subtract, ALU.mult))
                    nc.vector.scalar_tensor_tensor(x_tok[:, t, :], x_tok[:, t, :], rstd[:, t:t + 1], ln_gb[:, 1, :],
                                                   ALU.mult, ALU.add).then_inc(x_normed, 1)

                for t in range(TT):
                    first(t)
                    second(t)
                    if turn and t:
                        xT_tile_lo(d + 1, t - 1)
                if turn:
                    xT_tile_lo(d + 1, TT - 1)

            def sums(pm, c_last):
                def wait(t):
                    dve.wait_ge(part_made, pm + t + 1) if t < TT - 1 else dve.wait_ge(chunk_used, c_last + 1)
                return wait

            def swiglu(layer, c_ffn, c_down, pm):
                h0, f0 = NH * layer, (NH + 2) * layer
                dve.sem_inc(up_read, 2)
                with dve.Fori(0, NH // 2) as i:
                    for m in range(2):
                        make_lo(dve, Chunk(c_ffn + 2 + m, i))
                        if m == 0:
                            dve.wait_ge(part_made, pm + 2 * i + 2)
                        else:
                            dve.wait_ge(chunk_used, c_ffn + 2 * i + 2)
                        dve.wait_ge(gate_read, f0 + 2 * i + m + 3)
                        nc.vector.tensor_tensor(tmp[2 + m][:], tmp[m][:], ps[:, 2 + m, :], ALU.mult).then_inc(up_read, 1)
                        dve.wait_ge(h_hi_made, h0 + 2 * i + m + 1)
                        nc.vector.tensor_tensor(hT_lo[:, bass.ds(2 * i + m, 1), :], tmp[2 + m][:].unsqueeze(1),
                                                f32(hT_hi[:, bass.ds(2 * i + m, 1), :]), ALU.subtract)\
                            .then_inc(h_lo_made, 1)
                for j in range(NH // 2 - 2):
                    make_lo(dve, Chunk(c_down + j + 2))

            layer_norm(0, sums(PM_OUT0, C_FFN0 - 1))
            swiglu(0, C_FFN0, C_DOWN0, PM_FFN0)
            layer_norm(1, sums(PM_DOWN0, C_RET - 1))

            dve.sem_inc(ret_masked, FREE)
            dve.sem_inc(o_normed, FREE)
            dve.wait_ge(rope1_landed, 16)
            per_head = 12 + 8
            start = own.n
            with dve.Fori(0, RH) as h:
                own.per_turn, own.turn = 16, h
                cos, sin = rope1[:, 0, :], rope1[:, 1, :]
                for x, hi, lo in ((0, rq_hi, rq_lo), (1, rk_hi, rk_lo)):
                    make_lo(dve, Chunk(C_RET + 2 + x, h, 6))
                    dve.wait_ge(chunk_used, C_RET + 6 * h + x + 1)
                    x1, x2 = ps[:, 2 * x, :], ps[:, 2 * x + 1, :]
                    for half, op in ((0, ALU.subtract), (1, ALU.add)):
                        mine(nc.vector.tensor_tensor(tmp[0][:], (cos, sin)[half], x1, ALU.mult), wait=False)
                        mine(nc.vector.tensor_tensor(tmp[1][:], (sin, cos)[half], x2, ALU.mult))
                        nc.vector.tensor_tensor(tmp[2 + half][:], tmp[0][:], tmp[1][:], op).then_inc(rot_made, 1)
                        dve.wait_ge(rot_made, 4 * h + 2 * x + half + 1)
                    for half in range(2):
                        dve.wait_ge(rot_hi, 4 * h + 2 * x + half + 1)
                        nc.vector.tensor_tensor(lo[:, half, :], tmp[2 + half][:], f32(hi[:, half, :]), ALU.subtract)\
                            .then_inc(rot_lo, 1)
                make_lo(dve, Chunk(C_RET + 4, h, 6))
                for t in range(TT):
                    dve.wait_ge(rv_hi_made, 4 * h + t + 1)
                    nc.vector.tensor_tensor(rv_lo[:, t, :], ps[:, 4 + t, :], f32(rv_hi[:, t, :]), ALU.subtract)\
                        .then_inc(rv_lo_made, 1)

                def masked(kt):
                    dve.wait_ge(ret_scored, 4 * h + kt + 1)
                    if kt == 0:
                        dve.wait_ge(mask_made, h + 1)
                    if kt >= 2:
                        dve.wait_ge(sT_lo_made, 4 * h + kt - 1)
                    left = (SEQ - P) - P * kt
                    nc.vector.scalar_tensor_tensor(tmp[kt % 2][:], ps[:, kt, :], RK ** -0.5, mask[:, left:left + SEQ],
                                                   ALU.mult, ALU.mult).then_inc(ret_masked, 1)

                def masked_lo(kt):
                    dve.wait_ge(sT_hi_made, 4 * h + kt + 1)
                    nc.vector.tensor_tensor(sT_lo[:, kt % 2, :], tmp[kt % 2][:], f32(sT_hi[:, kt % 2, :]), ALU.subtract)\
                        .then_inc(sT_lo_made, 1)

                masked(0)
                for kt in range(1, TT):
                    masked(kt)
                    masked_lo(kt - 1)
                masked_lo(TT - 1)
                make_lo(dve, Chunk(C_RET + 5, h, 6))
                for t in range(TT):
                    dve.wait_ge(o_made, 4 * h + t + 1)
                    variance(t, [ps[:, 4 + t, :]], o_var, LN_EPS)
                for t in range(TT):
                    dve.wait_ge(o_rstd, 4 * h + t + 1)
                    nc.vector.tensor_scalar(y_tok[:, t, bass.ds(h * RV, RV)], ps[:, 4 + t, :], moments[:, t, 0:1],
                                            rstd[:, t:t + 1], ALU.subtract, ALU.mult).then_inc(o_normed, 1)
                make_lo(dve, Chunk(C_RET + 6, h, 6))
                for t in range(TT):
                    dve.wait_ge(g_read, 4 * h + t + 1 + FREE)
                    dve.wait_ge(o_normed, 4 * h + t + 1 + FREE)
                    y = y_tok[:, t, bass.ds(h * RV, RV)]
                    nc.vector.tensor_tensor(y, y, tmp[2 + t % 2][:], ALU.mult).then_inc(y_made, 1)
                make_lo(dve, Chunk(C_RET + 7, h, 6))
            assert own.n == start + 16, own.n - start
            own.n = start + 16 * RH
            own.per_turn = 0

            for q in range(32):
                kt, bank = q % 16, 4 + q % 4 if q < 20 else q % 4
                dve.wait_ge(yT_hi_made, q + 1)
                nc.vector.scalar_tensor_tensor(yT_lo[:, q % 8, :], ps[:, bank, :], ret_gain[:, kt:kt + 1],
                                               f32(yT_hi[:, q % 8, :]), ALU.mult, ALU.subtract).then_inc(yT_lo_made, 1)
                if q % 4 == 3 and 7 <= q < 28:
                    make_lo(dve, Chunk(C_OUT1 + (q - 7) // 4 + 2))
                if q == 19:
                    for t in range(TT):
                        sums(PM_OUT1A, C_OUT1 + 3)(t)
                        nc.vector.scalar_tensor_tensor(x_tok[:, t, 0:N], x_tok[:, t, 0:N], ALPHA, ps[:, t, :],
                                                       ALU.mult, ALU.add).then_inc(resid_read, 1)
            dve.wait_ge(resid_read, TT)
            layer_norm(2, sums(PM_OUT1B, C_FFN1 - 1), halves=(1,))
            swiglu(1, C_FFN1, C_DOWN1, PM_FFN1)
            layer_norm(3, sums(PM_DOWN1, N_CHUNKS - 1), turn=False)

        @block.tensor
        def _(pe):
            def product(dst, a, b, start, stop):
                nc.tensor.matmul(dst, a[0], b[0], start=start, stop=False)
                nc.tensor.matmul(dst, a[0], b[1], start=False, stop=False)
                return nc.tensor.matmul(dst, a[1], b[0], start=False, stop=stop)

            def weights(ch, k):
                return tuple(w[ch.s][:].rearrange("p (k n) -> p k n", k=k) for w in (w_hi, w_lo))

            def turn(stage, t):
                for half in range(2):
                    for k in range(4):
                        last = nc.tensor.transpose(ps[:, t + 4 * half, k * P:(k + 1) * P],
                                                   x_tok[:, t, (4 * half + k) * P:(4 * half + k + 1) * P], ident[:])
                    last.then_inc(turned, 1)

            def feature_tiles(ch, banks, bank_free):
                pe.wait_ge(lo_made, ch.lo)
                hi, lo = weights(ch, KD)
                for m in range(2):
                    bank_free(m)
                    cols = slice(m * P, (m + 1) * P)
                    for k in range(KD):
                        last = product(ps[:, banks + m, :], (hi[:, k, cols], lo[:, k, cols]),
                                       (xT_hi[:, k, :], xT_lo[:, k, :]), k == 0, k == KD - 1)
                    last.then_inc(chunk_used if m else part_made, 1)

            def token_tiles(chunks, banks, rows, cols, bank_free):
                for j, ch in enumerate(chunks):
                    pe.wait_ge(lo_made, ch.lo)
                    hi, lo = weights(ch, rows)
                    for k in range(rows):
                        for t in range(TT):
                            if j == 0 and k == 0:
                                bank_free(t)
                            row, tok = rows * j + k, slice(t * P, (t + 1) * P)
                            end = j == len(chunks) - 1 and k == rows - 1
                            last = product(ps[:, banks + t, 0:cols], (xT_hi[:, row, tok], xT_lo[:, row, tok]),
                                           (hi[:, k, :], lo[:, k, :]), row == 0, end)
                            if end and t < TT - 1:
                                last.then_inc(part_made, 1)
                    last.then_inc(chunk_used, 1)

            def out_projection(c, n, sT, ready, stage):
                def part(ch, k, row, t):
                    hi, lo = weights(ch, 2)
                    tok = slice(t * P, (t + 1) * P)
                    for a, b in ((0, 0), (0, 1), (1, 0)):
                        for half in range(2):
                            last = nc.tensor.matmul(ps[:, t + 4 * half, :], sT[a][:, row, tok],
                                                    (hi, lo)[b][:, k, N * half:N * half + N],
                                                    start=(row == 0 and a == b), stop=(row == 2 * n - 1 and a == 1))
                    return last

                for j in range(n - 2):
                    wait_split(pe, c + j)
                    for k in range(2):
                        ready(2 * j + k)
                        for t in range(TT):
                            last = part(Chunk(c + j), k, 2 * j + k, t)
                    last.then_inc(chunk_used, 1)
                for j in (n - 2, n - 1):
                    wait_split(pe, c + j)
                for row in range(2 * n - 4, 2 * n):
                    ready(row)
                for t in range(TT):
                    for j in (n - 2, n - 1):
                        for k in range(2):
                            last = part(Chunk(c + j), k, 2 * j + k, t)
                        if t == TT - 1:
                            last.then_inc(chunk_used, 1)
                        elif j == n - 1:
                            last.then_inc(part_made, 1)
                    if stage is not None and t == TT - 2:
                        turn_when_normed(stage, 0)
                if stage is not None:
                    for t in range(1, TT):
                        turn_when_normed(stage, t)

            def turn_when_normed(stage, t):
                pe.wait_ge(x_normed, 4 * (stage - 1) + t + 1)
                turn(stage, t)

            pe.wait_ge(pool_own, 2)
            for t in range(TT):
                pe.wait_ge(x_landed[t], 16)
                turn(0, t)
            pe.wait_ge(xT_lo_made, 8)
            for p in range(2):
                for part in range(2):
                    feature_tiles(Chunk(C_GLU + 2 * p + part), 2 * part,
                                  lambda m, p=p: pe.wait_ge(z_made, m + 1) if p else None)
            token_tiles([Chunk(C_Q), Chunk(C_Q + 1)], 4, 4, N, lambda t: None)
            token_tiles([Chunk(C_KV)], 0, KD, 256, lambda t: pe.wait_ge(z_made, 4) if t == 0 else None)
            pe.wait_ge(q_copied, TT)
            pe.wait_ge(v_split, 2 * TT)
            for t in range(TT):
                pe.wait_ge(rope_made, t + 1)
                for j in range(6):
                    last = nc.tensor.transpose(ps[:, 4 + j if j < 4 else j - 4, t * P:(t + 1) * P],
                                               roped[:, t, j * P:(j + 1) * P], ident[:])
                    if t == TT - 1:
                        last.then_inc(qk_turned, 1)

            def attention_step(s):
                if s < HEADS * TT:
                    h, t = s // TT, s % TT
                    if s < 3:
                        pe.wait_ge(qkT_lo_made, 8)
                    else:
                        pe.wait_ge(exp_made, s - 2)
                    q = tuple(x[:, h // 2, t * P:(t + 1) * P] for x in (qT_hi, qT_lo))
                    k = tuple(x[:, h // (HEADS // KV), h % 2, :] for x in (kT_hi, kT_lo))
                    product(ps[:, s % 3, :], q, k, True, True).then_inc(scores_made, 1)
                u = s - 2
                if 0 <= u < HEADS * TT:
                    pe.wait_ge(prob_made, u + 1)
                    if u >= 3:
                        pe.wait_ge(probT_lo_made, u - 2)
                    for k in range(TT):
                        last = nc.tensor.transpose(ps[:, 3 + u % 3, k * P:(k + 1) * P],
                                                   tmp[u % 3][:, k * P:(k + 1) * P], ident[:])
                    last.then_inc(prob_turned, 1)
                if s >= 8 and s % 4 == 0 and (s - 8) // 4 < HEADS:
                    h = (s - 8) // 4
                    pe.wait_ge(probT_lo_made, 4 * h + 4)
                    if h % 2 == 0 and h >= 4:
                        pe.wait_ge(cat_lo_made, h // 2 - 1)
                    g = h // (HEADS // KV)
                    for k in range(TT):
                        v = (v_hi[:, k, g, h % 2, :], v_lo[:, k, g, h % 2, :])
                        last = product(ps[:, 6 + (h // 2) % 2, :], v, (probT_hi[:, h % 2, k, :], probT_lo[:, h % 2, k, :]),
                                       k == 0 and h % 2 == 0, k == TT - 1 and h % 2 == 1)
                    last.then_inc(head_done, 1)

            for s in range(HEADS * TT + 6):
                attention_step(s)
            pe.wait_ge(tap_done, CT * TAPS)
            pe.wait_ge(probT_lo_made, HEADS * TT)
            for t in range(TT):
                for ct in range(CT):
                    last = nc.tensor.transpose(ps[:, t, ct * P:(ct + 1) * P], acc[:, ct, t * P:(t + 1) * P], ident[:])
                last.then_inc(conv_turned, 1)
            pe.wait_ge(cat_lo_made, 4)
            for t in range(TT):
                pe.wait_ge(conv_normed, t + 1)
                for ct in range(CT):
                    last = nc.tensor.transpose(ps[:, 4 + ct, t * P:(t + 1) * P], conv_norm[:, t, ct * P:(ct + 1) * P],
                                               ident[:])
                    if t == TT - 1:
                        last.then_inc(conv_back, 1)
            pe.wait_ge(silu_made, CT)
            out_projection(C_OUT0, 4, (catT_hi, catT_lo), lambda row: pe.wait_ge(cat_lo_made, row + 1), 1)

            def swiglu(layer, c_ffn, c_down, stage):
                h0, f0 = NH * layer, (NH + 2) * layer
                pe.wait_ge(xT_lo_made, 8 * (2 * layer + 2))
                wait_split(pe, c_ffn + 1)
                with pe.Fori(0, NH // 2) as i:
                    feature_tiles(Chunk(c_ffn, i), 0, lambda m: pe.wait_ge(gate_read, f0 + 2 * i + m + 1))
                    feature_tiles(Chunk(c_ffn + 1, i), 2, lambda m: pe.wait_ge(up_read, f0 + 2 * i + m + 1))
                pe.wait_ge(up_read, f0 + NH + 2)
                out_projection(c_down, NH // 2, (hT_hi, hT_lo), lambda row: pe.wait_ge(h_lo_made, h0 + row + 1), stage)

            swiglu(0, C_FFN0, C_DOWN0, 2)

            pe.wait_ge(xT_lo_made, 8 * 3)
            wait_split(pe, C_RET + 1)
            with pe.Fori(0, RH) as h:
                for x in range(2):
                    feature_tiles(Chunk(C_RET + x, h, 6), 2 * x,
                                  lambda m, x=x: pe.wait_ge(g_read, 4 * h + 2 * x + m + 1))
                token_tiles([Chunk(C_RET + 2, h, 6), Chunk(C_RET + 3, h, 6)], 4, 4, N,
                            lambda t: pe.wait_ge(o_normed, 4 * h + t + 1))
                pe.wait_ge(rot_lo, 4 * h + 4)
                for kt in range(TT):
                    for half in range(2):
                        last = product(ps[:, kt, :], (rk_hi[:, half, kt * P:(kt + 1) * P], rk_lo[:, half, kt * P:(kt + 1) * P]),
                                       (rq_hi[:, half, :], rq_lo[:, half, :]), half == 0, half == 1)
                    last.then_inc(ret_scored, 1)
                pe.wait_ge(rv_lo_made, 4 * h + 4)
                for kt in range(TT):
                    pe.wait_ge(sT_lo_made, 4 * h + kt + 1)
                    for t in range(TT):
                        tok = slice(t * P, (t + 1) * P)
                        last = product(ps[:, 4 + t, :], (sT_hi[:, kt % 2, tok], sT_lo[:, kt % 2, tok]),
                                       (rv_hi[:, kt, :], rv_lo[:, kt, :]), kt == 0, kt == TT - 1)
                        if kt == TT - 1:
                            last.then_inc(o_made, 1)
                    if kt < TT - 1:
                        last.then_inc(sT_used, 1)
                token_tiles([Chunk(C_RET + 4, h, 6), Chunk(C_RET + 5, h, 6)], 0, 4, N, lambda t: None)

            def turn_y(q):
                if q == 0:
                    pe.wait_ge(y_made, 4 * RH)
                if q == 20:
                    pe.wait_ge(resid_read, TT)
                elif q >= 4:
                    pe.wait_ge(yT_lo_made, q - 3)
                for t in range(TT):
                    last = nc.tensor.transpose(ps[:, 4 + q % 4 if q < 20 else q % 4, t * P:(t + 1) * P],
                                               y_tok[:, t, (q % 16) * P:(q % 16 + 1) * P], ident[:])
                last.then_inc(y_turned, 1)

            def y_part(q, t):
                ch, k, tok = Chunk(C_OUT1 + q // 4), q % 4, slice(t * P, (t + 1) * P)
                hi, lo = weights(ch, 4)
                return product(ps[:, 4 * (q // 16) + t, :], (yT_hi[:, q % 8, tok], yT_lo[:, q % 8, tok]),
                               (hi[:, k, :], lo[:, k, :]), q % 16 == 0, q % 16 == 15)

            for q in range(4):
                turn_y(q)
            for q in range(24):
                if q % 4 == 0:
                    wait_split(pe, C_OUT1 + q // 4)
                pe.wait_ge(yT_lo_made, q + 1 if q != 16 else 20)
                for t in range(TT):
                    last = y_part(q, t)
                    if q == 15 and t < TT - 1:
                        last.then_inc(part_made, 1)
                last.then_inc(chunk_used if q % 4 == 3 else yT_used, 1)
                turn_y(q + 4)
            for q in range(28, 32):
                turn_y(q)
            pe.wait_ge(yT_lo_made, 32)
            wait_split(pe, C_FFN1 - 1)
            for t in range(TT):
                for q in range(24, 32):
                    last = y_part(q, t)
                    if q == 27 and t == TT - 1:
                        last.then_inc(chunk_used, 1)
                last.then_inc(chunk_used if t == TT - 1 else part_made, 1)
                if t == TT - 2:
                    turn_when_normed(3, 0)
            for t in range(1, TT):
                turn_when_normed(3, t)
            swiglu(1, C_FFN1, C_DOWN1, None)


def rope_tables():
    t = np.arange(SEQ)
    row, col = (t // GRID_W).astype(np.float32), (t % GRID_W).astype(np.float32)

    def angles(head_dim):
        axis = head_dim // 2
        freq = np.float32(THETA) ** (-np.arange(0, axis, 2, dtype=np.float32) / np.float32(axis))
        return np.concatenate([row[:, None] * freq, col[:, None] * freq], axis=-1).astype(np.float32)

    a, r = angles(HD), angles(RK)
    by_token = np.stack([np.cos(a), np.sin(a)], axis=1).reshape(TT, P, 2, HD // 2).transpose(1, 0, 2, 3)
    by_freq = np.stack([np.cos(r).T, np.sin(r).T], axis=1)
    return np.ascontiguousarray(by_token, np.float32), np.ascontiguousarray(by_freq, np.float32)


_PLAIN = ["x", "l0_w_in", "l0_q_norm_g", "l0_k_norm_g", "l0_w_out", "l0_ln_mix_g", "l0_ln_mix_b",
          "l0_ffn_w_gate", "l0_ffn_w_up", "l0_ffn_w_down", "l0_ln_ffn_g", "l0_ln_ffn_b",
          "l1_w_in", "l1_w_out", "l1_ln_mix_g", "l1_ln_mix_b", "l1_ffn_w_gate", "l1_ffn_w_up",
          "l1_ffn_w_down", "l1_ln_ffn_g", "l1_ln_ffn_b"]


def kernel(**inputs):
    import numpy as _np
    import concourse.bacc as _bacc
    from concourse import mybir as _mybir
    from concourse.bass_utils import run_bass_kernel_spmd as _run

    given = {name: _np.asarray(a) for name, a in inputs.items()}
    arrays = {name: given[name] for name in _PLAIN}
    by_channel = _np.concatenate([given["l0_dw_w"], given["l0_dw_b"][None], given["l0_conv_norm_g"][None],
                                  given["l0_conv_norm_b"][None]])
    arrays["conv_par"] = by_channel.reshape(TAPS + 3, CT, P).transpose(2, 1, 0)
    arrays["decay"] = _np.stack([given["l1_log_decay_fwd"], given["l1_log_decay_bwd"]])
    arrays["ret_gain"] = given["l1_ret_norm_g"].reshape(-1, P).T
    arrays["rope0"], arrays["rope1"] = rope_tables()

    nc = _bacc.Bacc("TRN2", target_bir_lowering=False, num_devices=1)
    ins, feed = {}, {}
    for name, a in arrays.items():
        feed[f"in_{name}"] = _np.ascontiguousarray(a)
        ins[name] = nc.dram_tensor(f"in_{name}", a.shape, _mybir.dt.from_np(a.dtype), kind="ExternalInput").ap()
    out = nc.dram_tensor("out_0", (1, SEQ, D), _mybir.dt.float32, kind="ExternalOutput").ap()
    build_encoder(nc, ins, out)
    r = _run(nc, [feed], core_ids=[0])
    return r.results[0]["out_0"]
```

```python
from contextlib import ExitStack

import numpy as np

import concourse.bass as bass
from concourse import mybir

ALU = mybir.AluOpType
ACT = mybir.ActivationFunctionType
AX = mybir.AxisListType
F32 = mybir.dt.float32
F32R = mybir.dt.float32r

P = 128
SEQ = 512
D = 1024
TT = SEQ // P
KD = D // P
N = 512
HIDDEN = 2816
NH = HIDDEN // P
CHUNK = 2048
ALPHA = 4.0 ** 0.25
LN_EPS, RMS_EPS = 1e-5, 1e-6
GRID_W, THETA = 64, 10000.0

HEADS, KV, HD = 8, 2, 64
QK = (HEADS + KV) * HD
CT = 4
TAPS = 31
PAD = TAPS // 2
RH, RK, RV = 4, 256, 512
SPAN = 2 * SEQ - P

C_GLU = (0, 5)
C_Q = 2
C_KV = 4
C_OUT0 = 7
C_FFN0 = 11
C_DOWN0 = C_FFN0 + NH
C_RET = C_DOWN0 + NH // 2
C_OUT1 = C_RET + 6 * RH
C_FFN1 = C_OUT1 + 8
C_DOWN1 = C_FFN1 + NH
N_CHUNKS = C_DOWN1 + NH // 2

SEAMS = (C_FFN0, C_RET, C_FFN1)

SIDE_A, SIDE_B = (0, 1, 4, 5), (2, 3, 6, 7)
SCORE_BANKS, TURN_BANKS, HEAD_BANKS = (2, 3, 6), (0, 1, 4), (5, 7)
QK_BANKS = (4, 5, 6, 7, 0, 1)

FREE = 4


def build_encoder(nc, ins, out):
    ctx = ExitStack()
    with ctx:
        top = [-(-nc.sbuf_base // 32) * 32]

        def place(name, shape, dt, at=None):
            size = 4 * int(np.prod(shape[1:]))
            offset = top[0] if at is None else at
            if at is None:
                top[0] += -(-size // 32) * 32
            return nc.alloc_sbuf_tensor_at(name, shape, dt, offset=offset)

        x_tok = place("x_tok", [P, TT, D], F32)
        xt_at = top[0]
        xT_hi = place("xT_hi", [P, KD, SEQ], F32R)
        xT_lo = place("xT_lo", [P, KD, SEQ], F32R)
        raw = [place(f"raw{s}", [P, CHUNK], F32) for s in range(2)]
        w_hi = [place(f"w_hi{s}", [P, CHUNK], F32R) for s in range(2)]
        w_lo = [place(f"w_lo{s}", [P, CHUNK], F32R) for s in range(2)]
        gb_at = top[0]
        ln_gb = place("ln_gb", [P, 2, D], F32)
        tmp = [place(f"tmp{i}", [P, N], F32) for i in range(4)]
        ident = place("ident", [P, P], F32)
        conv_par = place("conv_par", [P, CT, TAPS + 3], F32)
        qk_gain = place("qk_gain", [P, HEADS + KV, HD], F32)
        rope0 = place("rope0", [P, TT, 2, HD // 2], F32)
        decay = place("decay", [P, 2, RH], F32)
        ret_gain = place("ret_gain", [P, RH * RV // P], F32)
        minus_half = place("minus_half", [P, 16], F32)
        stats = place("stats", [P, TT, 2, 6], F32)
        moments = place("moments", [P, TT, 2], F32)
        var_eps = place("var_eps", [P, TT], F32)
        rstd = place("rstd", [P, TT], F32)
        qk_ms = place("qk_ms", [P, TT, HEADS + KV], F32)
        qk_rstd = place("qk_rstd", [P, TT, HEADS + KV], F32)
        row_max = place("row_max", [P, HEADS * TT], F32)
        neg_max = place("neg_max", [P, HEADS * TT], F32)
        row_sum = place("row_sum", [P, HEADS * TT], F32)
        row_inv = place("row_inv", [P, HEADS * TT], F32)
        work = top[0]
        hT_hi = place("hT_hi", [P, NH, SEQ], F32R, work)
        hT_lo = place("hT_lo", [P, NH, SEQ], F32R, work + NH * SEQ * 4)
        KB = 1024
        catT_hi = place("catT_hi", [P, KD, SEQ], F32R, work)
        catT_lo = place("catT_lo", [P, KD, SEQ], F32R, work + 16 * KB)
        qk_tok = place("qk_tok", [P, TT, QK], F32, work)
        roped = place("roped", [P, TT, (HEADS + 2 * KV) * HD], F32, work + 12 * KB)
        qT_hi = place("qT_hi", [P, 4, SEQ], F32R, work + 32 * KB)
        qT_lo = place("qT_lo", [P, 4, SEQ], F32R, work + 40 * KB)
        kT_hi = place("kT_hi", [P, KV, 2, SEQ], F32R, work + 48 * KB)
        kT_lo = place("kT_lo", [P, KV, 2, SEQ], F32R, work + 56 * KB)
        v_hi = place("v_hi", [P, TT, KV, 2, P], F32R, work + 64 * KB)
        v_lo = place("v_lo", [P, TT, KV, 2, P], F32R, work + 72 * KB)
        zpad = place("zpad", [P, CT, SEQ + 2 * PAD], F32, work + 80 * KB)
        tap_part = place("tap_part", [P, 4, SEQ], F32, work + 24 * KB)
        conv_norm = place("conv_norm", [P, TT, CT * P], F32, work + 80 * KB)
        acc = place("acc", [P, CT, SEQ], F32, gb_at)
        probT_hi = place("probT_hi", [P, 2, TT, SEQ], F32R, xt_at)
        probT_lo = place("probT_lo", [P, 2, TT, SEQ], F32R, xt_at + 16 * KB)
        y_tok = place("y_tok", [P, TT, RH * RV], F32, work)
        rq_hi = place("rq_hi", [P, 2, SEQ], F32R, work + 32 * KB)
        rq_lo = place("rq_lo", [P, 2, SEQ], F32R, work + 36 * KB)
        rk_hi = place("rk_hi", [P, 2, SEQ], F32R, work + 40 * KB)
        rk_lo = place("rk_lo", [P, 2, SEQ], F32R, work + 44 * KB)
        rv_hi = place("rv_hi", [P, TT, RV], F32R, work + 48 * KB)
        rv_lo = place("rv_lo", [P, TT, RV], F32R, work + 56 * KB)
        sT_hi = place("sT_hi", [P, 2, SEQ], F32R, work + 64 * KB)
        sT_lo = place("sT_lo", [P, 2, SEQ], F32R, work + 68 * KB)
        ahead = place("ahead", [P, SPAN], F32, work + 72 * KB)
        behind = place("behind", [P, SPAN], F32, work + 72 * KB + 4 * SPAN)
        mask = place("mask", [P, SPAN], F32, work + 72 * KB + 8 * SPAN)
        mask_b = place("mask_b", [P, SPAN], F32, work + 72 * KB + 12 * SPAN)
        yT_hi = place("yT_hi", [P, 8, SEQ], F32R, work + 32 * KB)
        yT_lo = place("yT_lo", [P, 8, SEQ], F32R, work + 48 * KB)
        rope1 = place("rope1", [P, 2, SEQ], F32, gb_at)

        ps = ctx.enter_context(nc.psum_tensor("ps", [P, 8, N], F32))

        def f32(ap):
            return ap.bitcast(F32)

        def sem(name):
            return ctx.enter_context(nc.semaphore(name))

        raw_landed = [sem(f"raw_landed{s}") for s in range(2)]
        x_landed = [sem(f"x_landed{t}") for t in range(TT)]
        par_landed = sem("par_landed")
        gb_landed = sem("gb_landed")
        rope1_landed = sem("rope1_landed")
        out_landed = sem("out_landed")
        hi_made = sem("hi_made")
        lo_made = sem("lo_made")
        seam_lo_made = sem("seam_lo_made")
        chunk_used = sem("chunk_used")
        part_made = sem("part_made")
        consts_made = sem("consts_made")
        dve_own = sem("dve_own")
        stats_seen = sem("stats_seen")
        turned = sem("turned")
        xT_hi_made = sem("xT_hi_made")
        xT_lo_made = sem("xT_lo_made")
        var_made = sem("var_made")
        rstd_made = sem("rstd_made")
        x_normed = sem("x_normed")
        resid_read = sem("resid_read")
        gate_read = sem("gate_read")
        up_read = sem("up_read")
        h_hi_made = sem("h_hi_made")
        h_lo_made = sem("h_lo_made")
        sig_made = sem("sig_made")
        z_made = sem("z_made")
        tap_done = sem("tap_done")
        part_tapped = sem("part_tapped")
        part_added = sem("part_added")
        q_copied = sem("q_copied")
        k_copied = sem("k_copied")
        vh_made = sem("vh_made")
        v_split = sem("v_split")
        sq_made = sem("sq_made")
        ms_made = sem("ms_made")
        qk_scaled = sem("qk_scaled")
        pool_own = sem("pool_own")
        rope_made = sem("rope_made")
        qk_turned = sem("qk_turned")
        qkT_hi_made = sem("qkT_hi_made")
        qkT_lo_made = sem("qkT_lo_made")
        scores_made = sem("scores_made")
        max_made = sem("max_made")
        exp_made = sem("exp_made")
        inv_made = sem("inv_made")
        prob_made = sem("prob_made")
        prob_turned = sem("prob_turned")
        probT_hi_made = sem("probT_hi_made")
        probT_lo_made = sem("probT_lo_made")
        head_done = sem("head_done")
        cat_hi_made = sem("cat_hi_made")
        cat_lo_made = sem("cat_lo_made")
        conv_turned = sem("conv_turned")
        conv_var = sem("conv_var")
        conv_rstd = sem("conv_rstd")
        conv_normed = sem("conv_normed")
        conv_back = sem("conv_back")
        silu_made = sem("silu_made")
        rot_made = sem("rot_made")
        rot_hi = sem("rot_hi")
        rot_lo = sem("rot_lo")
        rv_hi_made = sem("rv_hi_made")
        rv_lo_made = sem("rv_lo_made")
        exponent_made = sem("exponent_made")
        mask_made = sem("mask_made")
        ret_scored = sem("ret_scored")
        ret_masked = sem("ret_masked")
        sT_hi_made = sem("sT_hi_made")
        sT_lo_made = sem("sT_lo_made")
        sT_used = sem("sT_used")
        o_made = sem("o_made")
        o_var = sem("o_var")
        o_rstd = sem("o_rstd")
        o_normed = sem("o_normed")
        g_read = sem("g_read")
        y_made = sem("y_made")
        y_turned = sem("y_turned")
        yT_hi_made = sem("yT_hi_made")
        yT_lo_made = sem("yT_lo_made")
        yT_used = sem("yT_used")

        PM_GLU, PM_Q, PM_KV, PM_OUT0, PM_FFN0 = (0, 8), 2, 5, 10, 13
        PM_DOWN0 = PM_FFN0 + NH
        PM_RET = PM_DOWN0 + 3
        PM_OUT1A = PM_RET + RH * (2 + 3 + 3)
        PM_OUT1B = PM_OUT1A + 3
        PM_FFN1 = PM_OUT1B + 3
        PM_DOWN1 = PM_FFN1 + NH

        def by_row_tile(w):
            return w.rearrange("(k p) n -> p k n", p=P)

        W0, WO0 = by_row_tile(ins["l0_w_in"]), by_row_tile(ins["l0_w_out"])
        W1, WO1 = by_row_tile(ins["l1_w_in"]), by_row_tile(ins["l1_w_out"])
        gate_w = [by_row_tile(ins[f"l{i}_ffn_w_gate"]) for i in range(2)]
        up_w = [by_row_tile(ins[f"l{i}_ffn_w_up"]) for i in range(2)]
        down_w = [by_row_tile(ins[f"l{i}_ffn_w_down"]) for i in range(2)]
        A0 = HEADS * HD + 2 * KV * HD

        class Chunk:

            def __init__(self, first, turn=0, stride=2):
                self.s = first % 2
                self.first = first
                self.c = first + stride * turn
                self.nth = first // 2 + stride // 2 * turn
                self.lo = self.c + 1 - 2 * sum(first >= seam for seam in SEAMS)

        def wait_split(eng, c):
            for n, seam in enumerate(SEAMS):
                if seam <= c < seam + 2:
                    eng.wait_ge(seam_lo_made, 2 * n + c - seam + 1)
                    return
            eng.wait_ge(lo_made, Chunk(c).lo)

        def load(eng, ch, src, looped=False):
            if looped:
                eng.wait_ge(lo_made, ch.lo - 2)
            elif ch.first >= 2:
                wait_split(eng, ch.first - 2)
            k, n = src.shape[1], src.shape[2]
            eng.dma_start(raw[ch.s][:].rearrange("p (k n) -> p k n", k=k), src)\
               .then_inc(raw_landed[ch.s], 16)

        def make_hi(act, ch):
            act.wait_ge(raw_landed[ch.s], 16 * ch.nth + 16)
            if ch.first >= 2:
                act.wait_ge(chunk_used, ch.c - 1)
            act.activation(w_hi[ch.s][:], raw[ch.s][:], ACT.Copy).then_inc(hi_made, 1)

        def make_lo(eng, ch, made=lo_made):
            eng.wait_ge(hi_made, ch.c + 1)
            eng.tensor_tensor(w_lo[ch.s][:], raw[ch.s][:], f32(w_hi[ch.s][:]), ALU.subtract)\
               .then_inc(made, 1)

        def y_bank(q):
            return (6, 7, 4, 5)[q % 4] if q < 20 else q % 4

        block = ctx.enter_context(nc.Block())

        @block.sync
        def _(sp):
            def load_glu(p, part):
                col = A0 + 512 * part + 256 * p
                load(sp, Chunk(C_GLU[p] + part), W0[:, :, col:col + 256])

            for t in range(TT):
                sp.dma_start(x_tok[:, t, :], ins["x"][0, t * P:(t + 1) * P, :]).then_inc(x_landed[t], 16)
                if t % 2:
                    load_glu(0, t // 2)
            for j in range(2):
                load(sp, Chunk(C_Q + j), W0[:, 4 * j:4 * j + 4, 0:512])
            load(sp, Chunk(C_KV), W0[:, :, 512:768])
            for part in range(2):
                load_glu(1, part)
            for j in range(4):
                load(sp, Chunk(C_OUT0 + j), WO0[:, 2 * j:2 * j + 2, :])

            def norm_params(d, name):
                sp.dma_start(ln_gb[:, 0, :], ins[f"{name}_g"].partition_broadcast(P)).then_inc(gb_landed, 16)
                sp.dma_start(ln_gb[:, 1, :], ins[f"{name}_b"].partition_broadcast(P)).then_inc(gb_landed, 16)

            def ffn_loads(layer, c_ffn, c_down):
                for i in range(2):
                    for k, w in enumerate((gate_w[layer], up_w[layer])):
                        load(sp, Chunk(c_ffn + 2 * i + k), w[:, :, i * 256:i * 256 + 256])
                with sp.Fori(2, NH // 2) as i:
                    load(sp, Chunk(c_ffn, i), gate_w[layer][:, :, bass.ds(i * 256, 256)], looped=True)
                    load(sp, Chunk(c_ffn + 1, i), up_w[layer][:, :, bass.ds(i * 256, 256)], looped=True)
                for j in range(NH // 2):
                    if j == 2:
                        sp.wait_ge(x_normed, 4 * (2 * layer + 1))
                        norm_params(2 * layer + 1, f"l{layer}_ln_ffn")
                    load(sp, Chunk(c_down + j), down_w[layer][:, 2 * j:2 * j + 2, :])

            sp.wait_ge(conv_turned, TT)
            norm_params(0, "l0_ln_mix")
            ffn_loads(0, C_FFN0, C_DOWN0)
            for c in range(2):
                load(sp, Chunk(C_RET + c), W1[:, :, D * c:D * c + 256])
            sp.wait_ge(x_normed, 4 * 2)
            sp.dma_start(rope1[:], ins["rope1"]).then_inc(rope1_landed, 16)
            for h in range(RH):
                if h:
                    for c in range(2):
                        load(sp, Chunk(C_RET + c + 6 * h), W1[:, :, D * c + RK * h:D * c + RK * h + 256])
                for c in range(4):
                    col = 2 * D + RH * RV * (c // 2) + RV * h
                    load(sp, Chunk(C_RET + 2 + c + 6 * h), W1[:, 4 * (c % 2):4 * (c % 2) + 4, col:col + RV])
            for j in range(8):
                if j == 2:
                    sp.wait_ge(rot_made, 4 * RH)
                    norm_params(2, "l1_ln_mix")
                kt, col = 4 * (j % 4), N * (j // 4)
                load(sp, Chunk(C_OUT1 + j), WO1[:, kt:kt + 4, col:col + N])
            ffn_loads(1, C_FFN1, C_DOWN1)
            for t in range(TT):
                sp.wait_ge(x_normed, 4 * 3 + t + 1)
                sp.dma_start(out[0, t * P:(t + 1) * P, :], x_tok[:, t, :]).then_inc(out_landed, 16)
            sp.wait_ge(out_landed, 16 * TT)

        @block.gpsimd
        def _(pool):
            own = [0]

            def mine(instruction):
                own[0] += 1
                instruction.then_inc(pool_own, 1)
                pool.wait_ge(pool_own, own[0])

            mine(nc.gpsimd.memset(ident[:], 0.0))
            mine(nc.gpsimd.affine_select(out=ident[:], in_=ident[:], compare_op=ALU.not_equal, fill=1.0,
                                         base=0, pattern=[[-1, P]], channel_multiplier=1))
            nc.gpsimd.memset(minus_half[:], -0.5).then_inc(consts_made, 1)
            nc.gpsimd.memset(zpad[:], 0.0).then_inc(consts_made, 1)
            for z in (kT_hi, kT_lo, v_hi, v_lo):
                nc.gpsimd.memset(f32(z[:]), 0.0).then_inc(consts_made, 1)

            def lo_at_seam(c):
                for k in range(2):
                    make_lo(pool, Chunk(c + k), seam_lo_made)

            added = [0]

            def add_taps(count):
                for n in range(added[0], min(added[0] + count, 2 * (TAPS - 1))):
                    ct = 2 * (n // (TAPS - 1)) + 1
                    pool.wait_ge(part_tapped, n + ct // 2 + 2)
                    if n:
                        pool.wait_ge(part_added, n)
                    nc.gpsimd.tensor_tensor(acc[:, ct, :], acc[:, ct, :], tap_part[:, n % 4, :], ALU.add)\
                        .then_inc(part_added, 1)
                    added[0] += 1

            add_taps(22)
            pool.wait_ge(par_landed, 16 * 6)
            for t in range(TT):
                pool.wait_ge(ms_made, t + 1)
                mine(nc.gpsimd.tensor_tensor(qk_rstd[:, t, :], qk_ms[:, t, :], minus_half[:, 0:HEADS + KV], ALU.pow))
                view = qk_tok[:, t, :].rearrange("p (h d) -> p h d", d=HD)
                mine(nc.gpsimd.tensor_tensor(view, view, qk_rstd[:, t, :].unsqueeze(2).broadcast_to([P, HEADS + KV, HD]),
                                             ALU.mult))
                nc.gpsimd.tensor_tensor(view, view, qk_gain[:], ALU.mult).then_inc(qk_scaled, 1)
            add_taps(8)
            for s in range(HEADS * TT):
                pool.wait_ge(inv_made, s + 1)
                prob = tmp[s % 3]
                nc.gpsimd.tensor_tensor(prob[:], prob[:], row_inv[:, s:s + 1].broadcast_to([P, SEQ]), ALU.mult)\
                    .then_inc(prob_made, 1)
                add_taps(1)
            for t in range(TT):
                pool.wait_ge(conv_var, t + 1)
                nc.gpsimd.tensor_tensor(rstd[:, t:t + 1], var_eps[:, t:t + 1], minus_half[:, 0:1], ALU.pow)\
                    .then_inc(conv_rstd, 1)

            def norm_rstd(d):
                for t in range(TT):
                    pool.wait_ge(var_made, 4 * d + t + 1)
                    nc.gpsimd.tensor_tensor(rstd[:, t:t + 1], var_eps[:, t:t + 1], minus_half[:, 0:1], ALU.pow)\
                        .then_inc(rstd_made, 1)

            norm_rstd(0)
            lo_at_seam(C_FFN0)
            norm_rstd(1)
            lo_at_seam(C_RET)
            pool.wait_ge(x_normed, 4 * 2)
            mine(nc.gpsimd.iota(mask[:], pattern=[[1, SPAN]], base=-(SEQ - P), channel_multiplier=-1,
                                allow_small_or_imprecise_dtypes=True))
            mine(nc.gpsimd.tensor_scalar(ahead[:], mask[:], 0.0, None, ALU.max))
            mine(nc.gpsimd.tensor_tensor(behind[:], ahead[:], mask[:], ALU.subtract))
            base = own[0]
            with pool.Fori(0, RH) as h:
                pool.wait_ge(ret_masked, 4 * h + FREE)
                nc.gpsimd.tensor_tensor(mask[:], ahead[:], decay[:, 0, bass.ds(h, 1)].broadcast_to([P, SPAN]), ALU.mult)\
                    .then_inc(pool_own, 1)
                nc.gpsimd.tensor_tensor(mask_b[:], behind[:], decay[:, 1, bass.ds(h, 1)].broadcast_to([P, SPAN]), ALU.mult)\
                    .then_inc(pool_own, 1)
                pool.wait_ge(pool_own, base + 2 * h + 2)
                nc.gpsimd.tensor_tensor(mask[:], mask[:], mask_b[:], ALU.add).then_inc(exponent_made, 1)
                for t in range(TT):
                    pool.wait_ge(o_var, 4 * h + t + 1)
                    nc.gpsimd.tensor_tensor(rstd[:, t:t + 1], var_eps[:, t:t + 1], minus_half[:, 0:1], ALU.pow)\
                        .then_inc(o_rstd, 1)
            norm_rstd(2)
            lo_at_seam(C_FFN1)
            norm_rstd(3)

        @block.scalar
        def _(act):
            for dst, src in ((conv_par[:], ins["conv_par"]),
                             (qk_gain[:, 0:HEADS, :], ins["l0_q_norm_g"].partition_broadcast(P).unsqueeze(1)
                              .broadcast_to([P, HEADS, HD])),
                             (qk_gain[:, HEADS:HEADS + KV, :], ins["l0_k_norm_g"].partition_broadcast(P).unsqueeze(1)
                              .broadcast_to([P, KV, HD])),
                             (rope0[:], ins["rope0"]),
                             (decay[:], ins["decay"].partition_broadcast(P)),
                             (ret_gain[:], ins["ret_gain"])):
                act.dma_start(dst, src).then_inc(par_landed, 16)

            def xT_tile_hi(stage, t):
                for half in range(2):
                    n = 8 * stage + 2 * t + half
                    act.wait_ge(turned, n + 1)
                    nc.scalar.activation(xT_hi[:, 4 * half:4 * half + 4, t * P:(t + 1) * P],
                                         ps[:, t + 4 * half, :].rearrange("p (k c) -> p k c", c=P), ACT.Copy)\
                        .then_inc(xT_hi_made, 1)

            act.preload_act_table(ACT.Sigmoid)
            for t in range(TT):
                xT_tile_hi(0, t)
                if t % 2:
                    make_hi(act, Chunk(t // 2))
            tapped = [0]

            def tap_products(count):
                for n in range(tapped[0], min(tapped[0] + count, 2 * TAPS)):
                    ct, k = 2 * (n // TAPS) + 1, n % TAPS
                    tap = conv_par[:, ct, k:k + 1]
                    if k == 0:
                        act.wait_ge(par_landed, 16 * 6)
                        act.wait_ge(z_made, ct + 1)
                        nc.scalar.activation(acc[:, ct, :], zpad[:, ct, k:k + SEQ], ACT.Identity, scale=tap,
                                             bias=conv_par[:, ct, TAPS:TAPS + 1]).then_inc(part_tapped, 1)
                    else:
                        m = n - n // TAPS - 1
                        if m >= 4:
                            act.wait_ge(part_added, m - 3)
                        nc.scalar.activation(tap_part[:, m % 4, :], zpad[:, ct, k:k + SEQ], ACT.Copy, scale=tap)\
                            .then_inc(part_tapped, 1)
                    tapped[0] += 1

            def glu_sigmoids(p):
                for m in range(2):
                    ct = 2 * p + m
                    make_hi(act, Chunk(C_GLU[p] + 2 + m))
                    if m == 0:
                        act.wait_ge(part_made, PM_GLU[p] + 2)
                    else:
                        act.wait_ge(chunk_used, C_GLU[p] + 2)
                    if ct:
                        act.wait_ge(z_made, ct)
                    nc.scalar.activation(tmp[3][:], ps[:, (SIDE_B if p else SIDE_A)[2 + m], :], ACT.Sigmoid)\
                        .then_inc(sig_made, 1)

            glu_sigmoids(0)
            tap_products(8)
            make_hi(act, Chunk(C_KV))
            tap_products(8)
            make_hi(act, Chunk(C_GLU[1]))
            for t in range(TT):
                act.wait_ge(part_made, PM_Q + t + 1) if t < TT - 1 else act.wait_ge(chunk_used, C_KV)
                nc.scalar.activation(qk_tok[:, t, 0:HEADS * HD], ps[:, SIDE_B[t], :], ACT.Copy).then_inc(q_copied, 1)
            tap_products(7)
            make_hi(act, Chunk(C_GLU[1] + 1))
            for t in range(TT):
                act.wait_ge(part_made, PM_KV + t + 1) if t < TT - 1 else act.wait_ge(chunk_used, C_KV + 1)
                nc.scalar.activation(qk_tok[:, t, HEADS * HD:QK], ps[:, SIDE_A[t], 0:KV * HD], ACT.Copy)\
                    .then_inc(k_copied, 1)
                act.wait_ge(q_copied, t + 1)
                act.wait_ge(k_copied, t + 1)
                nc.scalar.activation(roped[:, t, 0:QK], qk_tok[:, t, :], ACT.Square).then_inc(sq_made, 1)
                act.wait_ge(consts_made, 6)
                for side in range(2):
                    nc.scalar.activation(v_hi[:, t, :, side, HD * side:HD * side + HD],
                                         ps[:, SIDE_A[t], KV * HD:2 * KV * HD].rearrange("p (g d) -> p g d", d=HD),
                                         ACT.Copy).then_inc(vh_made, 1)
            tap_products(8)
            glu_sigmoids(1)
            act.preload_act_table(ACT.Exp)
            for j in range(4):
                act.wait_ge(qk_turned, j + 1)
                nc.scalar.activation(qT_hi[:, j, :], ps[:, QK_BANKS[j], :], ACT.Copy).then_inc(qkT_hi_made, 1)
            for g in range(KV):
                act.wait_ge(qk_turned, 4 + g + 1)
                for side in range(2):
                    rows = slice(HD * side, HD * side + HD)
                    nc.scalar.activation(kT_hi[rows, g, side, :], ps[rows, QK_BANKS[4 + g], :], ACT.Copy)\
                        .then_inc(qkT_hi_made, 1)

            def attention_step(s):
                if s < HEADS * TT:
                    act.wait_ge(max_made, s + 1)
                    if s >= 3:
                        act.wait_ge(prob_turned, s - 2)
                    nc.scalar.activation(tmp[s % 3][:], ps[:, SCORE_BANKS[s % 3], :], ACT.Exp, bias=neg_max[:, s:s + 1],
                                         scale=HD ** -0.5, accum_out=row_sum[:, s:s + 1]).then_inc(exp_made, 1)
                u = s - 2
                if 0 <= u < HEADS * TT:
                    h, t = u // TT, u % TT
                    act.wait_ge(prob_turned, u + 1)
                    if h >= 2 and t == 0:
                        act.wait_ge(head_done, h - 1)
                    nc.scalar.activation(probT_hi[:, h % 2, :, t * P:(t + 1) * P],
                                         ps[:, TURN_BANKS[u % 3], :].rearrange("p (k c) -> p k c", c=P), ACT.Copy)\
                        .then_inc(probT_hi_made, 1)
                tap_products(1)
                if s % 8 == 5 and s >= 13:
                    j = (s - 13) // 8
                    act.wait_ge(head_done, 2 * j + 2)
                    nc.scalar.activation(catT_hi[:, j, :], ps[:, HEAD_BANKS[j % 2], :], ACT.Copy).then_inc(cat_hi_made, 1)

            for s in range(HEADS * TT + 6):
                attention_step(s)
            act.preload_act_table(ACT.Silu)
            for ct in range(CT):
                act.wait_ge(conv_back, ct + 1)
                nc.scalar.activation(tmp[ct][:], ps[:, 4 + ct, :], ACT.Silu, bias=conv_par[:, ct, TAPS + 2:TAPS + 3],
                                     scale=conv_par[:, ct, TAPS + 1:TAPS + 2]).then_inc(silu_made, 1)
                act.wait_ge(silu_made, ct + 1)
                nc.scalar.activation(catT_hi[:, 4 + ct, :], tmp[ct][:], ACT.Copy).then_inc(cat_hi_made, 1)

            def seam(stage, c):
                for t in range(TT):
                    xT_tile_hi(stage, t)
                    if t == 1:
                        make_hi(act, Chunk(c))
                    if t == 2:
                        make_hi(act, Chunk(c + 1))

            def swiglu(layer, c_ffn, c_down, pm):
                g0, f0 = NH * layer, (NH + 2) * layer
                act.sem_inc(gate_read, 2)
                with act.Fori(0, NH // 2) as i:
                    for m in range(2):
                        if m == 0:
                            act.wait_ge(part_made, pm + 2 * i + 1)
                        else:
                            make_hi(act, Chunk(c_ffn + 2, i))
                            act.wait_ge(chunk_used, c_ffn + 2 * i + 1)
                        act.wait_ge(up_read, f0 + 2 * i + m + 1)
                        nc.scalar.activation(tmp[m][:], ps[:, m, :], ACT.Silu).then_inc(gate_read, 1)
                    for m in range(2):
                        act.wait_ge(up_read, f0 + 2 * i + m + 3)
                        nc.scalar.activation(hT_hi[:, bass.ds(2 * i + m, 1), :], tmp[2 + m][:].unsqueeze(1), ACT.Copy)\
                            .then_inc(h_hi_made, 1)
                    make_hi(act, Chunk(c_ffn + 3, i))
                for j in range(NH // 2 - 2):
                    make_hi(act, Chunk(c_down + j + 2))

            for j in range(2):
                make_hi(act, Chunk(C_OUT0 + 2 + j))
            seam(1, C_FFN0)
            swiglu(0, C_FFN0, C_DOWN0, PM_FFN0)
            seam(2, C_RET)
            act.sem_inc(g_read, FREE)
            with act.Fori(0, RH) as h:
                make_hi(act, Chunk(C_RET + 2, h, 6))
                for x, dst in ((0, rq_hi), (1, rk_hi)):
                    for half in range(2):
                        act.wait_ge(rot_made, 4 * h + 2 * x + half + 1)
                        nc.scalar.activation(dst[:, half, :], tmp[2 + half][:], ACT.Copy).then_inc(rot_hi, 1)
                    if x == 0:
                        make_hi(act, Chunk(C_RET + 3, h, 6))
                act.wait_ge(exponent_made, h + 1)
                nc.scalar.activation(mask[:], mask[:], ACT.Exp).then_inc(mask_made, 1)
                make_hi(act, Chunk(C_RET + 4, h, 6))
                for t in range(TT):
                    if t < TT - 1:
                        act.wait_ge(part_made, PM_RET + 8 * h + 2 + t + 1)
                    else:
                        act.wait_ge(chunk_used, C_RET + 6 * h + 4)
                    nc.scalar.activation(rv_hi[:, t, :], ps[:, SIDE_B[t], :], ACT.Copy).then_inc(rv_hi_made, 1)
                make_hi(act, Chunk(C_RET + 5, h, 6))
                for kt in range(TT):
                    act.wait_ge(ret_masked, 4 * h + kt + 1 + FREE)
                    if kt >= 2:
                        act.wait_ge(sT_used, 3 * h + kt - 1)
                    nc.scalar.activation(sT_hi[:, kt % 2, :], tmp[kt % 2][:], ACT.Copy).then_inc(sT_hi_made, 1)
                make_hi(act, Chunk(C_RET + 6, h, 6))
                for t in range(TT):
                    if t < TT - 1:
                        act.wait_ge(part_made, PM_RET + 8 * h + 5 + t + 1)
                    else:
                        act.wait_ge(chunk_used, C_RET + 6 * h + 6)
                    if t >= 2:
                        act.wait_ge(y_made, 4 * h + t - 1)
                    else:
                        act.wait_ge(rot_lo, 4 * h + 4)
                    nc.scalar.activation(tmp[2 + t % 2][:], ps[:, SIDE_A[t], :], ACT.Silu).then_inc(g_read, 1)
                make_hi(act, Chunk(C_RET + 7, h, 6))

            for q in range(32):
                kt = q % 16
                act.wait_ge(y_turned, q + 1)
                if q >= 8:
                    if q % 4 == 3:
                        act.wait_ge(chunk_used, C_OUT1 + (q - 8) // 4 + 1)
                    else:
                        act.wait_ge(yT_used, q - 7 - (q - 8) // 4)
                nc.scalar.activation(yT_hi[:, q % 8, :], ps[:, y_bank(q), :], ACT.Copy,
                                     scale=ret_gain[:, kt:kt + 1]).then_inc(yT_hi_made, 1)
                if q % 4 == 3 and 7 <= q < 28:
                    make_hi(act, Chunk(C_OUT1 + (q - 7) // 4 + 2))
            seam(3, C_FFN1)
            swiglu(1, C_FFN1, C_DOWN1, PM_FFN1)

        @block.vector
        def _(dve):
            class Own:
                n, per_turn, turn = 0, 0, 0

                def value(self):
                    return self.n + self.per_turn * self.turn if self.per_turn else self.n

            own = Own()

            def mine(instruction, wait=True):
                instruction.then_inc(dve_own, 1)
                own.n += 1
                if wait:
                    dve.wait_ge(dve_own, own.value())

            def xT_tile_lo(stage, t):
                for half in range(2):
                    n = 8 * stage + 2 * t + half
                    dve.wait_ge(xT_hi_made, n + 1)
                    spot = (slice(None), slice(4 * half, 4 * half + 4), slice(t * P, (t + 1) * P))
                    nc.vector.tensor_tensor(xT_lo[spot], ps[:, t + 4 * half, :].rearrange("p (k c) -> p k c", c=P),
                                            f32(xT_hi[spot]), ALU.subtract).then_inc(xT_lo_made, 1)

            taps = [(ct, k) for ct in (0, 2) for k in range(TAPS)]
            tapped = [0]

            def conv(count):
                for ct, k in taps[tapped[0]:tapped[0] + count]:
                    if k == 0:
                        dve.wait_ge(par_landed, 16 * 6)
                        dve.wait_ge(z_made, ct + 1)
                        nc.vector.tensor_scalar(acc[:, ct, :], zpad[:, ct, k:k + SEQ], conv_par[:, ct, k:k + 1],
                                                conv_par[:, ct, TAPS:TAPS + 1], ALU.mult, ALU.add).then_inc(tap_done, 1)
                    else:
                        dve.wait_ge(tap_done, tapped[0])
                        nc.vector.scalar_tensor_tensor(acc[:, ct, :], zpad[:, ct, k:k + SEQ], conv_par[:, ct, k:k + 1],
                                                       acc[:, ct, :], ALU.mult, ALU.add).then_inc(tap_done, 1)
                    tapped[0] += 1

            for t in range(TT):
                xT_tile_lo(0, t)
                if t % 2:
                    make_lo(dve, Chunk(t // 2))

            def glu_products(p):
                for m in range(2):
                    ct = 2 * p + m
                    make_lo(dve, Chunk(C_GLU[p] + 2 + m))
                    dve.wait_ge(sig_made, ct + 1)
                    nc.vector.tensor_tensor(zpad[:, ct, PAD:PAD + SEQ], tmp[3][:], ps[:, (SIDE_B if p else SIDE_A)[m], :],
                                            ALU.mult).then_inc(z_made, 1)

            dve.wait_ge(consts_made, 2)
            glu_products(0)
            conv(13)
            make_lo(dve, Chunk(C_KV))
            conv(13)
            make_lo(dve, Chunk(C_GLU[1]))
            conv(5)
            make_lo(dve, Chunk(C_GLU[1] + 1))

            def qk_mean_square(t):
                dve.wait_ge(sq_made, t + 1)
                mine(nc.vector.tensor_reduce(qk_ms[:, t, :], roped[:, t, 0:QK].rearrange("p (h d) -> p h d", d=HD),
                                             AX.X, ALU.add))
                nc.vector.tensor_scalar(qk_ms[:, t, :], qk_ms[:, t, :], 1.0 / HD, RMS_EPS, ALU.mult, ALU.add)\
                    .then_inc(ms_made, 1)

            def v_tile_lo(t):
                dve.wait_ge(vh_made, 2 * t + 2)
                for side in range(2):
                    cols = slice(HD * side, HD * side + HD)
                    nc.vector.tensor_tensor(v_lo[:, t, :, side, cols],
                                            ps[:, SIDE_A[t], KV * HD:2 * KV * HD].rearrange("p (g d) -> p g d", d=HD),
                                            f32(v_hi[:, t, :, side, cols]), ALU.subtract).then_inc(v_split, 1)

            def rope_tile(t):
                dve.wait_ge(qk_scaled, t + 1)
                x = qk_tok[:, t, :].rearrange("p (h s d) -> p h s d", s=2, d=HD // 2)
                cos, sin = (rope0[:, t, i, :].unsqueeze(1).broadcast_to([P, HEADS + KV, HD // 2]) for i in range(2))
                a = tmp[0][:, 0:QK // 2].rearrange("p (h d) -> p h d", d=HD // 2)
                b = tmp[1][:, 0:QK // 2].rearrange("p (h d) -> p h d", d=HD // 2)
                q_out = roped[:, t, 0:HEADS * HD].rearrange("p (h s d) -> p h s d", s=2, d=HD // 2)
                k_out = roped[:, t, HEADS * HD:].rearrange("p (h r s d) -> p h r s d", r=2, s=2, d=HD // 2)
                for s, op in ((0, ALU.subtract), (1, ALU.add)):
                    mine(nc.vector.tensor_tensor(a, x[:, :, 0, :], (cos, sin)[s], ALU.mult), wait=False)
                    mine(nc.vector.tensor_tensor(b, x[:, :, 1, :], (sin, cos)[s], ALU.mult))
                    mine(nc.vector.tensor_tensor(q_out[:, :, s, :], a[:, 0:HEADS], b[:, 0:HEADS], op), wait=False)
                    for r in range(2):
                        last = nc.vector.tensor_tensor(k_out[:, :, r, s, :], a[:, HEADS:], b[:, HEADS:], op)
                        if (s, r) == (1, 1):
                            last.then_inc(rope_made, 1)
                        else:
                            mine(last, wait=False)
                    dve.wait_ge(dve_own, own.value())
                dve.wait_ge(rope_made, t + 1)

            for t in range(TT):
                qk_mean_square(t)
                v_tile_lo(t)
            for t in range(TT):
                rope_tile(t)
            glu_products(1)
            for j in range(4):
                dve.wait_ge(qkT_hi_made, j + 1)
                nc.vector.tensor_tensor(qT_lo[:, j, :], ps[:, QK_BANKS[j], :], f32(qT_hi[:, j, :]), ALU.subtract)\
                    .then_inc(qkT_lo_made, 1)
            for g in range(KV):
                for side in range(2):
                    rows = slice(HD * side, HD * side + HD)
                    dve.wait_ge(qkT_hi_made, 4 + 2 * g + side + 1)
                    nc.vector.tensor_tensor(kT_lo[rows, g, side, :], ps[rows, QK_BANKS[4 + g], :], f32(kT_hi[rows, g, side, :]),
                                            ALU.subtract).then_inc(qkT_lo_made, 1)

            def attention_step(s):
                if s < HEADS * TT:
                    dve.wait_ge(scores_made, s + 1)
                    mine(nc.vector.tensor_reduce(row_max[:, s:s + 1], ps[:, SCORE_BANKS[s % 3], :], AX.X, ALU.max))
                    nc.vector.tensor_scalar(neg_max[:, s:s + 1], row_max[:, s:s + 1], -HD ** -0.5, None, ALU.mult)\
                        .then_inc(max_made, 1)
                u = s - 1
                if 0 <= u < HEADS * TT:
                    dve.wait_ge(exp_made, u + 1)
                    nc.vector.reciprocal(row_inv[:, u:u + 1], row_sum[:, u:u + 1]).then_inc(inv_made, 1)
                u = s - 3
                if 0 <= u < HEADS * TT:
                    h, t = u // TT, u % TT
                    dve.wait_ge(probT_hi_made, u + 1)
                    spot = (slice(None), h % 2, slice(None), slice(t * P, (t + 1) * P))
                    nc.vector.tensor_tensor(probT_lo[spot], ps[:, TURN_BANKS[u % 3], :].rearrange("p (k c) -> p k c", c=P),
                                            f32(probT_hi[spot]), ALU.subtract).then_inc(probT_lo_made, 1)
                conv(1)
                if s % 8 == 5 and s >= 13:
                    j = (s - 13) // 8
                    dve.wait_ge(cat_hi_made, j + 1)
                    nc.vector.tensor_tensor(catT_lo[:, j, :], ps[:, HEAD_BANKS[j % 2], :], f32(catT_hi[:, j, :]), ALU.subtract)\
                        .then_inc(cat_lo_made, 1)

            for s in range(HEADS * TT + 6):
                attention_step(s)
            conv(len(taps))

            def variance(t, halves, made, eps):
                for i, x in enumerate(halves):
                    mine(nc.vector.bn_stats(stats[:, t, i, :], x), wait=(i == len(halves) - 1))
                if own.per_turn:
                    dve.sem_inc(stats_seen, 1)
                mine(nc.vector.bn_aggr(moments[:, t, :], stats[:, t, 0:len(halves), :]))
                nc.vector.tensor_scalar(var_eps[:, t:t + 1], moments[:, t, 1:2], eps, None, ALU.add).then_inc(made, 1)

            for t in range(TT):
                dve.wait_ge(conv_turned, t + 1)
                variance(t, [ps[:, t, :]], conv_var, LN_EPS)
            for t in range(TT):
                dve.wait_ge(conv_rstd, t + 1)
                nc.vector.tensor_scalar(conv_norm[:, t, :], ps[:, t, :], moments[:, t, 0:1], rstd[:, t:t + 1],
                                        ALU.subtract, ALU.mult).then_inc(conv_normed, 1)
            for ct in range(CT):
                dve.wait_ge(cat_hi_made, 4 + ct + 1)
                nc.vector.tensor_tensor(catT_lo[:, 4 + ct, :], tmp[ct][:], f32(catT_hi[:, 4 + ct, :]), ALU.subtract)\
                    .then_inc(cat_lo_made, 1)
            for j in range(2):
                make_lo(dve, Chunk(C_OUT0 + 2 + j))

            def layer_norm(d, tile_sums, halves=(0, 1), turn=True):
                def first(t):
                    tile_sums(t)
                    for half in halves:
                        cols = slice(N * half, N * half + N)
                        mine(nc.vector.scalar_tensor_tensor(x_tok[:, t, cols], x_tok[:, t, cols], ALPHA,
                                                            ps[:, t + 4 * half, :], ALU.mult, ALU.add), wait=(half == 1))
                    variance(t, [x_tok[:, t, 0:N], x_tok[:, t, N:D]], var_made, LN_EPS)

                def second(t):
                    if t == 0:
                        dve.wait_ge(gb_landed, 32 * (d + 1))
                    dve.wait_ge(rstd_made, 4 * d + t + 1)
                    mine(nc.vector.scalar_tensor_tensor(x_tok[:, t, :], x_tok[:, t, :], moments[:, t, 0:1], ln_gb[:, 0, :],
                                                        ALU.subtract, ALU.mult))
                    nc.vector.scalar_tensor_tensor(x_tok[:, t, :], x_tok[:, t, :], rstd[:, t:t + 1], ln_gb[:, 1, :],
                                                   ALU.mult, ALU.add).then_inc(x_normed, 1)

                for t in range(TT):
                    first(t)
                    second(t)
                    if turn and t:
                        xT_tile_lo(d + 1, t - 1)
                if turn:
                    xT_tile_lo(d + 1, TT - 1)

            def sums(pm, c_last):
                def wait(t):
                    dve.wait_ge(part_made, pm + t + 1) if t < TT - 1 else dve.wait_ge(chunk_used, c_last + 1)
                return wait

            def swiglu(layer, c_ffn, c_down, pm):
                h0, f0 = NH * layer, (NH + 2) * layer
                dve.sem_inc(up_read, 2)
                with dve.Fori(0, NH // 2) as i:
                    make_lo(dve, Chunk(c_ffn + 2, i))
                    for m in range(2):
                        if m == 0:
                            dve.wait_ge(part_made, pm + 2 * i + 2)
                        else:
                            dve.wait_ge(chunk_used, c_ffn + 2 * i + 2)
                        dve.wait_ge(gate_read, f0 + 2 * i + m + 3)
                        nc.vector.tensor_tensor(tmp[2 + m][:], tmp[m][:], ps[:, SIDE_A[2 + m], :], ALU.mult)\
                            .then_inc(up_read, 1)
                        dve.wait_ge(h_hi_made, h0 + 2 * i + m + 1)
                        nc.vector.tensor_tensor(hT_lo[:, bass.ds(2 * i + m, 1), :], tmp[2 + m][:].unsqueeze(1),
                                                f32(hT_hi[:, bass.ds(2 * i + m, 1), :]), ALU.subtract)\
                            .then_inc(h_lo_made, 1)
                    make_lo(dve, Chunk(c_ffn + 3, i))
                for j in range(NH // 2 - 2):
                    make_lo(dve, Chunk(c_down + j + 2))

            layer_norm(0, sums(PM_OUT0, C_FFN0 - 1))
            swiglu(0, C_FFN0, C_DOWN0, PM_FFN0)
            layer_norm(1, sums(PM_DOWN0, C_RET - 1))

            dve.sem_inc(ret_masked, FREE)
            dve.sem_inc(o_normed, FREE)
            dve.wait_ge(rope1_landed, 16)
            per_head = 12 + 8
            start = own.n
            with dve.Fori(0, RH) as h:
                own.per_turn, own.turn = 16, h
                cos, sin = rope1[:, 0, :], rope1[:, 1, :]
                for x, hi, lo in ((0, rq_hi, rq_lo), (1, rk_hi, rk_lo)):
                    make_lo(dve, Chunk(C_RET + 2 + x, h, 6))
                    dve.wait_ge(chunk_used, C_RET + 6 * h + x + 1)
                    x1, x2 = ps[:, SIDE_A[2 * x], :], ps[:, SIDE_A[2 * x + 1], :]
                    for half, op in ((0, ALU.subtract), (1, ALU.add)):
                        mine(nc.vector.tensor_tensor(tmp[0][:], (cos, sin)[half], x1, ALU.mult), wait=False)
                        mine(nc.vector.tensor_tensor(tmp[1][:], (sin, cos)[half], x2, ALU.mult))
                        nc.vector.tensor_tensor(tmp[2 + half][:], tmp[0][:], tmp[1][:], op).then_inc(rot_made, 1)
                        dve.wait_ge(rot_made, 4 * h + 2 * x + half + 1)
                    for half in range(2):
                        dve.wait_ge(rot_hi, 4 * h + 2 * x + half + 1)
                        nc.vector.tensor_tensor(lo[:, half, :], tmp[2 + half][:], f32(hi[:, half, :]), ALU.subtract)\
                            .then_inc(rot_lo, 1)
                make_lo(dve, Chunk(C_RET + 4, h, 6))
                for t in range(TT):
                    dve.wait_ge(rv_hi_made, 4 * h + t + 1)
                    nc.vector.tensor_tensor(rv_lo[:, t, :], ps[:, SIDE_B[t], :], f32(rv_hi[:, t, :]), ALU.subtract)\
                        .then_inc(rv_lo_made, 1)

                def masked(kt):
                    dve.wait_ge(ret_scored, 4 * h + kt + 1)
                    if kt == 0:
                        dve.wait_ge(mask_made, h + 1)
                    if kt >= 2:
                        dve.wait_ge(sT_lo_made, 4 * h + kt - 1)
                    left = (SEQ - P) - P * kt
                    nc.vector.scalar_tensor_tensor(tmp[kt % 2][:], ps[:, SIDE_A[kt], :], RK ** -0.5, mask[:, left:left + SEQ],
                                                   ALU.mult, ALU.mult).then_inc(ret_masked, 1)

                def masked_lo(kt):
                    dve.wait_ge(sT_hi_made, 4 * h + kt + 1)
                    nc.vector.tensor_tensor(sT_lo[:, kt % 2, :], tmp[kt % 2][:], f32(sT_hi[:, kt % 2, :]), ALU.subtract)\
                        .then_inc(sT_lo_made, 1)

                masked(0)
                for kt in range(1, TT):
                    masked(kt)
                    masked_lo(kt - 1)
                masked_lo(TT - 1)
                make_lo(dve, Chunk(C_RET + 5, h, 6))
                for t in range(TT):
                    dve.wait_ge(o_made, 4 * h + t + 1)
                    variance(t, [ps[:, SIDE_B[t], :]], o_var, LN_EPS)
                for t in range(TT):
                    dve.wait_ge(o_rstd, 4 * h + t + 1)
                    nc.vector.tensor_scalar(y_tok[:, t, bass.ds(h * RV, RV)], ps[:, SIDE_B[t], :], moments[:, t, 0:1],
                                            rstd[:, t:t + 1], ALU.subtract, ALU.mult).then_inc(o_normed, 1)
                make_lo(dve, Chunk(C_RET + 6, h, 6))
                for t in range(TT):
                    dve.wait_ge(g_read, 4 * h + t + 1 + FREE)
                    dve.wait_ge(o_normed, 4 * h + t + 1 + FREE)
                    y = y_tok[:, t, bass.ds(h * RV, RV)]
                    nc.vector.tensor_tensor(y, y, tmp[2 + t % 2][:], ALU.mult).then_inc(y_made, 1)
                make_lo(dve, Chunk(C_RET + 7, h, 6))
            assert own.n == start + 16, own.n - start
            own.n = start + 16 * RH
            own.per_turn = 0

            for q in range(32):
                kt, bank = q % 16, y_bank(q)
                dve.wait_ge(yT_hi_made, q + 1)
                nc.vector.scalar_tensor_tensor(yT_lo[:, q % 8, :], ps[:, bank, :], ret_gain[:, kt:kt + 1],
                                               f32(yT_hi[:, q % 8, :]), ALU.mult, ALU.subtract).then_inc(yT_lo_made, 1)
                if q % 4 == 3 and 7 <= q < 28:
                    make_lo(dve, Chunk(C_OUT1 + (q - 7) // 4 + 2))
                if q == 19:
                    for t in range(TT):
                        sums(PM_OUT1A, C_OUT1 + 3)(t)
                        nc.vector.scalar_tensor_tensor(x_tok[:, t, 0:N], x_tok[:, t, 0:N], ALPHA, ps[:, t, :],
                                                       ALU.mult, ALU.add).then_inc(resid_read, 1)
            dve.wait_ge(resid_read, TT)
            layer_norm(2, sums(PM_OUT1B, C_FFN1 - 1), halves=(1,))
            swiglu(1, C_FFN1, C_DOWN1, PM_FFN1)
            layer_norm(3, sums(PM_DOWN1, N_CHUNKS - 1), turn=False)

        @block.tensor
        def _(pe):
            def product(dst, a, b, start, stop):
                nc.tensor.matmul(dst, a[0], b[0], start=start, stop=False)
                nc.tensor.matmul(dst, a[0], b[1], start=False, stop=False)
                return nc.tensor.matmul(dst, a[1], b[0], start=False, stop=stop)

            def weights(ch, k):
                return tuple(w[ch.s][:].rearrange("p (k n) -> p k n", k=k) for w in (w_hi, w_lo))

            def turn(stage, t):
                for half in range(2):
                    for k in range(4):
                        last = nc.tensor.transpose(ps[:, t + 4 * half, k * P:(k + 1) * P],
                                                   x_tok[:, t, (4 * half + k) * P:(4 * half + k + 1) * P], ident[:])
                    last.then_inc(turned, 1)

            def feature_tiles(ch, banks, bank_free, tokens=slice(0, SEQ), final=True):
                hi, lo = weights(ch, KD)
                for m in range(2):
                    bank_free(m)
                    cols = slice(m * P, (m + 1) * P)
                    for k in range(KD):
                        last = product(ps[:, banks[m], tokens], (hi[:, k, cols], lo[:, k, cols]),
                                       (xT_hi[:, k, tokens], xT_lo[:, k, tokens]), k == 0, k == KD - 1)
                    if final:
                        last.then_inc(chunk_used if m else part_made, 1)

            def first_tiles(stage, chunks, split, bank_free):
                for half in range(2):
                    pe.wait_ge(xT_lo_made, 8 * stage + 4 * half + 4)
                    for j, ch in enumerate(chunks):
                        if half == 0:
                            split(j)
                        feature_tiles(ch, SIDE_A[2 * j:2 * j + 2],
                                      (lambda m, j=j: bank_free(j, m)) if half == 0 else (lambda m: None),
                                      slice(half * SEQ // 2, (half + 1) * SEQ // 2), half == 1)

            def token_tiles(chunks, banks, rows, cols, bank_free):
                for j, ch in enumerate(chunks):
                    pe.wait_ge(lo_made, ch.lo)
                    hi, lo = weights(ch, rows)
                    for k in range(rows):
                        for t in range(TT):
                            if j == 0 and k == 0:
                                bank_free(t)
                            row, tok = rows * j + k, slice(t * P, (t + 1) * P)
                            end = j == len(chunks) - 1 and k == rows - 1
                            last = product(ps[:, banks[t], 0:cols], (xT_hi[:, row, tok], xT_lo[:, row, tok]),
                                           (hi[:, k, :], lo[:, k, :]), row == 0, end)
                            if end and t < TT - 1:
                                last.then_inc(part_made, 1)
                    last.then_inc(chunk_used, 1)

            TAIL = ((0, 0), (0, 1), (1, 0), (0, 2), (1, 1), (0, 3), (1, 2), (1, 3))

            def out_projection(c, n, sT, ready, stage, side_a_free):
                def part(ch, k, row, t):
                    hi, lo = weights(ch, 2)
                    tok = slice(t * P, (t + 1) * P)
                    for a, b in ((0, 0), (0, 1), (1, 0)):
                        for half in range(2):
                            last = nc.tensor.matmul(ps[:, t + 4 * half, :], sT[a][:, row, tok],
                                                    (hi, lo)[b][:, k, N * half:N * half + N],
                                                    start=(row == 0 and a == b), stop=(row == 2 * n - 1 and a == 1))
                    return last

                for j in range(n - 2):
                    wait_split(pe, c + j)
                    if j == 0:
                        for tiles, free in ((2, 3), lambda: None), ((0, 1), side_a_free):
                            free()
                            for k in range(2):
                                ready(k)
                                for t in tiles:
                                    last = part(Chunk(c), k, k, t)
                    else:
                        for k in range(2):
                            ready(2 * j + k)
                            for t in range(TT):
                                last = part(Chunk(c + j), k, 2 * j + k, t)
                    last.then_inc(chunk_used, 1)
                for j, t in TAIL:
                    if t == 0:
                        wait_split(pe, c + n - 2 + j)
                        for k in range(2):
                            ready(2 * (n - 2 + j) + k)
                    for k in range(2):
                        last = part(Chunk(c + n - 2 + j), k, 2 * (n - 2 + j) + k, t)
                    if t == TT - 1:
                        last.then_inc(chunk_used, 1)
                    elif j:
                        last.then_inc(part_made, 1)
                if stage is not None:
                    for t in range(TT):
                        turn_when_normed(stage, t)

            def turn_when_normed(stage, t):
                pe.wait_ge(x_normed, 4 * (stage - 1) + t + 1)
                turn(stage, t)

            pe.wait_ge(pool_own, 2)
            for t in range(TT):
                pe.wait_ge(x_landed[t], 16)
                turn(0, t)
            first_tiles(0, [Chunk(0), Chunk(1)], lambda j: wait_split(pe, j), lambda j, m: None)
            wait_split(pe, C_Q + 1)
            token_tiles([Chunk(C_Q), Chunk(C_Q + 1)], SIDE_B, 4, N, lambda t: None)
            token_tiles([Chunk(C_KV)], SIDE_A, KD, 256, lambda t: pe.wait_ge(z_made, 2) if t == 0 else None)
            for part in range(2):
                wait_split(pe, C_GLU[1] + part)
                feature_tiles(Chunk(C_GLU[1] + part), SIDE_B[2 * part:2 * part + 2],
                              lambda m: pe.wait_ge(q_copied, TT) if m == 0 else None)
            pe.wait_ge(v_split, 2 * TT)
            pe.wait_ge(z_made, 4)
            for t in range(TT):
                pe.wait_ge(rope_made, t + 1)
                for j in range(6):
                    last = nc.tensor.transpose(ps[:, QK_BANKS[j], t * P:(t + 1) * P],
                                               roped[:, t, j * P:(j + 1) * P], ident[:])
                    if t == TT - 1:
                        last.then_inc(qk_turned, 1)

            def attention_step(s):
                if s < HEADS * TT:
                    h, t = s // TT, s % TT
                    if s < 3:
                        pe.wait_ge(qkT_lo_made, 8)
                    else:
                        pe.wait_ge(exp_made, s - 2)
                    q = tuple(x[:, h // 2, t * P:(t + 1) * P] for x in (qT_hi, qT_lo))
                    k = tuple(x[:, h // (HEADS // KV), h % 2, :] for x in (kT_hi, kT_lo))
                    product(ps[:, SCORE_BANKS[s % 3], :], q, k, True, True).then_inc(scores_made, 1)
                u = s - 2
                if 0 <= u < HEADS * TT:
                    pe.wait_ge(prob_made, u + 1)
                    if u >= 3:
                        pe.wait_ge(probT_lo_made, u - 2)
                    for k in range(TT):
                        last = nc.tensor.transpose(ps[:, TURN_BANKS[u % 3], k * P:(k + 1) * P],
                                                   tmp[u % 3][:, k * P:(k + 1) * P], ident[:])
                    last.then_inc(prob_turned, 1)
                if s >= 8 and s % 4 == 0 and (s - 8) // 4 < HEADS:
                    h = (s - 8) // 4
                    pe.wait_ge(probT_lo_made, 4 * h + 4)
                    if h % 2 == 0 and h >= 4:
                        pe.wait_ge(cat_lo_made, h // 2 - 1)
                    g = h // (HEADS // KV)
                    for k in range(TT):
                        v = (v_hi[:, k, g, h % 2, :], v_lo[:, k, g, h % 2, :])
                        last = product(ps[:, HEAD_BANKS[(h // 2) % 2], :], v, (probT_hi[:, h % 2, k, :], probT_lo[:, h % 2, k, :]),
                                       k == 0 and h % 2 == 0, k == TT - 1 and h % 2 == 1)
                    last.then_inc(head_done, 1)

            for s in range(HEADS * TT + 6):
                attention_step(s)
            pe.wait_ge(tap_done, 2 * TAPS)
            pe.wait_ge(part_added, 2 * (TAPS - 1))
            pe.wait_ge(probT_lo_made, HEADS * TT)
            for t in range(TT):
                for ct in range(CT):
                    last = nc.tensor.transpose(ps[:, t, ct * P:(ct + 1) * P], acc[:, ct, t * P:(t + 1) * P], ident[:])
                last.then_inc(conv_turned, 1)
            pe.wait_ge(cat_lo_made, 4)
            for t in range(TT):
                pe.wait_ge(conv_normed, t + 1)
                for ct in range(CT):
                    last = nc.tensor.transpose(ps[:, 4 + ct, t * P:(t + 1) * P], conv_norm[:, t, ct * P:(ct + 1) * P],
                                               ident[:])
                    if t == TT - 1:
                        last.then_inc(conv_back, 1)
            pe.wait_ge(silu_made, CT)
            out_projection(C_OUT0, 4, (catT_hi, catT_lo), lambda row: pe.wait_ge(cat_lo_made, row + 1), 1, lambda: None)

            def swiglu(layer, c_ffn, c_down, stage):
                h0, f0 = NH * layer, (NH + 2) * layer
                first_tiles(2 * layer + 1, [Chunk(c_ffn), Chunk(c_ffn + 1)], lambda j: wait_split(pe, c_ffn + j),
                            lambda j, m: pe.wait_ge((gate_read, up_read)[j], f0 + m + 1))
                with pe.Fori(1, NH // 2) as i:
                    for j, read in enumerate((gate_read, up_read)):
                        ch = Chunk(c_ffn + j, i)
                        pe.wait_ge(lo_made, ch.lo)
                        feature_tiles(ch, SIDE_A[2 * j:2 * j + 2], lambda m: pe.wait_ge(read, f0 + 2 * i + m + 1))
                out_projection(c_down, NH // 2, (hT_hi, hT_lo), lambda row: pe.wait_ge(h_lo_made, h0 + row + 1), stage,
                               lambda: pe.wait_ge(up_read, f0 + NH + 2))

            swiglu(0, C_FFN0, C_DOWN0, 2)

            for j in range(2):
                wait_split(pe, C_RET + j)
            with pe.Fori(0, RH) as h:
                chunks = [Chunk(C_RET + j, h, 6) for j in range(2)]
                first_tiles(2, chunks, lambda j: pe.wait_ge(lo_made, chunks[j].lo),
                            lambda j, m: pe.wait_ge(g_read, 4 * h + 2 * j + m + 1))
                token_tiles([Chunk(C_RET + 2, h, 6), Chunk(C_RET + 3, h, 6)], SIDE_B, 4, N,
                            lambda t: pe.wait_ge(o_normed, 4 * h + t + 1))
                pe.wait_ge(rot_lo, 4 * h + 4)
                for kt in range(TT):
                    for half in range(2):
                        last = product(ps[:, SIDE_A[kt], :], (rk_hi[:, half, kt * P:(kt + 1) * P], rk_lo[:, half, kt * P:(kt + 1) * P]),
                                       (rq_hi[:, half, :], rq_lo[:, half, :]), half == 0, half == 1)
                    last.then_inc(ret_scored, 1)
                pe.wait_ge(rv_lo_made, 4 * h + 4)
                for kt in range(TT):
                    pe.wait_ge(sT_lo_made, 4 * h + kt + 1)
                    for t in range(TT):
                        tok = slice(t * P, (t + 1) * P)
                        last = product(ps[:, SIDE_B[t], :], (sT_hi[:, kt % 2, tok], sT_lo[:, kt % 2, tok]),
                                       (rv_hi[:, kt, :], rv_lo[:, kt, :]), kt == 0, kt == TT - 1)
                        if kt == TT - 1:
                            last.then_inc(o_made, 1)
                    if kt < TT - 1:
                        last.then_inc(sT_used, 1)
                token_tiles([Chunk(C_RET + 4, h, 6), Chunk(C_RET + 5, h, 6)], SIDE_A, 4, N, lambda t: None)

            def turn_y(q):
                if q == 0:
                    pe.wait_ge(o_normed, 4 * RH + FREE)
                elif q == 2:
                    pe.wait_ge(g_read, 4 * RH + FREE)
                if q < RH * TT and q % TT == 0:
                    pe.wait_ge(y_made, 4 * (q // TT + 1))
                if q == 20:
                    pe.wait_ge(resid_read, TT)
                elif q >= 4:
                    pe.wait_ge(yT_lo_made, q - 3)
                for t in range(TT):
                    last = nc.tensor.transpose(ps[:, y_bank(q), t * P:(t + 1) * P],
                                               y_tok[:, t, (q % 16) * P:(q % 16 + 1) * P], ident[:])
                last.then_inc(y_turned, 1)

            def y_part(q, t):
                ch, k, tok = Chunk(C_OUT1 + q // 4), q % 4, slice(t * P, (t + 1) * P)
                hi, lo = weights(ch, 4)
                return product(ps[:, 4 * (q // 16) + t, :], (yT_hi[:, q % 8, tok], yT_lo[:, q % 8, tok]),
                               (hi[:, k, :], lo[:, k, :]), q % 16 == 0, q % 16 == 15)

            for q in range(4):
                turn_y(q)
            for q in range(24):
                if q % 4 == 0:
                    wait_split(pe, C_OUT1 + q // 4)
                pe.wait_ge(yT_lo_made, q + 1 if q != 16 else 20)
                for t in range(TT):
                    last = y_part(q, t)
                    if q == 15 and t < TT - 1:
                        last.then_inc(part_made, 1)
                last.then_inc(chunk_used if q % 4 == 3 else yT_used, 1)
                if q == 17:
                    turn_y(20)
                if q != 16:
                    turn_y(q + 4)
            for q in range(28, 32):
                turn_y(q)
            for j, t in TAIL:
                if t == 0:
                    wait_split(pe, C_FFN1 - 2 + j)
                    pe.wait_ge(yT_lo_made, 28 + 4 * j)
                for q in range(24 + 4 * j, 28 + 4 * j):
                    last = y_part(q, t)
                if t == TT - 1:
                    last.then_inc(chunk_used, 1)
                elif j:
                    last.then_inc(part_made, 1)
            for t in range(TT):
                turn_when_normed(3, t)
            swiglu(1, C_FFN1, C_DOWN1, None)


def rope_tables():
    t = np.arange(SEQ)
    row, col = (t // GRID_W).astype(np.float32), (t % GRID_W).astype(np.float32)

    def angles(head_dim):
        axis = head_dim // 2
        freq = np.float32(THETA) ** (-np.arange(0, axis, 2, dtype=np.float32) / np.float32(axis))
        return np.concatenate([row[:, None] * freq, col[:, None] * freq], axis=-1).astype(np.float32)

    a, r = angles(HD), angles(RK)
    by_token = np.stack([np.cos(a), np.sin(a)], axis=1).reshape(TT, P, 2, HD // 2).transpose(1, 0, 2, 3)
    by_freq = np.stack([np.cos(r).T, np.sin(r).T], axis=1)
    return np.ascontiguousarray(by_token, np.float32), np.ascontiguousarray(by_freq, np.float32)


_PLAIN = ["x", "l0_w_in", "l0_q_norm_g", "l0_k_norm_g", "l0_w_out", "l0_ln_mix_g", "l0_ln_mix_b",
          "l0_ffn_w_gate", "l0_ffn_w_up", "l0_ffn_w_down", "l0_ln_ffn_g", "l0_ln_ffn_b",
          "l1_w_in", "l1_w_out", "l1_ln_mix_g", "l1_ln_mix_b", "l1_ffn_w_gate", "l1_ffn_w_up",
          "l1_ffn_w_down", "l1_ln_ffn_g", "l1_ln_ffn_b"]


def kernel(**inputs):
    import numpy as _np
    import concourse.bacc as _bacc
    from concourse import mybir as _mybir
    from concourse.bass_utils import run_bass_kernel_spmd as _run

    given = {name: _np.asarray(a) for name, a in inputs.items()}
    arrays = {name: given[name] for name in _PLAIN}
    by_channel = _np.concatenate([given["l0_dw_w"], given["l0_dw_b"][None], given["l0_conv_norm_g"][None],
                                  given["l0_conv_norm_b"][None]])
    arrays["conv_par"] = by_channel.reshape(TAPS + 3, CT, P).transpose(2, 1, 0)
    arrays["decay"] = _np.stack([given["l1_log_decay_fwd"], given["l1_log_decay_bwd"]])
    arrays["ret_gain"] = given["l1_ret_norm_g"].reshape(-1, P).T
    arrays["rope0"], arrays["rope1"] = rope_tables()

    nc = _bacc.Bacc("TRN2", target_bir_lowering=False, num_devices=1)
    ins, feed = {}, {}
    for name, a in arrays.items():
        feed[f"in_{name}"] = _np.ascontiguousarray(a)
        ins[name] = nc.dram_tensor(f"in_{name}", a.shape, _mybir.dt.from_np(a.dtype), kind="ExternalInput").ap()
    out = nc.dram_tensor("out_0", (1, SEQ, D), _mybir.dt.float32, kind="ExternalOutput").ap()
    build_encoder(nc, ins, out)
    r = _run(nc, [feed], core_ids=[0])
    return r.results[0]["out_0"]
```

```python
from contextlib import ExitStack

import numpy as np

import concourse.bass as bass
from concourse import mybir

ALU = mybir.AluOpType
ACT = mybir.ActivationFunctionType
AX = mybir.AxisListType
F32 = mybir.dt.float32
F32R = mybir.dt.float32r

P = 128
SEQ = 512
D = 1024
TT = SEQ // P
KD = D // P
N = 512
HIDDEN = 2816
NH = HIDDEN // P
CHUNK = 2048
ALPHA = 4.0 ** 0.25
LN_EPS, RMS_EPS = 1e-5, 1e-6
GRID_W, THETA = 64, 10000.0

HEADS, KV, HD = 8, 2, 64
CT = 4
TAPS = 31
PAD = TAPS // 2
RH, RK, RV = 4, 256, 512
SPAN = 2 * SEQ - P

C_GLU = (0, 5)
C_KV = 2
C_Q = 3
C_OUT0 = 7
C_FFN0 = 11
C_DOWN0 = C_FFN0 + NH
C_RET = C_DOWN0 + NH // 2
C_OUT1 = C_RET + 6 * RH
C_FFN1 = C_OUT1 + 8
C_DOWN1 = C_FFN1 + NH
N_CHUNKS = C_DOWN1 + NH // 2

SEAMS = (C_OUT0, C_FFN0, C_RET, C_FFN1)

SIDE_A, SIDE_B = (0, 1, 4, 5), (2, 3, 6, 7)
K_BANKS = (6, 7)
SCORE_BANKS, TURN_BANKS, OUT_BANKS, CONV_BANK, SPARE = (0, 1), (5, 2), (3, 6), 4, 7
BACK_BANKS = (0, 1, 4, 7)
BATCH = 4
BATCHES = 7
HANDED = 10
STEPS = HEADS * TT
GROUP = 4

OUT_TO_FEATURES = (14, 22, 30)
CONV_TO_TOKENS = (23, 25, 27, 29)
CONV_TO_FEATURES = STEPS
LAST_STEP = STEPS + 4
OUT0_SPLIT_STEPS = (8, 16)
SIDE_SUM_STEP = 21

OWN_PER_HEAD = 16

DVE_TAPS = 2 * TAPS - HANDED + TAPS - BATCH * BATCHES
ADDED = TAPS - 1 + HANDED - 1

FREE = 4


def build_encoder(nc, ins, out):
    ctx = ExitStack()
    with ctx:
        top = [-(-nc.sbuf_base // 32) * 32]

        def place(name, shape, dt, at=None):
            size = 4 * int(np.prod(shape[1:]))
            offset = top[0] if at is None else at
            if at is None:
                top[0] += -(-size // 32) * 32
            return nc.alloc_sbuf_tensor_at(name, shape, dt, offset=offset)

        x_tok = place("x_tok", [P, TT, D], F32)
        xt_at = top[0]
        xT_hi = place("xT_hi", [P, KD, SEQ], F32R)
        xT_lo = place("xT_lo", [P, KD, SEQ], F32R)
        raw = [place(f"raw{s}", [P, CHUNK], F32) for s in range(2)]
        w_hi = [place(f"w_hi{s}", [P, CHUNK], F32R) for s in range(2)]
        w_lo = [place(f"w_lo{s}", [P, CHUNK], F32R) for s in range(2)]
        gb_at = top[0]
        ln_gb = place("ln_gb", [P, 2, D], F32)
        tmp_at = top[0]
        tmp = [place(f"tmp{i}", [P, N], F32) for i in range(4)]
        ident = place("ident", [P, P], F32)
        conv_par = place("conv_par", [P, CT, TAPS + 3], F32)
        qk_gain = place("qk_gain", [P, 2, HD], F32)
        rope0 = place("rope0", [P, TT, 2, HD // 2], F32)
        decay = place("decay", [P, 2, RH], F32)
        ret_gain = place("ret_gain", [P, RH * RV // P], F32)
        minus_half = place("minus_half", [P, 16], F32)
        minus_one = place("minus_one", [P, GROUP], F32)
        stats = place("stats", [P, TT, 2, 6], F32)
        squares = place("squares", [P, D], F32, tmp_at)
        x_sum = place("x_sum", [P, TT, 2], F32)
        x_mean = place("x_mean", [P, TT], F32)
        minus_mean = place("minus_mean", [P, TT], F32)
        moments = place("moments", [P, TT, 2], F32)
        var_eps = place("var_eps", [P, TT], F32)
        rstd = place("rstd", [P, TT], F32)
        q_ms = place("q_ms", [P, TT, HEADS], F32)
        q_scale = place("q_scale", [P, TT, HEADS], F32)
        k_ms = place("k_ms", [P, TT, KV], F32)
        k_rstd = place("k_rstd", [P, TT, KV], F32)
        row_max = place("row_max", [P, STEPS], F32)
        neg_max = place("neg_max", [P, STEPS], F32)
        row_sum = place("row_sum", [P, STEPS], F32)
        row_inv = place("row_inv", [P, STEPS], F32)
        work = top[0]
        hT_hi = place("hT_hi", [P, NH, SEQ], F32R, work)
        hT_lo = place("hT_lo", [P, NH, SEQ], F32R, work + NH * SEQ * 4)
        KB = 1024
        catT_hi = place("catT_hi", [P, KD, SEQ], F32R, work)
        catT_lo = place("catT_lo", [P, KD, SEQ], F32R, work + 16 * KB)
        q_roped = place("q_roped", [P, TT, HEADS * HD], F32, work)
        k_roped = place("k_roped", [P, TT, KV, 2, HD], F32, work + 8 * KB)
        q_sq = place("q_sq", [P, TT, HEADS * HD], F32, work + 12 * KB)
        k_sq = place("k_sq", [P, TT, KV * HD], F32, work + 20 * KB)
        k_turned = place("k_turned", [P, TT, KV * HD], F32, work + 22 * KB)
        tap_part = place("tap_part", [P, 4, SEQ], F32, work + 24 * KB)
        qT_hi = place("qT_hi", [P, TT, 4, P], F32R, work + 32 * KB)
        qT_lo = place("qT_lo", [P, TT, 4, P], F32R, work + 40 * KB)
        kT_hi = place("kT_hi", [P, KV, 2, SEQ], F32R, work + 48 * KB)
        kT_lo = place("kT_lo", [P, KV, 2, SEQ], F32R, work + 56 * KB)
        v_parts = place("v_parts", [P, TT, KV, 2, HD], F32R, work + 64 * KB)
        rope_gain = place("rope_gain", [P, TT, 2, 2, HD], F32, work + 68 * KB)
        side_sum = place("side_sum", [P, SEQ], F32, work + 68 * KB)
        o_raw = [place(f"o_raw{i}", [P, GROUP, 2, HD], F32, work + at * KB) for i, at in enumerate((72, 78))]
        diag = place("diag", [P, 2, BATCH, P], F32, work + 74 * KB)
        diag_hi = place("diag_hi", [P, 2, BATCH, P], F32R, work + 8 * KB)
        diag_lo = place("diag_lo", [P, 2, BATCH, P], F32R, work + 12 * KB)
        z_hi = place("z_hi", [P, SEQ + 2 * PAD], F32R, xt_at + 24 * KB)
        z_lo = place("z_lo", [P, SEQ + 2 * PAD], F32R, xt_at + 28 * KB)
        zpad = place("zpad", [P, CT, SEQ + 2 * PAD], F32, work + 80 * KB)
        conv_norm = place("conv_norm", [P, TT, CT * P], F32, work + 80 * KB)
        acc = place("acc", [P, CT, SEQ], F32, gb_at)
        probT_hi = place("probT_hi", [P, 3, SEQ], F32R, xt_at)
        probT_lo = place("probT_lo", [P, 3, SEQ], F32R, xt_at + 6 * KB)
        o_tok = place("o_tok", [P, 2, HEADS * HD], F32, xt_at + 12 * KB)
        swished = place("swished", [P, CT, SEQ], F32, xt_at + 16 * KB)
        y_tok = place("y_tok", [P, RH * TT * RV], F32, work)
        rq_hi = place("rq_hi", [P, 2, SEQ], F32R, work + 32 * KB)
        rq_lo = place("rq_lo", [P, 2, SEQ], F32R, work + 36 * KB)
        rk_hi = place("rk_hi", [P, 2, SEQ], F32R, work + 40 * KB)
        rk_lo = place("rk_lo", [P, 2, SEQ], F32R, work + 44 * KB)
        rv_hi = place("rv_hi", [P, TT, RV], F32R, work + 48 * KB)
        rv_lo = place("rv_lo", [P, TT, RV], F32R, work + 56 * KB)
        sT_hi = place("sT_hi", [P, 2, SEQ], F32R, work + 64 * KB)
        sT_lo = place("sT_lo", [P, 2, SEQ], F32R, work + 68 * KB)
        ahead = place("ahead", [P, SPAN], F32, work + 72 * KB)
        behind = place("behind", [P, SPAN], F32, work + 72 * KB + 4 * SPAN)
        mask = place("mask", [P, SPAN], F32, work + 72 * KB + 8 * SPAN)
        mask_b = place("mask_b", [P, SPAN], F32, work + 72 * KB + 12 * SPAN)
        yT_at = [work + 32 * KB + 4 * KB * q if q < 14 else work + 4 * KB * (q - 14) for q in range(RH * TT)]
        yT_hi = [place(f"yT_hi{q}", [P, SEQ], F32R, at) for q, at in enumerate(yT_at)]
        yT_lo = [place(f"yT_lo{q}", [P, SEQ], F32R, at + 2 * KB) for q, at in enumerate(yT_at)]
        rope1 = place("rope1", [P, 2, SEQ], F32, gb_at)

        ps = ctx.enter_context(nc.psum_tensor("ps", [P, 8, N], F32))

        def f32(ap):
            return ap.bitcast(F32)

        def sem(name):
            return ctx.enter_context(nc.semaphore(name))

        raw_landed = [sem(f"raw_landed{s}") for s in range(2)]
        x_landed = [sem(f"x_landed{t}") for t in range(TT)]
        par_landed = sem("par_landed")
        gb_landed = sem("gb_landed")
        rope1_landed = sem("rope1_landed")
        out_landed = sem("out_landed")
        hi_made = sem("hi_made")
        lo_made = sem("lo_made")
        seam_lo_made = sem("seam_lo_made")
        chunk_used = sem("chunk_used")
        part_made = sem("part_made")
        consts_made = sem("consts_made")
        dve_own = sem("dve_own")
        stats_seen = sem("stats_seen")
        turned = sem("turned")
        xT_hi_made = sem("xT_hi_made")
        xT_lo_made = sem("xT_lo_made")
        mean_made = sem("mean_made")
        var_made = sem("var_made")
        rstd_made = sem("rstd_made")
        x_normed = sem("x_normed")
        resid_read = sem("resid_read")
        gate_read = sem("gate_read")
        up_read = sem("up_read")
        h_hi_made = sem("h_hi_made")
        h_lo_made = sem("h_lo_made")
        sig_made = sem("sig_made")
        z_made = sem("z_made")
        tap_done = sem("tap_done")
        part_tapped = sem("part_tapped")
        part_added = sem("part_added")
        diag_made = sem("diag_made")
        diag_hi_made = sem("diag_hi_made")
        diag_lo_made = sem("diag_lo_made")
        diag_used = sem("diag_used")
        z_hi_made = sem("z_hi_made")
        z_lo_made = sem("z_lo_made")
        conv_copied = sem("conv_copied")
        v_hi_made = sem("v_hi_made")
        v_lo_made = sem("v_lo_made")
        k_sq_made = sem("k_sq_made")
        k_ms_made = sem("k_ms_made")
        k_turn_made = sem("k_turn_made")
        k_roped_made = sem("k_roped_made")
        q_sq_made = sem("q_sq_made")
        q_ms_made = sem("q_ms_made")
        q_scale_made = sem("q_scale_made")
        rope_gain_made = sem("rope_gain_made")
        pool_own = sem("pool_own")
        q_roped_made = sem("q_roped_made")
        k_in_psum = sem("k_in_psum")
        q_in_psum = sem("q_in_psum")
        kT_hi_made = sem("kT_hi_made")
        kT_lo_made = sem("kT_lo_made")
        qT_hi_made = sem("qT_hi_made")
        qT_lo_made = sem("qT_lo_made")
        scores_made = sem("scores_made")
        max_made = sem("max_made")
        exp_made = sem("exp_made")
        prob_turned = sem("prob_turned")
        probT_hi_made = sem("probT_hi_made")
        probT_lo_made = sem("probT_lo_made")
        head_done = sem("head_done")
        o_copied = sem("o_copied")
        o_divided = sem("o_divided")
        o_turned = sem("o_turned")
        att_hi_made = sem("att_hi_made")
        att_lo_made = sem("att_lo_made")
        swish_hi_made = sem("swish_hi_made")
        swish_lo_made = sem("swish_lo_made")
        conv_turned = sem("conv_turned")
        conv_var = sem("conv_var")
        conv_rstd = sem("conv_rstd")
        conv_normed = sem("conv_normed")
        conv_back = sem("conv_back")
        silu_made = sem("silu_made")
        rot_made = sem("rot_made")
        rot_hi = sem("rot_hi")
        rot_lo = sem("rot_lo")
        rv_hi_made = sem("rv_hi_made")
        rv_lo_made = sem("rv_lo_made")
        exponent_made = sem("exponent_made")
        mask_made = sem("mask_made")
        ret_scored = sem("ret_scored")
        ret_masked = sem("ret_masked")
        sT_hi_made = sem("sT_hi_made")
        sT_lo_made = sem("sT_lo_made")
        sT_used = sem("sT_used")
        o_made = sem("o_made")
        o_var = sem("o_var")
        o_rstd = sem("o_rstd")
        o_normed = sem("o_normed")
        g_read = sem("g_read")
        y_made = sem("y_made")
        y_turned = sem("y_turned")
        yT_hi_made = sem("yT_hi_made")
        yT_lo_made = sem("yT_lo_made")

        PM_GLU, PM_KV, PM_Q, PM_OUT0, PM_FFN0 = (0, 8), 2, 5, 10, 13
        PM_DOWN0 = PM_FFN0 + NH
        PM_RET = PM_DOWN0 + 3
        PM_OUT1A = PM_RET + RH * (2 + 3 + 3)
        PM_OUT1B = PM_OUT1A + 3
        PM_FFN1 = PM_OUT1B + 3
        PM_DOWN1 = PM_FFN1 + NH

        def by_row_tile(w):
            return w.rearrange("(k p) n -> p k n", p=P)

        W0, WO0 = by_row_tile(ins["l0_w_in"]), by_row_tile(ins["l0_w_out"])
        W1, WO1 = by_row_tile(ins["l1_w_in"]), by_row_tile(ins["l1_w_out"])
        gate_w = [by_row_tile(ins[f"l{i}_ffn_w_gate"]) for i in range(2)]
        up_w = [by_row_tile(ins[f"l{i}_ffn_w_up"]) for i in range(2)]
        down_w = [by_row_tile(ins[f"l{i}_ffn_w_down"]) for i in range(2)]
        A0 = HEADS * HD + 2 * KV * HD

        class Chunk:

            def __init__(self, first, turn=0, stride=2):
                self.s = first % 2
                self.first = first
                self.c = first + stride * turn
                self.nth = first // 2 + stride // 2 * turn
                self.lo = self.c + 1 - 2 * sum(first >= seam for seam in SEAMS)

        def wait_split(eng, c):
            for n, seam in enumerate(SEAMS):
                if seam <= c < seam + 2:
                    eng.wait_ge(seam_lo_made, 2 * n + c - seam + 1)
                    return
            eng.wait_ge(lo_made, Chunk(c).lo)

        def load(eng, ch, src, looped=False):
            if looped:
                eng.wait_ge(lo_made, ch.lo - 2)
            elif ch.first >= 2:
                wait_split(eng, ch.first - 2)
            k, n = src.shape[1], src.shape[2]
            eng.dma_start(raw[ch.s][:].rearrange("p (k n) -> p k n", k=k), src)\
               .then_inc(raw_landed[ch.s], 16)

        def make_hi(act, ch):
            act.wait_ge(raw_landed[ch.s], 16 * ch.nth + 16)
            if ch.first >= 2:
                act.wait_ge(chunk_used, ch.c - 1)
            act.activation(w_hi[ch.s][:], raw[ch.s][:], ACT.Copy).then_inc(hi_made, 1)

        def make_lo(eng, ch, made=lo_made):
            eng.wait_ge(hi_made, ch.c + 1)
            eng.tensor_tensor(w_lo[ch.s][:], raw[ch.s][:], f32(w_hi[ch.s][:]), ALU.subtract)\
               .then_inc(made, 1)

        def y_bank(q):
            return SIDE_B[q] if q < 4 else (6, 7, 4, 5)[q % 4]

        block = ctx.enter_context(nc.Block())

        @block.sync
        def _(sp):
            def load_glu(p, part):
                col = A0 + 512 * part + 256 * p
                load(sp, Chunk(C_GLU[p] + part), W0[:, :, col:col + 256])

            for t in range(TT):
                sp.dma_start(x_tok[:, t, :], ins["x"][0, t * P:(t + 1) * P, :]).then_inc(x_landed[t], 16)
                if t % 2:
                    load_glu(0, t // 2)
            for dst, src in ((qk_gain[:, 0, :], ins["l0_q_norm_g"].partition_broadcast(P)),
                             (qk_gain[:, 1, :], ins["l0_k_norm_g"].partition_broadcast(P)),
                             (rope0[:], ins["rope0"]),
                             (conv_par[:], ins["conv_par"]),
                             (decay[:], ins["decay"].partition_broadcast(P)),
                             (ret_gain[:], ins["ret_gain"])):
                sp.dma_start(dst, src).then_inc(par_landed, 16)
            load(sp, Chunk(C_KV), W0[:, :, 512:768])
            for j in range(2):
                load(sp, Chunk(C_Q + j), W0[:, 4 * j:4 * j + 4, 0:512])
            for part in range(2):
                load_glu(1, part)
            for j in range(4):
                load(sp, Chunk(C_OUT0 + j), WO0[:, 2 * j:2 * j + 2, :])

            def norm_params(d, name):
                sp.dma_start(ln_gb[:, 0, :], ins[f"{name}_g"].partition_broadcast(P)).then_inc(gb_landed, 16)
                sp.dma_start(ln_gb[:, 1, :], ins[f"{name}_b"].partition_broadcast(P)).then_inc(gb_landed, 16)

            def ffn_loads(layer, c_ffn, c_down):
                for i in range(2):
                    for k, w in enumerate((gate_w[layer], up_w[layer])):
                        load(sp, Chunk(c_ffn + 2 * i + k), w[:, :, i * 256:i * 256 + 256])
                with sp.Fori(2, NH // 2) as i:
                    load(sp, Chunk(c_ffn, i), gate_w[layer][:, :, bass.ds(i * 256, 256)], looped=True)
                    load(sp, Chunk(c_ffn + 1, i), up_w[layer][:, :, bass.ds(i * 256, 256)], looped=True)
                for j in range(NH // 2):
                    if j == 2:
                        sp.wait_ge(x_normed, 8 * (2 * layer + 1))
                        norm_params(2 * layer + 1, f"l{layer}_ln_ffn")
                    load(sp, Chunk(c_down + j), down_w[layer][:, 2 * j:2 * j + 2, :])

            sp.wait_ge(conv_turned, TT)
            norm_params(0, "l0_ln_mix")
            ffn_loads(0, C_FFN0, C_DOWN0)
            for c in range(2):
                load(sp, Chunk(C_RET + c), W1[:, :, D * c:D * c + 256])
            sp.wait_ge(x_normed, 8 * 2)
            sp.dma_start(rope1[:], ins["rope1"]).then_inc(rope1_landed, 16)
            for h in range(RH):
                if h:
                    for c in range(2):
                        load(sp, Chunk(C_RET + c + 6 * h), W1[:, :, D * c + RK * h:D * c + RK * h + 256])
                for c in range(4):
                    col = 2 * D + RH * RV * (c // 2) + RV * h
                    load(sp, Chunk(C_RET + 2 + c + 6 * h), W1[:, 4 * (c % 2):4 * (c % 2) + 4, col:col + RV])
            for j in range(8):
                if j == 2:
                    sp.wait_ge(rot_made, 4 * RH)
                    norm_params(2, "l1_ln_mix")
                kt, col = 4 * (j % 4), N * (j // 4)
                load(sp, Chunk(C_OUT1 + j), WO1[:, kt:kt + 4, col:col + N])
            ffn_loads(1, C_FFN1, C_DOWN1)
            for t in range(TT):
                for half in range(2):
                    sp.wait_ge(x_normed, 8 * 3 + 2 * t + half + 1)
                    sp.dma_start(out[0, t * P:(t + 1) * P, N * half:N * half + N], x_tok[:, t, N * half:N * half + N])\
                        .then_inc(out_landed, 16)
            sp.wait_ge(out_landed, 16 * 2 * TT)

        @block.gpsimd
        def _(pool):
            own = [0]

            def mine(instruction):
                own[0] += 1
                instruction.then_inc(pool_own, 1)
                pool.wait_ge(pool_own, own[0])

            mine(nc.gpsimd.memset(ident[:], 0.0))
            mine(nc.gpsimd.affine_select(out=ident[:], in_=ident[:], compare_op=ALU.not_equal, fill=1.0,
                                         base=0, pattern=[[-1, P]], channel_multiplier=1))
            mine(nc.gpsimd.memset(minus_one[:], -1.0))
            nc.gpsimd.memset(minus_half[:], -0.5).then_inc(consts_made, 1)
            nc.gpsimd.memset(zpad[:], 0.0).then_inc(consts_made, 1)
            for z in (kT_hi, kT_lo):
                nc.gpsimd.memset(f32(z[:]), 0.0).then_inc(consts_made, 1)
            pool.wait_ge(par_landed, 16 * 6)
            for x in range(2):
                for out_half, (a, b) in enumerate(((0, 1), (1, 0))):
                    for in_half, table in enumerate((a, b)):
                        dims = slice(HD // 2 * in_half, HD // 2 * (in_half + 1))
                        nc.gpsimd.tensor_tensor(rope_gain[:, :, x, out_half, dims], rope0[:, :, table, :],
                                                qk_gain[:, x, dims].unsqueeze(1).broadcast_to([P, TT, HD // 2]), ALU.mult)\
                            .then_inc(rope_gain_made, 1)

            added = [0]

            def add_taps(count):
                for a in range(added[0], min(added[0] + count, ADDED)):
                    own_tile = a < TAPS - 1
                    total = acc[:, 1, :] if own_tile else side_sum[:]
                    pool.wait_ge(part_tapped, a + (2 if own_tile else 3))
                    if a:
                        pool.wait_ge(part_added, a)
                    nc.gpsimd.tensor_tensor(total, total, tap_part[:, a % 4, :], ALU.add).then_inc(part_added, 1)
                    added[0] += 1

            add_taps(6)
            for t in range(TT):
                pool.wait_ge(k_ms_made, t + 1)
                mine(nc.gpsimd.tensor_tensor(k_rstd[:, t, :], k_ms[:, t, :], minus_half[:, 0:KV], ALU.pow))
                pool.wait_ge(k_turn_made, 2 * t + 2)
                for copy in range(2):
                    nc.gpsimd.tensor_tensor(k_roped[:, t, :, copy, :], k_turned[:, t, :].rearrange("p (h d) -> p h d", d=HD),
                                            k_rstd[:, t, :].unsqueeze(2).broadcast_to([P, KV, HD]), ALU.mult)\
                        .then_inc(k_roped_made, 1)
            add_taps(20)
            for t in range(TT):
                pool.wait_ge(q_ms_made, t + 1)
                nc.gpsimd.tensor_tensor(q_scale[:, t, :], q_ms[:, t, :], minus_half[:, 0:HEADS], ALU.pow)\
                    .then_inc(q_scale_made, 1)
            add_taps(TAPS - 1 - added[0])

            def diagonals(b):
                first = BATCH * b
                if b >= 2:
                    pool.wait_ge(diag_lo_made, b - 1)
                nc.gpsimd.tensor_tensor(diag[:, b % 2, 0:BATCH, :], ident[:].unsqueeze(1).broadcast_to([P, BATCH, P]),
                                        conv_par[:, 3, first:first + BATCH].unsqueeze(2).broadcast_to([P, BATCH, P]),
                                        ALU.mult).then_inc(diag_made, 1)

            for b in range(2):
                diagonals(b)

            def attention_step(s):
                b = s // 2
                if s % 2:
                    add_taps(1)
                if s == SIDE_SUM_STEP:
                    pool.wait_ge(tap_done, 2 * TAPS - HANDED)
                    pool.wait_ge(part_added, ADDED)
                    nc.gpsimd.tensor_tensor(acc[:, 2, :], acc[:, 2, :], side_sum[:], ALU.add).then_inc(part_added, 1)
                if s % 2 == 0 and b < BATCHES:
                    pool.wait_ge(diag_hi_made, b + 1)
                    nc.gpsimd.tensor_tensor(diag_lo[:, b % 2, 0:BATCH, :], diag[:, b % 2, 0:BATCH, :],
                                            f32(diag_hi[:, b % 2, 0:BATCH, :]), ALU.subtract).then_inc(diag_lo_made, 1)
                    if b + 2 < BATCHES:
                        diagonals(b + 2)
                if s >= 8 and s % GROUP == 0:
                    divide_outputs(s // GROUP - 2)
                if s in CONV_TO_TOKENS:
                    conv_rsqrt(CONV_TO_TOKENS.index(s))
                if s in OUT0_SPLIT_STEPS:
                    make_lo(pool, Chunk(C_OUT0 + OUT0_SPLIT_STEPS.index(s)), seam_lo_made)

            def conv_rsqrt(t):
                pool.wait_ge(conv_var, t + 1)
                nc.gpsimd.tensor_tensor(rstd[:, t:t + 1], var_eps[:, t:t + 1], minus_half[:, 0:1], ALU.pow)\
                    .then_inc(conv_rstd, 1)

            def divide_outputs(n):
                t, steps = n // 2, slice(GROUP * n, GROUP * (n + 1))
                pool.wait_ge(o_copied, n + 1)
                if t >= 2 and n % 2 == 0:
                    pool.wait_ge(o_turned, t - 1)
                o = o_tok[:, t % 2, GROUP * HD * (n % 2):GROUP * HD * (n % 2 + 1)].rearrange("p (h d) -> p h d", d=HD)
                mine(nc.gpsimd.tensor_tensor(row_inv[:, steps], row_sum[:, steps], minus_one[:], ALU.pow))
                mine(nc.gpsimd.tensor_tensor(o, o_raw[n % 2][:, :, 0, :], o_raw[n % 2][:, :, 1, :], ALU.add))
                nc.gpsimd.tensor_tensor(o, o, row_inv[:, steps].unsqueeze(2).broadcast_to([P, GROUP, HD]), ALU.mult)\
                    .then_inc(o_divided, 1)

            for s in range(STEPS):
                attention_step(s)
            for n in (STEPS // GROUP - 2, STEPS // GROUP - 1):
                divide_outputs(n)

            def norm_rstd(d, t):
                pool.wait_ge(var_made, 4 * d + t + 1)
                mine(nc.gpsimd.tensor_scalar(var_eps[:, t:t + 1], var_eps[:, t:t + 1], LN_EPS, None, ALU.add))
                nc.gpsimd.tensor_tensor(rstd[:, t:t + 1], var_eps[:, t:t + 1], minus_half[:, 0:1], ALU.pow)\
                    .then_inc(rstd_made, 1)

            def seam(d, c):
                norm_rstd(d, 0)
                norm_rstd(d, 1)
                make_lo(pool, Chunk(c), seam_lo_made)
                norm_rstd(d, 2)
                make_lo(pool, Chunk(c + 1), seam_lo_made)
                norm_rstd(d, 3)

            seam(0, C_FFN0)
            seam(1, C_RET)
            pool.wait_ge(x_normed, 8 * 2)
            mine(nc.gpsimd.iota(mask[:], pattern=[[1, SPAN]], base=-(SEQ - P), channel_multiplier=-1,
                                allow_small_or_imprecise_dtypes=True))
            mine(nc.gpsimd.tensor_scalar(ahead[:], mask[:], 0.0, None, ALU.max))
            mine(nc.gpsimd.tensor_tensor(behind[:], ahead[:], mask[:], ALU.subtract))
            base = own[0]
            with pool.Fori(0, RH) as h:
                pool.wait_ge(ret_masked, 4 * h + FREE)
                nc.gpsimd.tensor_tensor(mask[:], ahead[:], decay[:, 0, bass.ds(h, 1)].broadcast_to([P, SPAN]), ALU.mult)\
                    .then_inc(pool_own, 1)
                nc.gpsimd.tensor_tensor(mask_b[:], behind[:], decay[:, 1, bass.ds(h, 1)].broadcast_to([P, SPAN]), ALU.mult)\
                    .then_inc(pool_own, 1)
                pool.wait_ge(pool_own, base + 2 * h + 2)
                nc.gpsimd.tensor_tensor(mask[:], mask[:], mask_b[:], ALU.add).then_inc(exponent_made, 1)
                for t in range(TT):
                    pool.wait_ge(o_var, 4 * h + t + 1)
                    nc.gpsimd.tensor_tensor(rstd[:, t:t + 1], var_eps[:, t:t + 1], minus_half[:, 0:1], ALU.pow)\
                        .then_inc(o_rstd, 1)
            own[0] = base + 2 * RH
            seam(2, C_FFN1)
            for t in range(TT):
                norm_rstd(3, t)

        @block.scalar
        def _(act):
            def xT_tile_hi(stage, t):
                for half in range(2):
                    n = 8 * stage + 2 * t + half
                    act.wait_ge(turned, n + 1)
                    nc.scalar.activation(xT_hi[:, 4 * half:4 * half + 4, t * P:(t + 1) * P],
                                         ps[:, t + 4 * half, :].rearrange("p (k c) -> p k c", c=P), ACT.Copy)\
                        .then_inc(xT_hi_made, 1)

            act.preload_act_table(ACT.Sigmoid)
            for t in range(TT):
                xT_tile_hi(0, t)
                if t % 2:
                    make_hi(act, Chunk(t // 2))
            tapped = [0]

            def tap_products(count):
                for n in range(tapped[0], min(tapped[0] + count, TAPS + HANDED)):
                    ct, k = (1, n) if n < TAPS else (2, n - HANDED)
                    tap, z = conv_par[:, ct, k:k + 1], zpad[:, ct, k:k + SEQ]
                    if n == 0:
                        act.wait_ge(par_landed, 16 * 6)
                        act.wait_ge(z_made, 2)
                        nc.scalar.activation(acc[:, 1, :], z, ACT.Identity, scale=tap,
                                             bias=conv_par[:, 1, TAPS:TAPS + 1]).then_inc(part_tapped, 1)
                    elif n == TAPS:
                        nc.scalar.activation(side_sum[:], z, ACT.Copy, scale=tap).then_inc(part_tapped, 1)
                    else:
                        a = n - 1 if n < TAPS else n - 2
                        if a >= 4:
                            act.wait_ge(part_added, a - 3)
                        nc.scalar.activation(tap_part[:, a % 4, :], z, ACT.Copy, scale=tap).then_inc(part_tapped, 1)
                    tapped[0] += 1

            def glu_sigmoids(p):
                for m in range(2):
                    ct = 2 * p + m
                    if p == 0:
                        make_hi(act, Chunk(C_KV + m))
                    if m == 0:
                        act.wait_ge(part_made, PM_GLU[p] + 2)
                    else:
                        act.wait_ge(chunk_used, C_GLU[p] + 2)
                    nc.scalar.activation(tmp[3 - m][:], ps[:, (SIDE_B if p else SIDE_A)[2 + m], :], ACT.Sigmoid)\
                        .then_inc(sig_made, 1)

            def q_tile_hi(t):
                act.wait_ge(q_in_psum, t + 1)
                nc.scalar.activation(qT_hi[:, t, :, :], ps[:, SIDE_A[t], :].rearrange("p (j c) -> p j c", c=P), ACT.Copy)\
                    .then_inc(qT_hi_made, 1)

            glu_sigmoids(0)
            tap_products(7)
            make_hi(act, Chunk(C_Q + 1))
            for t in range(TT):
                act.wait_ge(part_made, PM_KV + t + 1) if t < TT - 1 else act.wait_ge(chunk_used, C_KV + 1)
                nc.scalar.activation(k_sq[:, t, :], ps[:, SIDE_B[t], 0:KV * HD], ACT.Square).then_inc(k_sq_made, 1)
                nc.scalar.activation(v_parts[:, t, :, 0, :], ps[:, SIDE_B[t], KV * HD:2 * KV * HD].rearrange("p (g d) -> p g d", d=HD),
                                     ACT.Copy).then_inc(v_hi_made, 1)
            tap_products(6)
            make_hi(act, Chunk(C_GLU[1]))
            act.wait_ge(consts_made, 4)
            for g in range(KV):
                act.wait_ge(k_in_psum, g + 1)
                for side in range(2):
                    rows = slice(HD * side, HD * side + HD)
                    nc.scalar.activation(kT_hi[rows, g, side, :], ps[rows, K_BANKS[g], :], ACT.Copy).then_inc(kT_hi_made, 1)
            tap_products(6)
            for t in range(TT):
                act.wait_ge(part_made, PM_Q + t + 1) if t < TT - 1 else act.wait_ge(chunk_used, C_Q + 2)
                nc.scalar.activation(q_sq[:, t, :], ps[:, SIDE_A[t], :], ACT.Square).then_inc(q_sq_made, 1)
                if t == 0:
                    make_hi(act, Chunk(C_GLU[1] + 1))
            tap_products(3)
            tap_products(5)
            for t in range(2):
                q_tile_hi(t)
            tap_products(TAPS - tapped[0])
            for t in range(2, TT):
                q_tile_hi(t)
            glu_sigmoids(1)
            act.preload_act_table(ACT.Exp)
            def z_tile_hi():
                act.wait_ge(z_made, 4)
                nc.scalar.activation(z_hi[:], zpad[:, 3, :], ACT.Copy).then_inc(z_hi_made, 1)

            def attention_step(s):
                if s < STEPS:
                    t, h = s // HEADS, s % HEADS
                    act.wait_ge(max_made, s + 1)
                    if s >= 3:
                        act.wait_ge(prob_turned, s - 2)
                    nc.scalar.activation(tmp[s % 3][:], ps[:, SCORE_BANKS[s % 2], :], ACT.Exp, bias=neg_max[:, s:s + 1],
                                         scale=q_scale[:, t, h:h + 1], accum_out=row_sum[:, s:s + 1]).then_inc(exp_made, 1)
                if s == 0:
                    z_tile_hi()
                if s % 2 == 0:
                    tap_products(1)
                u = s - 2
                if 0 <= u < STEPS:
                    act.wait_ge(prob_turned, u + 1)
                    if u >= 3:
                        act.wait_ge(head_done, u - 2)
                    nc.scalar.activation(probT_hi[:, u % 3, :], ps[:, TURN_BANKS[u % 2], :], ACT.Copy)\
                        .then_inc(probT_hi_made, 1)
                b = s // 2
                if s % 2 == 0 and b < BATCHES:
                    act.wait_ge(diag_made, b + 1)
                    if b >= 2:
                        act.wait_ge(diag_used, b - 1)
                    nc.scalar.activation(diag_hi[:, b % 2, 0:BATCH, :], diag[:, b % 2, 0:BATCH, :], ACT.Copy)\
                        .then_inc(diag_hi_made, 1)
                if s == 2 * BATCHES + 3:
                    act.wait_ge(diag_used, BATCHES)
                    nc.scalar.activation(acc[:, 3, :], ps[:, CONV_BANK, :], ACT.Identity, bias=conv_par[:, 3, TAPS:TAPS + 1])\
                        .then_inc(conv_copied, 1)
                if s + 1 in OUT0_SPLIT_STEPS:
                    make_hi(act, Chunk(C_OUT0 + OUT0_SPLIT_STEPS.index(s + 1)))
                if s >= 8 and s % GROUP == 0:
                    copy_outputs(s // GROUP - 2)
                if s in OUT_TO_FEATURES:
                    output_hi(OUT_TO_FEATURES.index(s))

            def copy_outputs(n):
                act.wait_ge(head_done, GROUP * (n + 1))
                if n >= 2:
                    act.wait_ge(o_divided, n - 1)
                nc.scalar.activation(o_raw[n % 2][:], ps[:, OUT_BANKS[n % 2], :].rearrange("p (h c d) -> p h c d", c=2, d=HD),
                                     ACT.Copy).then_inc(o_copied, 1)

            def output_hi(t):
                act.wait_ge(o_turned, t + 1)
                nc.scalar.activation(catT_hi[:, 0:4, t * P:(t + 1) * P], ps[:, SPARE, :].rearrange("p (j c) -> p j c", c=P),
                                     ACT.Copy).then_inc(att_hi_made, 1)

            for s in range(LAST_STEP):
                attention_step(s)
            act.preload_act_table(ACT.Silu)
            for ct in range(CT):
                act.wait_ge(conv_back, ct + 1)
                nc.scalar.activation(swished[:, ct, :], ps[:, BACK_BANKS[ct], :], ACT.Silu,
                                     bias=conv_par[:, ct, TAPS + 2:TAPS + 3],
                                     scale=conv_par[:, ct, TAPS + 1:TAPS + 2]).then_inc(silu_made, 1)
                if ct == 0:
                    copy_outputs(STEPS // GROUP - 1)
            for ct in range(CT):
                act.wait_ge(silu_made, ct + 1)
                nc.scalar.activation(catT_hi[:, 4 + ct, :], swished[:, ct, :], ACT.Copy).then_inc(swish_hi_made, 1)
            output_hi(TT - 1)

            def variance(d, t):
                act.wait_ge(mean_made, 4 * d + t + 1)
                nc.scalar.activation(squares[:], x_tok[:, t, :], ACT.Square, bias=minus_mean[:, t:t + 1], scale=D ** -0.5,
                                     accum_out=var_eps[:, t:t + 1]).then_inc(var_made, 1)
                act.wait_ge(var_made, 4 * d + t + 1)

            def seam(d, c):
                variance(d, 0)
                variance(d, 1)
                make_hi(act, Chunk(c))
                xT_tile_hi(d + 1, 0)
                xT_tile_hi(d + 1, 1)
                variance(d, 2)
                make_hi(act, Chunk(c + 1))
                variance(d, 3)
                xT_tile_hi(d + 1, 2)
                xT_tile_hi(d + 1, 3)

            def swiglu(layer, c_ffn, c_down, pm):
                g0, f0 = NH * layer, (NH + 2) * layer
                with act.Fori(0, NH // 2) as i:
                    for m in range(2):
                        if m == 0:
                            act.wait_ge(part_made, pm + 2 * i + 1)
                        else:
                            make_hi(act, Chunk(c_ffn + 2, i))
                            act.wait_ge(chunk_used, c_ffn + 2 * i + 1)
                        act.wait_ge(up_read, f0 + 2 * i + m + 1)
                        nc.scalar.activation(tmp[m][:], ps[:, m, :], ACT.Silu).then_inc(gate_read, 1)
                    for m in range(2):
                        act.wait_ge(up_read, f0 + 2 * i + m + 3)
                        nc.scalar.activation(hT_hi[:, bass.ds(2 * i + m, 1), :], tmp[2 + m][:].unsqueeze(1), ACT.Copy)\
                            .then_inc(h_hi_made, 1)
                    make_hi(act, Chunk(c_ffn + 3, i))
                for j in range(NH // 2 - 2):
                    make_hi(act, Chunk(c_down + j + 2))

            for j in range(2):
                make_hi(act, Chunk(C_OUT0 + 2 + j))
            act.sem_inc(gate_read, 2)
            seam(0, C_FFN0)
            swiglu(0, C_FFN0, C_DOWN0, PM_FFN0)
            act.sem_inc(g_read, FREE)
            seam(1, C_RET)
            def y_tile_hi(q):
                act.wait_ge(y_turned, q + 1)
                nc.scalar.activation(yT_hi[q][:], ps[:, y_bank(q), :], ACT.Copy, scale=ret_gain[:, q:q + 1]).then_inc(yT_hi_made, 1)

            def head(h, between=lambda: None):
                make_hi(act, Chunk(C_RET + 2, h, 6))
                for x, dst in ((0, rq_hi), (1, rk_hi)):
                    for half in range(2):
                        act.wait_ge(rot_made, 4 * h + 2 * x + half + 1)
                        nc.scalar.activation(dst[:, half, :], tmp[2 + half][:], ACT.Copy).then_inc(rot_hi, 1)
                    if x == 0:
                        make_hi(act, Chunk(C_RET + 3, h, 6))
                act.wait_ge(exponent_made, h + 1)
                nc.scalar.activation(mask[:], mask[:], ACT.Exp).then_inc(mask_made, 1)
                make_hi(act, Chunk(C_RET + 4, h, 6))
                for t in range(TT):
                    if t < TT - 1:
                        act.wait_ge(part_made, PM_RET + 8 * h + 2 + t + 1)
                    else:
                        act.wait_ge(chunk_used, C_RET + 6 * h + 4)
                    nc.scalar.activation(rv_hi[:, t, :], ps[:, SIDE_B[t], :], ACT.Copy).then_inc(rv_hi_made, 1)
                make_hi(act, Chunk(C_RET + 5, h, 6))
                for kt in range(TT):
                    act.wait_ge(ret_masked, 4 * h + kt + 1 + FREE)
                    if kt >= 2:
                        act.wait_ge(sT_used, 3 * h + kt - 1)
                    nc.scalar.activation(sT_hi[:, kt % 2, :], tmp[kt % 2][:], ACT.Copy).then_inc(sT_hi_made, 1)
                make_hi(act, Chunk(C_RET + 6, h, 6))
                between()
                for t in range(TT):
                    if t < TT - 1:
                        act.wait_ge(part_made, PM_RET + 8 * h + 5 + t + 1)
                    else:
                        act.wait_ge(chunk_used, C_RET + 6 * h + 6)
                    if t >= 2:
                        act.wait_ge(y_made, 4 * h + t - 1)
                    else:
                        act.wait_ge(rot_lo, 4 * h + 4)
                    nc.scalar.activation(tmp[2 + t % 2][:], ps[:, SIDE_A[t], :], ACT.Silu).then_inc(g_read, 1)

            with act.Fori(0, RH - 1) as h:
                head(h)
                make_hi(act, Chunk(C_RET + 7, h, 6))
            head(RH - 1, lambda: [y_tile_hi(q) for q in range(4)])
            make_hi(act, Chunk(C_OUT1 + 1))

            for q in range(4, RH * TT):
                y_tile_hi(q)
                if q in (7, 11, 15):
                    make_hi(act, Chunk(C_OUT1 + (q + 1) // 4))
            for j in range(5, 8):
                make_hi(act, Chunk(C_OUT1 + j))
            act.sem_inc(gate_read, 2)
            seam(2, C_FFN1)
            swiglu(1, C_FFN1, C_DOWN1, PM_FFN1)
            for t in range(TT):
                variance(3, t)

        @block.vector
        def _(dve):
            class Own:
                n, per_turn, turn = 0, 0, 0

                def value(self):
                    return self.n + self.per_turn * self.turn if self.per_turn else self.n

            own = Own()

            def mine(instruction, wait=True):
                instruction.then_inc(dve_own, 1)
                own.n += 1
                if wait:
                    dve.wait_ge(dve_own, own.value())

            def xT_tile_lo(stage, t):
                for half in range(2):
                    n = 8 * stage + 2 * t + half
                    dve.wait_ge(xT_hi_made, n + 1)
                    spot = (slice(None), slice(4 * half, 4 * half + 4), slice(t * P, (t + 1) * P))
                    nc.vector.tensor_tensor(xT_lo[spot], ps[:, t + 4 * half, :].rearrange("p (k c) -> p k c", c=P),
                                            f32(xT_hi[spot]), ALU.subtract).then_inc(xT_lo_made, 1)

            taps = [(0, k) for k in range(TAPS)] + [(2, k) for k in range(TAPS - HANDED)] \
                + [(3, k) for k in range(BATCH * BATCHES, TAPS)]
            tapped = [0]

            def conv(count):
                for ct, k in taps[tapped[0]:tapped[0] + count]:
                    if k == 0:
                        dve.wait_ge(par_landed, 16 * 6)
                        dve.wait_ge(z_made, ct + 1)
                        nc.vector.tensor_scalar(acc[:, ct, :], zpad[:, ct, k:k + SEQ], conv_par[:, ct, k:k + 1],
                                                conv_par[:, ct, TAPS:TAPS + 1], ALU.mult, ALU.add).then_inc(tap_done, 1)
                    else:
                        if (ct, k) == (3, BATCH * BATCHES):
                            dve.wait_ge(conv_copied, 1)
                        dve.wait_ge(tap_done, tapped[0])
                        nc.vector.scalar_tensor_tensor(acc[:, ct, :], zpad[:, ct, k:k + SEQ], conv_par[:, ct, k:k + 1],
                                                       acc[:, ct, :], ALU.mult, ALU.add).then_inc(tap_done, 1)
                    tapped[0] += 1

            for t in range(TT):
                xT_tile_lo(0, t)
                if t % 2:
                    make_lo(dve, Chunk(t // 2))

            def glu_products(p):
                for m in range(2):
                    ct = 2 * p + m
                    if p == 0:
                        make_lo(dve, Chunk(C_KV + m))
                    dve.wait_ge(sig_made, ct + 1)
                    nc.vector.tensor_tensor(zpad[:, ct, PAD:PAD + SEQ], tmp[3 - m][:], ps[:, (SIDE_B if p else SIDE_A)[m], :],
                                            ALU.mult).then_inc(z_made, 1)

            dve.wait_ge(consts_made, 2)
            def v_tile_lo(t):
                dve.wait_ge(v_hi_made, t + 1)
                nc.vector.tensor_tensor(v_parts[:, t, :, 1, :], ps[:, SIDE_B[t], KV * HD:2 * KV * HD].rearrange("p (g d) -> p g d", d=HD),
                                        f32(v_parts[:, t, :, 0, :]), ALU.subtract).then_inc(v_lo_made, 1)

            def rope_tile(t, x, bank, heads, out, made):
                src = ps[:, bank, 0:heads * HD].rearrange("p (h d) -> p h d", d=HD)
                turned_halves = []
                for half in range(2):
                    dst = tmp[half][:, 0:heads * HD].rearrange("p (h d) -> p h d", d=HD)
                    mine(nc.vector.tensor_tensor(dst, src, rope_gain[:, t, x, half, :].unsqueeze(1).broadcast_to([P, heads, HD]),
                                                 ALU.mult), wait=half == 1)
                    turned_halves.append(dst.rearrange("p h (s d) -> p h s d", s=2))
                out = out.rearrange("p (h s d) -> p h s d", s=2, d=HD // 2)
                for half, op in ((0, ALU.subtract), (1, ALU.add)):
                    u = turned_halves[half]
                    nc.vector.tensor_tensor(out[:, :, half, :], u[:, :, 0, :], u[:, :, 1, :], op).then_inc(made, 1)
                dve.wait_ge(made, 2 * t + 2)

            def q_tile_lo(t):
                dve.wait_ge(qT_hi_made, t + 1)
                nc.vector.tensor_tensor(qT_lo[:, t, :, :], ps[:, SIDE_A[t], :].rearrange("p (j c) -> p j c", c=P),
                                        f32(qT_hi[:, t, :, :]), ALU.subtract).then_inc(qT_lo_made, 1)

            glu_products(0)
            conv(10)
            make_lo(dve, Chunk(C_Q + 1))
            dve.wait_ge(rope_gain_made, 8)
            for t in range(TT):
                dve.wait_ge(k_sq_made, t + 1)
                mine(nc.vector.tensor_reduce(k_ms[:, t, :], k_sq[:, t, :].rearrange("p (h d) -> p h d", d=HD), AX.X, ALU.add))
                nc.vector.tensor_scalar(k_ms[:, t, :], k_ms[:, t, :], 1.0 / HD, RMS_EPS, ALU.mult, ALU.add)\
                    .then_inc(k_ms_made, 1)
                v_tile_lo(t)
                rope_tile(t, 1, SIDE_B[t], KV, k_turned[:, t, :], k_turn_made)
            conv(4)
            make_lo(dve, Chunk(C_GLU[1]))
            for g in range(KV):
                for side in range(2):
                    rows = slice(HD * side, HD * side + HD)
                    dve.wait_ge(kT_hi_made, 2 * g + side + 1)
                    nc.vector.tensor_tensor(kT_lo[rows, g, side, :], ps[rows, K_BANKS[g], :], f32(kT_hi[rows, g, side, :]),
                                            ALU.subtract).then_inc(kT_lo_made, 1)
            conv(7)
            for t in range(TT):
                dve.wait_ge(q_sq_made, t + 1)
                rope_tile(t, 0, SIDE_A[t], HEADS, q_roped[:, t, :], q_roped_made)
                mine(nc.vector.tensor_reduce(q_ms[:, t, :], q_sq[:, t, :].rearrange("p (h d) -> p h d", d=HD), AX.X, ALU.add))
                nc.vector.tensor_scalar(q_ms[:, t, :], q_ms[:, t, :], HD * RMS_EPS, None, ALU.add).then_inc(q_ms_made, 1)
                if t == 0:
                    make_lo(dve, Chunk(C_GLU[1] + 1))
            q_tile_lo(0)
            q_tile_lo(1)
            conv(4)
            q_tile_lo(2)
            q_tile_lo(3)

            def row_maximum(s):
                t, h = s // HEADS, s % HEADS
                if h == 0:
                    dve.wait_ge(q_scale_made, t + 1)
                dve.wait_ge(scores_made, s + 1)
                mine(nc.vector.tensor_reduce(row_max[:, s:s + 1], ps[:, SCORE_BANKS[s % 2], :], AX.X, ALU.max))
                nc.vector.tensor_scalar(neg_max[:, s:s + 1], row_max[:, s:s + 1], q_scale[:, t, h:h + 1], -1.0,
                                        ALU.mult, ALU.mult).then_inc(max_made, 1)

            row_maximum(0)
            row_maximum(1)
            glu_products(1)

            def attention_step(s):
                if 2 <= s < STEPS:
                    row_maximum(s)
                if s == 1:
                    dve.wait_ge(z_hi_made, 1)
                    nc.vector.tensor_tensor(z_lo[:], zpad[:, 3, :], f32(z_hi[:]), ALU.subtract).then_inc(z_lo_made, 1)
                u = s - 3
                if 0 <= u < STEPS:
                    dve.wait_ge(probT_hi_made, u + 1)
                    nc.vector.tensor_tensor(probT_lo[:, u % 3, :], ps[:, TURN_BANKS[u % 2], :], f32(probT_hi[:, u % 3, :]),
                                            ALU.subtract).then_inc(probT_lo_made, 1)
                conv(2 - s % 2)
                if s in CONV_TO_TOKENS:
                    t = CONV_TO_TOKENS.index(s)
                    dve.wait_ge(conv_turned, t + 1)
                    variance(t, [ps[:, CONV_BANK, :]], conv_var, LN_EPS)
                if s - 1 in CONV_TO_TOKENS:
                    t = CONV_TO_TOKENS.index(s - 1)
                    dve.wait_ge(conv_rstd, t + 1)
                    nc.vector.tensor_scalar(conv_norm[:, t, :], ps[:, CONV_BANK, :], moments[:, t, 0:1], rstd[:, t:t + 1],
                                            ALU.subtract, ALU.mult).then_inc(conv_normed, 1)
                if s in OUT_TO_FEATURES:
                    output_lo(OUT_TO_FEATURES.index(s))

            def variance(t, halves, made, eps):
                for i, x in enumerate(halves):
                    mine(nc.vector.bn_stats(stats[:, t, i, :], x), wait=(i == len(halves) - 1))
                if own.per_turn:
                    dve.sem_inc(stats_seen, 1)
                mine(nc.vector.bn_aggr(moments[:, t, :], stats[:, t, 0:len(halves), :]))
                nc.vector.tensor_scalar(var_eps[:, t:t + 1], moments[:, t, 1:2], eps, None, ALU.add).then_inc(made, 1)

            def output_lo(t):
                dve.wait_ge(att_hi_made, t + 1)
                nc.vector.tensor_tensor(catT_lo[:, 0:4, t * P:(t + 1) * P], ps[:, SPARE, :].rearrange("p (j c) -> p j c", c=P),
                                        f32(catT_hi[:, 0:4, t * P:(t + 1) * P]), ALU.subtract).then_inc(att_lo_made, 1)

            for s in range(LAST_STEP):
                attention_step(s)
            for ct in range(CT):
                dve.wait_ge(swish_hi_made, ct + 1)
                nc.vector.tensor_tensor(catT_lo[:, 4 + ct, :], swished[:, ct, :], f32(catT_hi[:, 4 + ct, :]), ALU.subtract)\
                    .then_inc(swish_lo_made, 1)
            output_lo(TT - 1)
            for j in range(2):
                make_lo(dve, Chunk(C_OUT0 + 2 + j))

            def add_residual(t, half, made=None):
                cols = slice(N * half, N * half + N)
                added = nc.vector.scalar_tensor_tensor(x_tok[:, t, cols], x_tok[:, t, cols], ALPHA, ps[:, t + 4 * half, :],
                                                       ALU.mult, ALU.add, accum_out=x_sum[:, t, half:half + 1])
                if made is not None:
                    added.then_inc(made, 1)
                else:
                    mine(added, wait=(half == 1))

            def layer_norm(d, tile_sums, halves=(0, 1), turn=True):
                def centre(t):
                    if turn and t == 2:
                        xT_tile_lo(d + 1, 0)
                    tile_sums(t)
                    for half in halves:
                        add_residual(t, half)
                    sums = x_sum[:, t, 0:1], x_sum[:, t, 1:2]
                    nc.vector.tensor_scalar(minus_mean[:, t:t + 1], *sums, -D ** -1.5, ALU.add, ALU.mult).then_inc(mean_made, 1)
                    mine(nc.vector.tensor_scalar(x_mean[:, t:t + 1], *sums, 1 / D, ALU.add, ALU.mult))
                    if turn and t == 2:
                        xT_tile_lo(d + 1, 1)
                    if t == 0:
                        dve.wait_ge(gb_landed, 32 * (d + 1))
                    for half in range(2):
                        cols = slice(N * half, N * half + N)
                        mine(nc.vector.scalar_tensor_tensor(ps[:, t + 4 * half, :], x_tok[:, t, cols], x_mean[:, t:t + 1],
                                                            ln_gb[:, 0, cols], ALU.subtract, ALU.mult), wait=(half == 1))

                def scale(t):
                    dve.wait_ge(rstd_made, 4 * d + t + 1)
                    for half in range(2):
                        cols = slice(N * half, N * half + N)
                        nc.vector.scalar_tensor_tensor(x_tok[:, t, cols], ps[:, t + 4 * half, :], rstd[:, t:t + 1],
                                                       ln_gb[:, 1, cols], ALU.mult, ALU.add).then_inc(x_normed, 1)

                for step, t in ((centre, 0), (scale, 0), (centre, 1), (scale, 1)) if turn else \
                        ((centre, 0), (centre, 1), (scale, 0), (scale, 1)):
                    step(t)
                for t in range(2, TT):
                    centre(t)
                    scale(t)
                if turn:
                    for t in range(TT - 2, TT):
                        xT_tile_lo(d + 1, t)

            def sums(pm, c_last):
                def wait(t):
                    dve.wait_ge(part_made, pm + t + 1) if t < TT - 1 else dve.wait_ge(chunk_used, c_last + 1)
                return wait

            def swiglu(layer, c_ffn, c_down, pm):
                h0, f0 = NH * layer, (NH + 2) * layer
                with dve.Fori(0, NH // 2) as i:
                    make_lo(dve, Chunk(c_ffn + 2, i))
                    for m in range(2):
                        if m == 0:
                            dve.wait_ge(part_made, pm + 2 * i + 2)
                        else:
                            dve.wait_ge(chunk_used, c_ffn + 2 * i + 2)
                        dve.wait_ge(gate_read, f0 + 2 * i + m + 3)
                        nc.vector.tensor_tensor(tmp[2 + m][:], tmp[m][:], ps[:, SIDE_A[2 + m], :], ALU.mult)\
                            .then_inc(up_read, 1)
                        dve.wait_ge(h_hi_made, h0 + 2 * i + m + 1)
                        nc.vector.tensor_tensor(hT_lo[:, bass.ds(2 * i + m, 1), :], tmp[2 + m][:].unsqueeze(1),
                                                f32(hT_hi[:, bass.ds(2 * i + m, 1), :]), ALU.subtract)\
                            .then_inc(h_lo_made, 1)
                    make_lo(dve, Chunk(c_ffn + 3, i))
                for j in range(NH // 2 - 2):
                    make_lo(dve, Chunk(c_down + j + 2))

            dve.sem_inc(up_read, 2)
            layer_norm(0, sums(PM_OUT0, C_FFN0 - 1))
            swiglu(0, C_FFN0, C_DOWN0, PM_FFN0)
            layer_norm(1, sums(PM_DOWN0, C_RET - 1))

            dve.sem_inc(ret_masked, FREE)
            dve.sem_inc(o_normed, FREE)
            dve.wait_ge(rope1_landed, 16)
            start = own.n

            def y_tile_lo(q):
                dve.wait_ge(yT_hi_made, q + 1)
                nc.vector.scalar_tensor_tensor(yT_lo[q][:], ps[:, y_bank(q), :], ret_gain[:, q:q + 1], f32(yT_hi[q][:]),
                                               ALU.mult, ALU.subtract).then_inc(yT_lo_made, 1)

            def head(h, between=lambda: None):
                own.n, own.per_turn, own.turn = start, OWN_PER_HEAD, h
                cos, sin = rope1[:, 0, :], rope1[:, 1, :]
                for x, hi, lo in ((0, rq_hi, rq_lo), (1, rk_hi, rk_lo)):
                    make_lo(dve, Chunk(C_RET + 2 + x, h, 6))
                    dve.wait_ge(chunk_used, C_RET + 6 * h + x + 1)
                    x1, x2 = ps[:, SIDE_A[2 * x], :], ps[:, SIDE_A[2 * x + 1], :]
                    for half, op in ((0, ALU.subtract), (1, ALU.add)):
                        mine(nc.vector.tensor_tensor(tmp[0][:], (cos, sin)[half], x1, ALU.mult), wait=False)
                        mine(nc.vector.tensor_tensor(tmp[1][:], (sin, cos)[half], x2, ALU.mult))
                        nc.vector.tensor_tensor(tmp[2 + half][:], tmp[0][:], tmp[1][:], op).then_inc(rot_made, 1)
                        dve.wait_ge(rot_made, 4 * h + 2 * x + half + 1)
                    for half in range(2):
                        dve.wait_ge(rot_hi, 4 * h + 2 * x + half + 1)
                        nc.vector.tensor_tensor(lo[:, half, :], tmp[2 + half][:], f32(hi[:, half, :]), ALU.subtract)\
                            .then_inc(rot_lo, 1)
                make_lo(dve, Chunk(C_RET + 4, h, 6))
                for t in range(TT):
                    dve.wait_ge(rv_hi_made, 4 * h + t + 1)
                    nc.vector.tensor_tensor(rv_lo[:, t, :], ps[:, SIDE_B[t], :], f32(rv_hi[:, t, :]), ALU.subtract)\
                        .then_inc(rv_lo_made, 1)

                def masked(kt):
                    dve.wait_ge(ret_scored, 4 * h + kt + 1)
                    if kt == 0:
                        dve.wait_ge(mask_made, h + 1)
                    if kt >= 2:
                        dve.wait_ge(sT_lo_made, 4 * h + kt - 1)
                    left = (SEQ - P) - P * kt
                    nc.vector.scalar_tensor_tensor(tmp[kt % 2][:], ps[:, SIDE_A[kt], :], RK ** -0.5, mask[:, left:left + SEQ],
                                                   ALU.mult, ALU.mult).then_inc(ret_masked, 1)

                def masked_lo(kt):
                    dve.wait_ge(sT_hi_made, 4 * h + kt + 1)
                    nc.vector.tensor_tensor(sT_lo[:, kt % 2, :], tmp[kt % 2][:], f32(sT_hi[:, kt % 2, :]), ALU.subtract)\
                        .then_inc(sT_lo_made, 1)

                masked(0)
                for kt in range(1, TT):
                    masked(kt)
                    masked_lo(kt - 1)
                masked_lo(TT - 1)
                make_lo(dve, Chunk(C_RET + 5, h, 6))
                for t in range(TT):
                    dve.wait_ge(o_made, 4 * h + t + 1)
                    variance(t, [ps[:, SIDE_B[t], :]], o_var, LN_EPS)
                for t in range(TT):
                    dve.wait_ge(o_rstd, 4 * h + t + 1)
                    nc.vector.tensor_scalar(y_tok[:, bass.ds(h * TT * RV + t * RV, RV)], ps[:, SIDE_B[t], :], moments[:, t, 0:1],
                                            rstd[:, t:t + 1], ALU.subtract, ALU.mult).then_inc(o_normed, 1)
                make_lo(dve, Chunk(C_RET + 6, h, 6))
                between()
                for t in range(TT):
                    dve.wait_ge(g_read, 4 * h + t + 1 + FREE)
                    dve.wait_ge(o_normed, 4 * h + t + 1 + FREE)
                    y = y_tok[:, bass.ds(h * TT * RV + t * RV, RV)]
                    nc.vector.tensor_tensor(y, y, tmp[2 + t % 2][:], ALU.mult).then_inc(y_made, 1)
                assert own.n == start + OWN_PER_HEAD

            with dve.Fori(0, RH - 1) as h:
                head(h)
                make_lo(dve, Chunk(C_RET + 7, h, 6))
            head(RH - 1, lambda: [y_tile_lo(q) for q in range(4)])
            make_lo(dve, Chunk(C_OUT1 + 1))
            own.n = start + OWN_PER_HEAD * RH
            own.per_turn = 0

            for q in range(4, RH * TT):
                y_tile_lo(q)
                if q in (7, 11, 15):
                    make_lo(dve, Chunk(C_OUT1 + (q + 1) // 4))
            for t in range(TT):
                sums(PM_OUT1A, C_OUT1 + 3)(t)
                add_residual(t, 0, resid_read)
            for j in range(5, 8):
                make_lo(dve, Chunk(C_OUT1 + j))
            dve.wait_ge(resid_read, TT)
            dve.sem_inc(up_read, 2)
            layer_norm(2, sums(PM_OUT1B, C_FFN1 - 1), halves=(1,))
            swiglu(1, C_FFN1, C_DOWN1, PM_FFN1)
            layer_norm(3, sums(PM_DOWN1, N_CHUNKS - 1), turn=False)

        @block.tensor
        def _(pe):
            def product(dst, a, b, start, stop):
                nc.tensor.matmul(dst, a[0], b[0], start=start, stop=False)
                nc.tensor.matmul(dst, a[0], b[1], start=False, stop=False)
                return nc.tensor.matmul(dst, a[1], b[0], start=False, stop=stop)

            def weights(ch, k):
                return tuple(w[ch.s][:].rearrange("p (k n) -> p k n", k=k) for w in (w_hi, w_lo))

            def turn(stage, t, ready=lambda half: None):
                for half in range(2):
                    ready(half)
                    for k in range(4):
                        last = nc.tensor.transpose(ps[:, t + 4 * half, k * P:(k + 1) * P],
                                                   x_tok[:, t, (4 * half + k) * P:(4 * half + k + 1) * P], ident[:])
                    last.then_inc(turned, 1)

            def feature_tiles(ch, banks, bank_free, tokens=slice(0, SEQ), final=True):
                hi, lo = weights(ch, KD)
                for m in range(2):
                    bank_free(m)
                    cols = slice(m * P, (m + 1) * P)
                    for k in range(KD):
                        last = product(ps[:, banks[m], tokens], (hi[:, k, cols], lo[:, k, cols]),
                                       (xT_hi[:, k, tokens], xT_lo[:, k, tokens]), k == 0, k == KD - 1)
                    if final:
                        last.then_inc(chunk_used if m else part_made, 1)

            def first_tiles(stage, chunks, split, bank_free, turns=lambda t: None):
                def before(half, j, m):
                    if half == 0:
                        bank_free(j, m)
                        if m == 1:
                            turns(2 + j)

                for half in range(2):
                    pe.wait_ge(xT_lo_made, 8 * stage + 4 * half + 4)
                    for j, ch in enumerate(chunks):
                        if half == 0:
                            split(j)
                        feature_tiles(ch, SIDE_A[2 * j:2 * j + 2], lambda m, j=j: before(half, j, m),
                                      slice(half * SEQ // 2, (half + 1) * SEQ // 2), half == 1)

            def token_tiles(chunks, banks, rows, cols, bank_free, after_first=lambda: None):
                for j, ch in enumerate(chunks):
                    pe.wait_ge(lo_made, ch.lo)
                    hi, lo = weights(ch, rows)
                    for k in range(rows):
                        for t in range(TT):
                            if j == 0 and k == 0:
                                bank_free(t)
                            row, tok = rows * j + k, slice(t * P, (t + 1) * P)
                            end = j == len(chunks) - 1 and k == rows - 1
                            last = product(ps[:, banks[t], 0:cols], (xT_hi[:, row, tok], xT_lo[:, row, tok]),
                                           (hi[:, k, :], lo[:, k, :]), row == 0, end)
                            if end and t < TT - 1:
                                last.then_inc(part_made, 1)
                    last.then_inc(chunk_used, 1)
                    if j == 0:
                        after_first()

            LAST_TAIL = ((0, 0), (0, 1), (1, 0), (1, 1), (0, 2), (1, 2), (0, 3), (1, 3))
            TAIL = ((0, 0), (0, 1), (1, 0), (0, 2), (1, 1), (0, 3), (1, 2), (1, 3))

            def out_projection(c, n, sT, ready, stage, order, before_tiles):
                def part(ch, k, row, t):
                    hi, lo = weights(ch, 2)
                    tok = slice(t * P, (t + 1) * P)
                    for a, b in ((0, 0), (0, 1), (1, 0)):
                        for half in range(2):
                            last = nc.tensor.matmul(ps[:, t + 4 * half, :], sT[a][:, row, tok],
                                                    (hi, lo)[b][:, k, N * half:N * half + N],
                                                    start=(row == 0 and a == b), stop=(row == 2 * n - 1 and a == 1))
                    return last

                for j in range(n - 2):
                    wait_split(pe, c + j)
                    if j == 0:
                        for tiles in order:
                            before_tiles(tiles)
                            for k in range(2):
                                ready(k)
                                for t in tiles:
                                    last = part(Chunk(c), k, k, t)
                    else:
                        for k in range(2):
                            ready(2 * j + k)
                            for t in range(TT):
                                last = part(Chunk(c + j), k, 2 * j + k, t)
                    last.then_inc(chunk_used, 1)
                for j, t in LAST_TAIL if stage is None else TAIL:
                    if t == 0:
                        wait_split(pe, c + n - 2 + j)
                        for k in range(2):
                            ready(2 * (n - 2 + j) + k)
                    for k in range(2):
                        last = part(Chunk(c + n - 2 + j), k, 2 * (n - 2 + j) + k, t)
                    if t == TT - 1:
                        last.then_inc(chunk_used, 1)
                    elif j:
                        last.then_inc(part_made, 1)
                    early_turns(stage, j, t)

            def early_turns(stage, j, t):
                if stage is not None and (j, t) == (0, 3):
                    turn_when_normed(stage, 0)
                elif stage is not None and (j, t) == (1, 2):
                    turn_when_normed(stage, 1)

            def turn_when_normed(stage, t):
                turn(stage, t, lambda half: pe.wait_ge(x_normed, 8 * (stage - 1) + 2 * t + half + 1))

            pe.wait_ge(pool_own, 2)

            def turn_when_landed(t):
                turn(0, t, lambda half: pe.wait_ge(x_landed[t], 16) if half == 0 else None)

            for t in range(TT):
                turn_when_landed(t)
            first_tiles(0, [Chunk(0), Chunk(1)], lambda j: wait_split(pe, j), lambda j, m: None)
            token_tiles([Chunk(C_KV)], SIDE_B, KD, 256, lambda t: None)

            def k_transposes():
                pe.wait_ge(k_roped_made, 2 * TT)
                pe.wait_ge(v_lo_made, TT)
                for g in range(KV):
                    for t in range(TT):
                        last = nc.tensor.transpose(ps[:, K_BANKS[g], t * P:(t + 1) * P],
                                                   k_roped[:, t, g].rearrange("p c d -> p (c d)"), ident[:])
                    last.then_inc(k_in_psum, 1)

            token_tiles([Chunk(C_Q), Chunk(C_Q + 1)], SIDE_A, 4, N, lambda t: pe.wait_ge(z_made, 2) if t == 0 else None,
                        k_transposes)

            def q_transposes(t):
                pe.wait_ge(q_roped_made, 2 * t + 2)
                for j in range(4):
                    last = nc.tensor.transpose(ps[:, SIDE_A[t], j * P:(j + 1) * P], q_roped[:, t, j * P:(j + 1) * P], ident[:])
                last.then_inc(q_in_psum, 1)

            def scores(s):
                t, h = s // HEADS, s % HEADS
                if s < 2:
                    pe.wait_ge(qT_lo_made, s + 1)
                else:
                    pe.wait_ge(exp_made, s - 1)
                q = tuple(x[:, t, h // 2, :] for x in (qT_hi, qT_lo))
                k = tuple(x[:, h // (HEADS // KV), h % 2, :] for x in (kT_hi, kT_lo))
                product(ps[:, SCORE_BANKS[s % 2], :], q, k, True, True).then_inc(scores_made, 1)

            wait_split(pe, C_GLU[1])
            feature_tiles(Chunk(C_GLU[1]), SIDE_B[0:2], lambda m: None)
            for t in range(2):
                q_transposes(t)
            wait_split(pe, C_GLU[1] + 1)
            feature_tiles(Chunk(C_GLU[1] + 1), SIDE_B[2:4],
                          lambda m: [step(i) for step, i in ((q_transposes, 2), (q_transposes, 3), (scores, 0), (scores, 1))] if m
                          else pe.wait_ge(kT_lo_made, 4))

            def attention_step(s):
                if 2 <= s < STEPS:
                    scores(s)
                u = s - 2
                if 0 <= u < STEPS:
                    pe.wait_ge(exp_made, u + 1)
                    if u == 0:
                        pe.wait_ge(qT_lo_made, TT)
                    if u == 1:
                        pe.wait_ge(z_made, 4)
                    if u >= 2:
                        pe.wait_ge(probT_lo_made, u - 1)
                    for k in range(TT):
                        last = nc.tensor.transpose(ps[:, TURN_BANKS[u % 2], k * P:(k + 1) * P],
                                                   tmp[u % 3][:, k * P:(k + 1) * P], ident[:])
                    last.then_inc(prob_turned, 1)
                b = (s - 3) // 2
                if s % 2 and 0 <= b < BATCHES:
                    if b == 0:
                        pe.wait_ge(z_lo_made, 1)
                    pe.wait_ge(diag_lo_made, b + 1)
                    for i in range(BATCH):
                        k = BATCH * b + i
                        last = product(ps[:, CONV_BANK, :], (diag_hi[:, b % 2, i, :], diag_lo[:, b % 2, i, :]),
                                       (z_hi[:, k:k + SEQ], z_lo[:, k:k + SEQ]), k == 0, k == BATCH * BATCHES - 1)
                    last.then_inc(diag_used, 1)
                w = s - 4
                if 0 <= w < STEPS:
                    pe.wait_ge(probT_lo_made, w + 1)
                    n, g = w // GROUP, w % HEADS // (HEADS // KV)
                    if w % GROUP == 0 and n >= 2:
                        pe.wait_ge(o_copied, n - 1)
                    dst = ps[:, OUT_BANKS[n % 2], 2 * HD * (w % GROUP):2 * HD * (w % GROUP + 1)]
                    for k in range(TT):
                        keys = slice(k * P, (k + 1) * P)
                        parts = [(dst, probT_hi[:, w % 3, keys], v_parts[:, k, g].rearrange("p c d -> p (c d)")),
                                 (dst[:, 0:HD], probT_lo[:, w % 3, keys], v_parts[:, k, g, 0, :])]
                        for i, (to, a, b) in enumerate(parts if k < TT - 1 else parts[::-1]):
                            last = nc.tensor.matmul(to, a, b, start=(k == 0 and i == 0), stop=(k == TT - 1 and i == 1))
                    last.then_inc(head_done, 1)
                if s in OUT_TO_FEATURES:
                    output_transposes(OUT_TO_FEATURES.index(s))
                if s in CONV_TO_TOKENS:
                    t = CONV_TO_TOKENS.index(s)
                    if t == 0:
                        pe.wait_ge(tap_done, DVE_TAPS)
                        pe.wait_ge(part_added, ADDED + 1)
                        pe.wait_ge(conv_copied, 1)
                    else:
                        pe.wait_ge(conv_normed, t)
                    for ct in range(CT):
                        last = nc.tensor.transpose(ps[:, CONV_BANK, ct * P:(ct + 1) * P], acc[:, ct, t * P:(t + 1) * P], ident[:])
                    last.then_inc(conv_turned, 1)
                if s == CONV_TO_FEATURES:
                    pe.wait_ge(conv_normed, TT)
                    pe.wait_ge(exp_made, STEPS)
                    pe.wait_ge(att_lo_made, TT - 1)
                    for ct in range(CT):
                        for t in range(TT):
                            last = nc.tensor.transpose(ps[:, BACK_BANKS[ct], t * P:(t + 1) * P],
                                                       conv_norm[:, t, ct * P:(ct + 1) * P], ident[:])
                        last.then_inc(conv_back, 1)

            def output_transposes(t):
                pe.wait_ge(o_divided, 2 * t + 2)
                if t:
                    pe.wait_ge(att_lo_made, t)
                for j in range(4):
                    last = nc.tensor.transpose(ps[:, SPARE, j * P:(j + 1) * P], o_tok[:, t % 2, j * P:(j + 1) * P], ident[:])
                last.then_inc(o_turned, 1)

            for s in range(2, LAST_STEP):
                attention_step(s)

            def before_tiles(tiles):
                if tiles == (0, 1):
                    pe.wait_ge(silu_made, 3)
                elif tiles == (2,):
                    pe.wait_ge(silu_made, CT)
                    output_transposes(TT - 1)
                    pe.wait_ge(o_copied, STEPS // GROUP)
                else:
                    pe.wait_ge(att_lo_made, TT)

            out_projection(C_OUT0, 4, (catT_hi, catT_lo),
                           lambda row: pe.wait_ge(swish_lo_made, row - 3) if row >= 4 else None, 1,
                           ((0, 1), (2,), (3,)), before_tiles)

            def swiglu(layer, c_ffn, c_down, stage):
                h0, f0 = NH * layer, (NH + 2) * layer
                first_tiles(2 * layer + 1, [Chunk(c_ffn), Chunk(c_ffn + 1)], lambda j: wait_split(pe, c_ffn + j),
                            lambda j, m: pe.wait_ge((gate_read, up_read)[j], f0 + m + 1),
                            lambda t: turn_when_normed(2 * layer + 1, t))
                with pe.Fori(1, NH // 2) as i:
                    for j, read in enumerate((gate_read, up_read)):
                        ch = Chunk(c_ffn + j, i)
                        pe.wait_ge(lo_made, ch.lo)
                        feature_tiles(ch, SIDE_A[2 * j:2 * j + 2], lambda m: pe.wait_ge(read, f0 + 2 * i + m + 1))
                out_projection(c_down, NH // 2, (hT_hi, hT_lo), lambda row: pe.wait_ge(h_lo_made, h0 + row + 1), stage,
                               ((2, 3), (0, 1)),
                               lambda tiles: pe.wait_ge(up_read, f0 + NH + 2) if tiles == (0, 1) else None)

            swiglu(0, C_FFN0, C_DOWN0, 2)

            def turn_y(q):
                if q == 0:
                    pe.wait_ge(o_normed, 4 * RH + FREE)
                if q % TT == 0:
                    pe.wait_ge(y_made, 4 * (q // TT + 1))
                if q == 6:
                    pe.wait_ge(g_read, 4 * RH + FREE)
                if q >= 4:
                    pe.wait_ge(yT_lo_made, max(q - 3, 4))
                for t in range(TT):
                    col = (q // TT * TT + t) * RV + q % TT * P
                    last = nc.tensor.transpose(ps[:, y_bank(q), t * P:(t + 1) * P], y_tok[:, col:col + P], ident[:])
                last.then_inc(y_turned, 1)

            def queries_and_keys(h, split, turns=lambda t: None):
                first_tiles(2, [Chunk(C_RET + j, h, 6) for j in range(2)], split,
                            lambda j, m: pe.wait_ge(g_read, 4 * h + 2 * j + m + 1), turns)

            def rest_of_head(h, between=lambda: None):
                token_tiles([Chunk(C_RET + 2, h, 6), Chunk(C_RET + 3, h, 6)], SIDE_B, 4, N,
                            lambda t: pe.wait_ge(o_normed, 4 * h + t + 1))
                pe.wait_ge(rot_lo, 4 * h + 4)
                for kt in range(TT):
                    for half in range(2):
                        last = product(ps[:, SIDE_A[kt], :], (rk_hi[:, half, kt * P:(kt + 1) * P], rk_lo[:, half, kt * P:(kt + 1) * P]),
                                       (rq_hi[:, half, :], rq_lo[:, half, :]), half == 0, half == 1)
                    last.then_inc(ret_scored, 1)
                pe.wait_ge(rv_lo_made, 4 * h + 4)
                for kt in range(TT):
                    pe.wait_ge(sT_lo_made, 4 * h + kt + 1)
                    for t in range(TT):
                        tok = slice(t * P, (t + 1) * P)
                        last = product(ps[:, SIDE_B[t], :], (sT_hi[:, kt % 2, tok], sT_lo[:, kt % 2, tok]),
                                       (rv_hi[:, kt, :], rv_lo[:, kt, :]), kt == 0, kt == TT - 1)
                        if kt == TT - 1:
                            last.then_inc(o_made, 1)
                    if kt < TT - 1:
                        last.then_inc(sT_used, 1)
                token_tiles([Chunk(C_RET + 4, h, 6), Chunk(C_RET + 5, h, 6)], SIDE_A, 4, N, lambda t: None, between)

            queries_and_keys(0, lambda j: wait_split(pe, C_RET + j), lambda t: turn_when_normed(2, t))
            with pe.Fori(0, RH - 1) as h:
                rest_of_head(h)
                queries_and_keys(h + 1, lambda j: pe.wait_ge(lo_made, Chunk(C_RET + j, h + 1, 6).lo))
            rest_of_head(RH - 1, lambda: [turn_y(q) for q in range(4)])
            pe.wait_ge(g_read, 4 * (RH - 1) + 2 + FREE)

            def y_part(q, t):
                ch, k, tok = Chunk(C_OUT1 + q // 4), q % 4, slice(t * P, (t + 1) * P)
                hi, lo = weights(ch, 4)
                return product(ps[:, 4 * (q // 16) + t, :], (yT_hi[q % 16][:, tok], yT_lo[q % 16][:, tok]),
                               (hi[:, k, :], lo[:, k, :]), q % 16 == 0, q % 16 == 15)

            for q in range(24):
                if q % 4 == 0:
                    wait_split(pe, C_OUT1 + q // 4)
                if q < 16:
                    pe.wait_ge(yT_lo_made, q + 1 if q else 2)
                for t in range(TT):
                    last = y_part(q, t)
                    if q == 15 and t < TT - 1:
                        last.then_inc(part_made, 1)
                if q % 4 == 3:
                    last.then_inc(chunk_used, 1)
                if q + 4 < RH * TT:
                    turn_y(q + 4)
            for j, t in TAIL:
                if t == 0:
                    wait_split(pe, C_FFN1 - 2 + j)
                for q in range(24 + 4 * j, 28 + 4 * j):
                    last = y_part(q, t)
                if t == TT - 1:
                    last.then_inc(chunk_used, 1)
                elif j:
                    last.then_inc(part_made, 1)
                early_turns(3, j, t)
            swiglu(1, C_FFN1, C_DOWN1, None)


def rope_tables():
    t = np.arange(SEQ)
    row, col = (t // GRID_W).astype(np.float32), (t % GRID_W).astype(np.float32)

    def angles(head_dim):
        axis = head_dim // 2
        freq = np.float32(THETA) ** (-np.arange(0, axis, 2, dtype=np.float32) / np.float32(axis))
        return np.concatenate([row[:, None] * freq, col[:, None] * freq], axis=-1).astype(np.float32)

    a, r = angles(HD), angles(RK)
    by_token = np.stack([np.cos(a), np.sin(a)], axis=1).reshape(TT, P, 2, HD // 2).transpose(1, 0, 2, 3)
    by_freq = np.stack([np.cos(r).T, np.sin(r).T], axis=1)
    return np.ascontiguousarray(by_token, np.float32), np.ascontiguousarray(by_freq, np.float32)


_PLAIN = ["x", "l0_w_in", "l0_q_norm_g", "l0_k_norm_g", "l0_w_out", "l0_ln_mix_g", "l0_ln_mix_b",
          "l0_ffn_w_gate", "l0_ffn_w_up", "l0_ffn_w_down", "l0_ln_ffn_g", "l0_ln_ffn_b",
          "l1_w_in", "l1_w_out", "l1_ln_mix_g", "l1_ln_mix_b", "l1_ffn_w_gate", "l1_ffn_w_up",
          "l1_ffn_w_down", "l1_ln_ffn_g", "l1_ln_ffn_b"]


def kernel(**inputs):
    import numpy as _np
    import concourse.bacc as _bacc
    from concourse import mybir as _mybir
    from concourse.bass_utils import run_bass_kernel_spmd as _run

    given = {name: _np.asarray(a) for name, a in inputs.items()}
    arrays = {name: given[name] for name in _PLAIN}
    by_channel = _np.concatenate([given["l0_dw_w"], given["l0_dw_b"][None], given["l0_conv_norm_g"][None],
                                  given["l0_conv_norm_b"][None]])
    arrays["conv_par"] = by_channel.reshape(TAPS + 3, CT, P).transpose(2, 1, 0)
    arrays["decay"] = _np.stack([given["l1_log_decay_fwd"], given["l1_log_decay_bwd"]])
    arrays["ret_gain"] = given["l1_ret_norm_g"].reshape(-1, P).T
    arrays["rope0"], arrays["rope1"] = rope_tables()

    nc = _bacc.Bacc("TRN2", target_bir_lowering=False, num_devices=1)
    ins, feed = {}, {}
    for name, a in arrays.items():
        feed[f"in_{name}"] = _np.ascontiguousarray(a)
        ins[name] = nc.dram_tensor(f"in_{name}", a.shape, _mybir.dt.from_np(a.dtype), kind="ExternalInput").ap()
    out = nc.dram_tensor("out_0", (1, SEQ, D), _mybir.dt.float32, kind="ExternalOutput").ap()
    build_encoder(nc, ins, out)
    r = _run(nc, [feed], core_ids=[0])
    return r.results[0]["out_0"]
```
